# Optimizing a Trainium2 kernel written in Bass

```python
import jax, jax.numpy as jnp
from jax import lax
import numpy as np

D_MODEL = 1024
BATCH = 1
SEQ = 256
DEPTH = 1
DEC_BATCH = 8
DEC_SEQ = 1
PAST_LEN = 2048
PAGE_SIZE = 128

GLA_HEADS = 4
GLA_DK_T = D_MODEL // 2
GLA_DV_T = D_MODEL
GLA_DK = GLA_DK_T // GLA_HEADS
GLA_DV = GLA_DV_T // GLA_HEADS
GK_RANK = 16
GATE_NORMALIZER = 16.0
GLA_CHUNK = 64
D_GMLP = D_MODEL
MIX_HEADS = 4
MIX_DH = D_GMLP // MIX_HEADS
MIX_CHUNK = 128
N_EXPERTS = 32
TOP_K = 4
D_FF = D_MODEL
SWIGLU_LIMIT = 7.0
SWIGLU_ALPHA = 1.702
MOE_BLOCK = 128
D_PLE = 256
EPS = 1e-6
SPLIT_SIZES = (GLA_DK_T, GLA_DK_T, GLA_DV_T, GLA_DV_T, GK_RANK, D_GMLP, D_GMLP, D_MODEL, D_MODEL)
N_IN = 2 * GLA_DK_T + 2 * GLA_DV_T + GK_RANK + 2 * D_GMLP + 2 * D_MODEL

kernel_name = 'gla_gmlp_moe_hybrid_step'

def rms_norm(x, g):
    xf = x.astype(jnp.float32)
    y = xf * lax.rsqrt(jnp.mean(xf * xf, axis=-1, keepdims=True) + EPS)
    return (y * g.astype(jnp.float32)).astype(x.dtype)

def layer_norm(x, g, b):
    xf = x.astype(jnp.float32)
    mu = jnp.mean(xf, axis=-1, keepdims=True)
    var = jnp.mean(jnp.square(xf - mu), axis=-1, keepdims=True)
    y = (xf - mu) * lax.rsqrt(var + EPS)
    return (y * g.astype(jnp.float32) + b.astype(jnp.float32)).astype(x.dtype)

def gla_chunked(q, k, v, log_a, s0):
    N, L, H, _ = q.shape
    C = min(GLA_CHUNK, L)
    n_c = -(-L // C)
    pad = n_c * C - L

    def blocks(t):
        t = jnp.pad(t.astype(jnp.float32), ((0, 0), (0, pad), (0, 0), (0, 0)))
        return t.reshape(N, n_c, C, H, t.shape[-1]).transpose(1, 0, 3, 2, 4)

    mask = jnp.tril(jnp.ones((C, C), dtype=bool))

    def step(S, blk):
        qc, kc, vc, gc = blk
        b = jnp.cumsum(gc, axis=2)
        qe = qc * jnp.exp(b)
        ke = kc * jnp.exp(-b)
        att = jnp.where(mask, jnp.einsum('nhtk,nhsk->nhts', qe, ke), 0.0)
        o = jnp.einsum('nhts,nhsv->nhtv', att, vc) + jnp.einsum('nhtk,nhkv->nhtv', qe, S)
        b_last = b[:, :, -1:, :]
        S = jnp.exp(b_last[:, :, 0, :, None]) * S + jnp.einsum('nhsk,nhsv->nhkv', kc * jnp.exp(b_last - b), vc)
        return S, o

    S, o = lax.scan(step, s0.astype(jnp.float32), (blocks(q), blocks(k), blocks(v), blocks(log_a)))
    o = o.transpose(1, 0, 3, 2, 4).reshape(N, n_c * C, H, -1)[:, :L]
    return o, S

def causal_chunk_mix(v, w_s, b_s):
    N, L = v.shape[:2]
    C = min(MIX_CHUNK, L)
    n_c = -(-L // C)
    v = jnp.pad(v, ((0, 0), (0, n_c * C - L), (0, 0), (0, 0)))
    vc = v.reshape(N, n_c, C, MIX_HEADS, MIX_DH)
    w = jnp.tril(w_s[:, :C, :C])
    out = jnp.einsum('hts,ncshd->ncthd', w, vc) + b_s[:, :C].T[None, None, :, :, None]
    return out.reshape(N, n_c * C, MIX_HEADS, MIX_DH)[:, :L]

def moe(x, w_router, b_router, w_gate, b_gate, w_up, b_up, w_down, b_down):
    T, D = x.shape
    logits = (x @ w_router + b_router).astype(jnp.float32)
    top_v, top_i = lax.top_k(logits, TOP_K)
    wts = jax.nn.softmax(top_v, axis=-1)
    TK = T * TOP_K
    e = top_i.reshape(TK)
    tok = jnp.repeat(jnp.arange(T, dtype=jnp.int32), TOP_K)
    w = wts.reshape(TK)
    order = jnp.argsort(e, stable=True)
    e_s, tok_s, w_s = e[order], tok[order], w[order]
    counts = jnp.bincount(e, length=N_EXPERTS)
    padded = (counts + MOE_BLOCK - 1) // MOE_BLOCK * MOE_BLOCK
    pad_end = jnp.cumsum(padded)
    pad_start = pad_end - padded
    raw_start = jnp.cumsum(counts) - counts
    dest = pad_start[e_s] + jnp.arange(TK) - raw_start[e_s]
    n_blocks = (TK + N_EXPERTS * (MOE_BLOCK - 1) + MOE_BLOCK - 1) // MOE_BLOCK
    P = n_blocks * MOE_BLOCK
    row_tok = jnp.full((P,), T, dtype=jnp.int32).at[dest].set(tok_s)
    row_w = jnp.zeros((P,), jnp.float32).at[dest].set(w_s)
    block_e = jnp.minimum(jnp.searchsorted(pad_end, jnp.arange(n_blocks) * MOE_BLOCK, side='right'), N_EXPERTS - 1)
    x_pad = jnp.concatenate([x, jnp.zeros((1, D), x.dtype)], axis=0)
    xb = x_pad[row_tok].reshape(n_blocks, MOE_BLOCK, D)

    def expert_block(args):
        xblk, eid = args
        g = xblk @ w_gate[eid] + b_gate[eid]
        u = xblk @ w_up[eid] + b_up[eid]
        g = jnp.minimum(g, SWIGLU_LIMIT)
        u = jnp.clip(u, -SWIGLU_LIMIT, SWIGLU_LIMIT)
        hmid = (u + 1.0) * (g * jax.nn.sigmoid(SWIGLU_ALPHA * g))
        return hmid @ w_down[eid] + b_down[eid]

    yb = lax.map(expert_block, (xb, block_e)).reshape(P, D)
    y = jax.ops.segment_sum(yb * row_w[:, None].astype(yb.dtype), row_tok, num_segments=T + 1)
    return y[:T]

def hybrid_layer(x, p, s0, norm1_g, w_in, w_gk2, b_gk, gla_norm_g, v_norm_g, v_norm_b, w_sp, b_sp, w_o,
                 norm2_g, w_router, b_router, w_gate, b_gate, w_up, b_up, w_down, b_down,
                 norm3_g, w_ple_gate, w_ple_proj):
    N, L, _ = x.shape
    hn = rms_norm(x, norm1_g)
    z = hn @ w_in
    idx = [int(c) for c in np.cumsum(SPLIT_SIZES)[:-1]]
    q, k, v, r, gk, u, vg, ga, gb = jnp.split(z, idx, axis=-1)
    q = q.reshape(N, L, GLA_HEADS, GLA_DK) * (GLA_DK ** -0.5)
    k = k.reshape(N, L, GLA_HEADS, GLA_DK)
    v = v.reshape(N, L, GLA_HEADS, GLA_DV)
    log_a = jax.nn.log_sigmoid((gk @ w_gk2 + b_gk).astype(jnp.float32)) / GATE_NORMALIZER
    log_a = log_a.reshape(N, L, GLA_HEADS, GLA_DK)
    o, s_new = gla_chunked(q, k, v, log_a, s0)
    o_a = rms_norm(o, gla_norm_g).reshape(N, L, GLA_DV_T).astype(x.dtype) * jax.nn.silu(r)
    u = jax.nn.gelu(u, approximate=False)
    vn = layer_norm(jax.nn.gelu(vg, approximate=False), v_norm_g, v_norm_b)
    mix = causal_chunk_mix(vn.reshape(N, L, MIX_HEADS, MIX_DH), w_sp, b_sp).reshape(N, L, D_GMLP)
    o_b = u * mix
    h = x + (jax.nn.sigmoid(ga) * o_a + jax.nn.sigmoid(gb) * o_b) @ w_o
    h = h + moe(rms_norm(h, norm2_g).reshape(N * L, D_MODEL), w_router, b_router,
                w_gate, b_gate, w_up, b_up, w_down, b_down).reshape(N, L, D_MODEL)
    h = h + jax.nn.sigmoid(rms_norm(h, norm3_g) @ w_ple_gate) * (p @ w_ple_proj)
    return h, s_new, vn

def setup_inputs(seed: int = 0) -> dict:
    key = jax.random.key(seed)
    ks = jax.random.split(key, 32)

    def nrm(k, shape, scale):
        return jax.random.normal(k, shape, jnp.float32) * scale

    return {
        'x_prompt': nrm(ks[0], (BATCH, SEQ, D_MODEL), 1.0),
        'x_sample': nrm(ks[1], (DEC_BATCH, DEC_SEQ, D_MODEL), 1.0),
        'state_gla': nrm(ks[2], (DEPTH, DEC_BATCH, GLA_HEADS, GLA_DK, GLA_DV), 0.5),
        'p_prompt': nrm(ks[3], (DEPTH, BATCH, SEQ, D_PLE), 1.0),
        'p_sample': nrm(ks[4], (DEPTH, DEC_BATCH, DEC_SEQ, D_PLE), 1.0),
        'norm1_g': 1.0 + nrm(ks[5], (DEPTH, D_MODEL), 0.05),
        'w_in': nrm(ks[6], (DEPTH, D_MODEL, N_IN), D_MODEL ** -0.5),
        'w_gk2': nrm(ks[7], (DEPTH, GK_RANK, GLA_DK_T), GK_RANK ** -0.5),
        'b_gk': nrm(ks[8], (DEPTH, GLA_DK_T), 0.1),
        'gla_norm_g': 1.0 + nrm(ks[9], (DEPTH, GLA_DV), 0.05),
        'v_norm_g': 1.0 + nrm(ks[10], (DEPTH, D_GMLP), 0.05),
        'v_norm_b': nrm(ks[11], (DEPTH, D_GMLP), 0.02),
        'w_sp': nrm(ks[12], (DEPTH, MIX_HEADS, MIX_CHUNK, MIX_CHUNK), MIX_CHUNK ** -0.5),
        'b_sp': 1.0 + nrm(ks[13], (DEPTH, MIX_HEADS, MIX_CHUNK), 0.1),
        'w_o': nrm(ks[14], (DEPTH, D_MODEL, D_MODEL), D_MODEL ** -0.5),
        'norm2_g': 1.0 + nrm(ks[15], (DEPTH, D_MODEL), 0.05),
        'w_router': nrm(ks[16], (DEPTH, D_MODEL, N_EXPERTS), D_MODEL ** -0.5),
        'b_router': nrm(ks[17], (DEPTH, N_EXPERTS), 0.01),
        'w_gate': nrm(ks[18], (DEPTH, N_EXPERTS, D_MODEL, D_FF), D_MODEL ** -0.5),
        'b_gate': nrm(ks[19], (DEPTH, N_EXPERTS, D_FF), 0.01),
        'w_up': nrm(ks[20], (DEPTH, N_EXPERTS, D_MODEL, D_FF), D_MODEL ** -0.5),
        'b_up': nrm(ks[21], (DEPTH, N_EXPERTS, D_FF), 0.01),
        'w_down': nrm(ks[22], (DEPTH, N_EXPERTS, D_FF, D_MODEL), D_FF ** -0.5),
        'b_down': nrm(ks[23], (DEPTH, N_EXPERTS, D_MODEL), 0.01),
        'norm3_g': 1.0 + nrm(ks[24], (DEPTH, D_MODEL), 0.05),
        'w_ple_gate': nrm(ks[25], (DEPTH, D_MODEL, D_MODEL), D_MODEL ** -0.5),
        'w_ple_proj': nrm(ks[26], (DEPTH, D_PLE, D_MODEL), D_PLE ** -0.5),
        'final_g': 1.0 + nrm(ks[27], (D_MODEL,), 0.05),
    }

def reference(x_prompt, x_sample, state_gla, p_prompt, p_sample, norm1_g, w_in, w_gk2, b_gk, gla_norm_g,
              v_norm_g, v_norm_b, w_sp, b_sp, w_o, norm2_g, w_router, b_router, w_gate, b_gate, w_up, b_up,
              w_down, b_down, norm3_g, w_ple_gate, w_ple_proj, final_g):
    hp, hs = x_prompt, x_sample
    st_prompt, st_sample, v_sample = [], [], []
    for i in range(DEPTH):
        lw = (norm1_g[i], w_in[i], w_gk2[i], b_gk[i], gla_norm_g[i], v_norm_g[i], v_norm_b[i], w_sp[i], b_sp[i],
              w_o[i], norm2_g[i], w_router[i], b_router[i], w_gate[i], b_gate[i], w_up[i], b_up[i],
              w_down[i], b_down[i], norm3_g[i], w_ple_gate[i], w_ple_proj[i])
        s0 = jnp.zeros((hp.shape[0], GLA_HEADS, GLA_DK, GLA_DV), jnp.float32)
        hp, sp, _ = hybrid_layer(hp, p_prompt[i], s0, *lw)
        hs, ss, vs = hybrid_layer(hs, p_sample[i], state_gla[i], *lw)
        st_prompt.append(sp.astype(state_gla.dtype))
        st_sample.append(ss.astype(state_gla.dtype))
        v_sample.append(vs)
    y_prompt = rms_norm(hp, final_g)
    y_sample = rms_norm(hs, final_g)
    new_state_gla_prompt = jnp.stack(st_prompt)
    new_state_gla_sample = jnp.stack(st_sample)
    new_mix_v_sample = jnp.stack(v_sample)
    return (y_prompt, y_sample, new_state_gla_prompt, new_state_gla_sample, new_mix_v_sample)


_drawn_inputs = setup_inputs


def setup_inputs(seed=0):
    import zlib

    import numpy as np

    out = dict(_drawn_inputs(seed))
    spreads = {}
    factors = {'b_gate': 8.0, 'b_up': 8.0, 'b_down': 8.0, 'norm3_g': 7.173}
    for name, (base, spread) in spreads.items():
        noise = np.random.default_rng([zlib.crc32(name.encode()), seed]).standard_normal(out[name].shape)
        drawn = base * np.exp(spread * noise) if base else spread * noise
        out[name] = __import__('jax').numpy.asarray(drawn.astype(out[name].dtype))
    for name, factor in factors.items():
        out[name] = (out[name] * factor).astype(out[name].dtype)
    return out
```

```python
from contextlib import ExitStack

import numpy as np

import concourse.bass as bass
from concourse import mybir

F32 = mybir.dt.float32
I32 = mybir.dt.int32
U32 = mybir.dt.uint32
ALU = mybir.AluOpType
ACT = mybir.ActivationFunctionType
AX = mybir.AxisListType

P = 128
EPS = 1e-6
GLA_CHUNK = 64
TOP_K = 4
LIMIT, ALPHA = 7.0, 1.702
CAP = 80
GATE_NORMALIZER = 16.0

SLOT = 2048
SLOTS = 16
FRONT_SLOTS = 6
LATE_SLOTS = 2
PER_EXPERT = 12
UNROLL = 4


def hybrid_step(nc, x_prompt, x_sample, state_gla, p_prompt, p_sample, norm1_g, w_in, w_gk2, b_gk, gla_norm_g,
                v_norm_g, v_norm_b, w_sp, b_sp, w_o, norm2_g, w_router, b_router, w_gate, b_gate, w_up, b_up,
                w_down, b_down, norm3_g, w_ple_gate, w_ple_proj, final_g,
                y_prompt, y_sample, st_prompt, st_sample, mix_v_sample):
    L, D = x_prompt.shape[1:]
    NS = x_sample.shape[0]
    T = L + NS
    NB = L // P
    KT = D // P
    H, DK, DV = state_gla.shape[2:]
    RANK = w_gk2.shape[1]
    E = w_gate.shape[1]
    MH = w_sp.shape[1]
    DP = p_prompt.shape[3]
    PK = DP // P
    NCH = L // GLA_CHUNK
    HALF = KT // 2
    MAX_OV = T * TOP_K // CAP + 1
    LEVELS = (T - 1) // CAP
    ROUNDS = E // UNROLL
    BLOCKS = [(b, P, b * P) for b in range(NB)] + [(NB, NS, L)]

    CQ, CK, CV, CR = 0, H * DK, 2 * H * DK, 2 * H * DK + H * DV
    CGK = CR + H * DV
    CU, CVG, CGA, CGB = CGK + RANK, CGK + RANK + D, CGK + RANK + 2 * D, CGK + RANK + 3 * D

    def in_turn(a, b):
        return [(k, f) for c in range(0, KT, 2) for k in (a, b) for f in (c, c + 1)]

    ztiles = [("k", f) for f in range(H)] + [("q", f) for f in range(H)] + [("v", f) for f in range(KT)] + \
        [("vg", f) for f in range(KT)] + in_turn("u", "gb") + in_turn("r", "ga") + [("wo", f) for f in range(KT)]
    zcol = {"k": CK, "q": CQ, "v": CV, "vg": CVG, "u": CU, "gb": CGB, "r": CR, "ga": CGA, "wo": 0}
    zpos = {tile: n for n, tile in enumerate(ztiles)}
    NFRONT = len(ztiles) // 2
    ZBANKS = 4
    zby = ["vector" if kind in ("r", "wo") else "scalar" for kind, _ in ztiles]

    def z(kind, *fs):
        return [("z", kind, f) for f in fs]

    plan = ["vec"] + [("nT", f) for f in range(KT)] + ["gk"] + [("xT", f) for f in range(KT)] + \
        [("bias", 0), ("bias", 1)] + [("pT", k) for k in range(PK)] + ["wsp"] + z("k", *range(H)) + \
        [("la", h) for h in range(H)] + z("q", *range(H)) + z("v", 0)
    for f in range(1, KT):
        plan += z("v", f) + [("vT", f - 1)]
    between = [[("kdT", 0), ("kdT", 1), ("kdT", 2)], [("att", 0), ("att", 1)]] + \
        [[("dS", c, 0), ("dS", c, 1)] for c in range(NCH)] + [[("o", b, 0), ("o", b, 1)] for b in range(NB)]
    for f in range(KT):
        plan += z("vg", f) + [("vT", KT - 1) if f == 0 else ("vgT", f - 1)] + between[f]
    for c in range(0, KT, 2):
        plan += z("u", c) + ([("vgT", KT - 1)] if c == 0 else []) + [("kv", c, 0), ("kv", c, 1)] + z("u", c + 1) + \
            [("kv", c + 1, 0), ("kv", c + 1, 1), ("so", c)] + z("gb", c) + [("so", c + 1)] + z("gb", c + 1) + \
            [("mix", c), ("mix", c + 1)]
    plan += [("soT", 0), ("soT", 1)]
    for c in range(0, KT, 2):
        plan += z("r", c, c + 1) + z("ga", c, c + 1) + [("oT", c), ("oT", c + 1)]
    plan += z("wo", *range(KT))
    assert [x[1:] for x in plan if x[0] == "z"] == ztiles

    misc = [x for x in plan if x[0] != "z"]
    mpos = {x: n for n, x in enumerate(misc)}
    mby = ["scalar" if x[0] in ("gk", "xT", "pT", "kdT", "o", "so", "soT") or x == "gk" else "vector" for x in misc]

    ctx = ExitStack()
    with ctx:
        def sb(name, shape, dt=F32):
            return ctx.enter_context(nc.sbuf_tensor(name, shape, dt))

        def sem(name):
            return ctx.enter_context(nc.semaphore(name))

        bank = [ctx.enter_context(nc.psum_tensor(f"bank{i}", [P, 512], F32)) for i in range(8)]

        def view(tensor, at, *shape):
            n = int(np.prod(shape))
            v = tensor[:, at:at + n]
            if len(shape) == 1:
                return v
            names = "abcd"[:len(shape)]
            return v.rearrange("p (%s) -> p %s" % (" ".join(names), " ".join(names)),
                               **dict(zip(names[1:], shape[1:])))

        ring = sb("ring", [P, SLOTS * SLOT])
        hT = sb("hT", [P, KT * T])
        ident = sb("ident", [P, P])
        ones = sb("ones", [P, P])
        before = sb("before", [P, P])
        upto = sb("upto", [P, P])
        vecT = sb("vecT", [P, 40])
        biasT = sb("biasT", [P, 3 * KT * E])
        iota_c = sb("iota_c", [P, CAP])
        iota_e = sb("iota_e", [P, E])
        rank = sb("rank", [P, (NB + 1) * (E + 1)])
        wts = sb("wts", [P, (NB + 1) * (E + 1)])
        small = sb("small", [P, 128])
        ov_table = sb("ov_table", [P, 2 * MAX_OV + 1])
        ov_table_i = sb("ov_table_i", [P, 2 * MAX_OV + 1], I32)
        wrt = sb("wrt", [P, KT * E])
        brrow = sb("brrow", [P, E])
        pT = sb("pT", [P, PK * T])
        g2row = sb("g2row", [P, D])
        regA = sb("regA", [P, KT * T])
        regB = sb("regB", [P, (NB + 1) * D])
        regC = sb("regC", [P, (NB + 1) * D])
        regD = sb("regD", [P, KT * T])
        regE = sb("regE", [P, max(2 * D + H * T, (KT + 2) * T + MAX_OV * E)])
        w00 = sb("w00", [NS, MH])
        dw = sb("dw", [NS, MH * NS])
        rk = sb("rk", [P, NB + 1])

        hTv = view(hT, 0, KT, T)
        slot = [view(ring, s * SLOT, SLOT) for s in range(SLOTS)]
        by_k = [s.rearrange("p (k f) -> p k f", k=2) for s in slot]
        by_col = [s.rearrange("p (k f) -> p k f", k=KT) for s in slot]
        biasv = view(biasT, 0, 3, KT, E)
        rankv, wtsv = view(rank, 0, NB + 1, E + 1), view(wts, 0, NB + 1, E + 1)
        wrtv, pTv = view(wrt, 0, KT, E), view(pT, 0, PK, T)

        place = [FRONT_SLOTS * SLOT, (SLOTS - LATE_SLOTS) * SLOT]

        def front_buffer(*shape, late=False):
            at = place[late]
            place[late] += int(np.prod(shape))
            assert place[late] <= (SLOTS - LATE_SLOTS + late * LATE_SLOTS) * SLOT
            return view(ring, at, *shape)

        x_tok = front_buffer(NB + 1, D)
        S_ver = view(ring, FRONT_SLOTS * SLOT, NCH - 1, H * DV)
        S_last = front_buffer(H * DV)
        at_b = place[0]
        bT = front_buffer(H, T)
        att = view(ring, at_b, NB, H, P)
        e1 = front_buffer(H, T)
        qT = front_buffer(H, T)
        kT = front_buffer(H, T)
        at_junk = place[0]
        keT = front_buffer(H, T)
        kdT = front_buffer(H, T)
        v_tok = front_buffer(NB + 1, D)
        kd_tok = front_buffer(NB + 1, H * DK)
        kmask = front_buffer(2, H * DK)
        t = [front_buffer(T, late=True) for _ in range(5)]
        WT = front_buffer(MH, P, late=True)
        st = front_buffer(2, H * DV, late=True)
        attmask = front_buffer(P, late=True)
        scanmask = t[4]

        nT, acc = view(regA, 0, KT, T), view(regA, 0, KT, T)
        bias_rows = view(regB, 0, 3, D)
        o_tok, x2 = view(regB, 0, NB + 1, D), view(regB, 0, NB + 1, D)
        xn, vn, hgT = view(regC, 0, NB + 1, D), view(regC, 0, NB + 1, D), view(regC, 0, KT, T)
        mixT = view(regD, 0, KT, T)
        wgk, wgk2, gkT = view(regD, 0, KT, RANK), view(regD, P, H * DK), view(regD, P + H * DK, T)
        vrows, wsp = view(regD, 1024, P), view(regD, 1024 + P, MH, P)
        p_tok = view(sb("p_tok", [P, (NB + 1) * DP]), 0, NB + 1, DP)
        vngrow, vnbrow, bspT = view(regE, 0, D), view(regE, D, D), view(regE, 2 * D, H, T)
        junk = view(ring, at_junk, D)

        EC = KT * CAP
        gs, us, sg, xe = (view(regC, i * EC, KT, CAP) for i in range(4))
        Ssel, Swt = (view(regC, 4 * EC + i * (NB + 1) * CAP, NB + 1, CAP) for i in range(2))
        yT, ye = view(regD, 0, KT, CAP), view(regD, EC, D)
        pwT = view(regE, 0, KT, T)
        SWT = [view(regE, KT * T + i * T, T) for i in range(2)]
        cols = [0]

        def small_tile(n):
            cols[0] += n
            assert cols[0] <= 128
            return small[:, cols[0] - n:cols[0]]

        xss, xrs = small_tile(NB + 1), small_tile(NB + 1)
        decay, sdecay = small_tile(H * NCH).rearrange("p (h c) -> p h c", h=H), \
            sb("sdecay", [P, H * NS])[:].rearrange("p (h s) -> p h s", h=H)
        oss, ors = small_tile((NB + 1) * H), small_tile((NB + 1) * H)
        vstat, vmv, vrs = small_tile(12), small_tile(2 * (NB + 1)), small_tile(NB + 1)
        hss, hrs = small_tile(2 * (NB + 1)), small_tile(NB + 1)
        yss = small_tile(NB + 1)
        oST = sb("oST", [P, 2 * H * NS])[:].rearrange("p (j s) -> p j s", s=NS)

        rt = [KT * T]

        def route_tile(*shape):
            rt[0] += int(np.prod(shape))
            assert rt[0] <= (NB + 1) * D
            return view(regC, rt[0] - int(np.prod(shape)), *shape)

        lg = route_tile(NB + 1, E)
        m8, ew = route_tile(NB + 1, 8), route_tile(NB + 1, TOP_K)
        idx = route_tile(NB + 1, 8)
        idx_f = route_tile(NB + 1, TOP_K)
        esum = route_tile(NB + 1)
        negm = route_tile(NB + 1)
        hit = route_tile(TOP_K, E)
        selm = route_tile(NB + 1, E)
        cnt, nov, nov_end = sb("cnt", [P, E])[:], sb("nov", [P, E])[:], sb("nov_end", [P, E])[:]
        ovt = view(regE, (KT + 2) * T, MAX_OV, E)

        sqT, n3T, y3T = view(regC, 0, KT, T), view(regD, 0, KT, T), view(regA, 0, KT, T)
        gt = [view(regC, (KT + i) * T, T) for i in range(3)]
        rb = view(regE, KT * T, T)

        ld_x, ld_vec, ld_gk, ld_bias, ld_p = sem("ld_x"), sem("ld_vec"), sem("ld_gk"), sem("ld_bias"), sem("ld_p")
        ld_wsp, ld_rows, ld_router = sem("ld_wsp"), sem("ld_rows"), sem("ld_router")
        slot_loaded = [sem(f"slot_loaded{s}") for s in range(SLOTS)]
        st_loaded = [sem(f"st_loaded{s}") for s in range(2)]
        st_stored = [sem(f"st_stored{s}") for s in range(2)]
        sp_stored, vn_stored, y_stored = sem("sp_stored"), sem("vn_stored"), sem("y_stored")
        consts_ready = sem("consts_ready")
        pool_step, dve_step, act_step = sem("pool_step"), sem("dve_step"), sem("act_step")
        z_done, misc_done, chunk_used = sem("z_done"), sem("misc_done"), sem("chunk_used")
        z_free = {"scalar": sem("z_free_scalar"), "vector": sem("z_free_vector")}
        misc_free = {"scalar": sem("misc_free_scalar"), "vector": sem("misc_free_vector")}
        x_squares, x_scale_sum, x_root = sem("x_squares"), sem("x_scale_sum"), sem("x_root")
        xn_ready = sem("xn_ready")
        abs_ready, exp_ready, la_ready, cum_ready, back_ready = (
            sem(n) for n in ("abs_ready", "exp_ready", "la_ready", "cum_ready", "back_ready"))
        decays_ready, gla_in_ready = sem("decays_ready"), sem("gla_in_ready")
        att_ready, state_ready = sem("att_ready"), sem("state_ready")
        o_squares, o_sum, o_root, o_ready = sem("o_squares"), sem("o_sum"), sem("o_root"), sem("o_ready")
        vn_var, vn_root, vn_scaled, vn_ready = sem("vn_var"), sem("vn_root"), sem("vn_scaled"), sem("vn_ready")
        dw_ready, bsp_ready = sem("dw_ready"), sem("bsp_ready")
        kmask_ready, st_ready = sem("kmask_ready"), sem("st_ready")
        b_done, a_done = sem("b_done"), sem("a_done")
        r_sig = sem("r_sig")
        h_ready, hg_ready, hrow_done, router_done = sem("h_ready"), sem("hg_ready"), sem("hrow_done"), sem("router_done")
        h_squares, h_sum, h_root = sem("h_squares"), sem("h_sum"), sem("h_root")
        top_ready, top_exp, sel_ready, rank_done = sem("top_ready"), sem("top_exp"), sem("sel_ready"), sem("rank_done")
        zeros_ready, x2_ready, table_ready = sem("zeros_ready"), sem("x2_ready"), sem("table_ready")
        pw_done, pw_ready = sem("pw_done"), sem("pw_ready")
        h2_ready, sq_ready, rms_done, rms_sum, rms_root = (
            sem(n) for n in ("h2_ready", "sq_ready", "rms_done", "rms_sum", "rms_root"))
        gate_done, gate_free, gate_pre, gate_act, h3_ready = (
            sem(n) for n in ("gate_done", "gate_free", "gate_pre", "gate_act", "h3_ready"))
        ysq_ready, y_stat, y_sum, y_root, yrow_done = (
            sem(n) for n in ("ysq_ready", "y_stat", "y_sum", "y_root", "yrow_done"))
        yrow_ready = {"vector": sem("yrow_ready_vector"), "scalar": sem("yrow_ready_scalar")}
        h3_sum, y_scale = sem("h3_sum"), sem("y_scale")
        ojunk, hjunk = [kT[:, h, 0:DV] for h in range(2)], [view(regE, i * 512, 512) for i in range(4)]
        tail_step = sem("tail_step")

        class Pass:
            def __init__(self, kind):
                self.selected = sem(f"{kind}_selected")
                self.gathered = sem(f"{kind}_gathered")
                self.xe_ready = sem(f"{kind}_xe_ready")
                self.g_ready = sem(f"{kind}_g_ready")
                self.sig_ready = sem(f"{kind}_sig_ready")
                self.mid_ready = sem(f"{kind}_mid_ready")
                self.y_biased = sem(f"{kind}_y_biased")
                self.turned = sem(f"{kind}_turned")
                self.ye_ready = sem(f"{kind}_ye_ready")
                self.scattered = sem(f"{kind}_scattered")
                self.added = sem(f"{kind}_added")
                self.vector_step = sem(f"{kind}_vector_step")

        main, extra = Pass("main"), Pass("extra")
        main.used, extra.used = chunk_used, sem("extra_used")
        extra_loaded = [sem(f"extra_loaded{s}") for s in range(PER_EXPERT)]

        def freed(by, free, n):
            return free[by[n]], by[:n + 1].count(by[n])

        def zcount(tile):
            return zpos[tile] + 1

        def mcount(x):
            return mpos[x] + 1

        def zbank(tile):
            return bank[zpos[tile] % ZBANKS]

        def mbank(x):
            return bank[ZBANKS + mpos[x] % ZBANKS]

        FRONT_LOADS = [len(range(s, NFRONT, FRONT_SLOTS)) for s in range(FRONT_SLOTS)] + [0] * (SLOTS - FRONT_SLOTS)

        def expert_loads(m):
            return 16 * (FRONT_LOADS[m % SLOTS] + m // SLOTS + 1)

        LAST = E * PER_EXPERT
        K3 = [(w_gate, "gate"), (w_up, "up"), (w_down, "down")]

        def chunk_source(e, c):
            w = K3[c // 4][0]
            return w[0, e, (c % 4) * 2 * P:(c % 4 + 1) * 2 * P, :].rearrange("(k p) f -> p k f", p=P)

        def chained(eng, s, base=0):
            n = [0]

            def link(ins):
                ins.then_inc(s, 1)
                n[0] += 1
                eng.wait_ge(s, base + n[0])
            link.count = n
            return link

        block = ctx.enter_context(nc.Block())

        @block.sync
        def _(sp):
            for b, rows, t0 in BLOCKS:
                src = x_prompt[0, t0:t0 + rows, :] if b < NB else x_sample[:, 0, :]
                sp.dma_start(x_tok[0:rows, b, :], src).then_inc(ld_x, 16)
            for n in range(NFRONT):
                kind, f = ztiles[2 * n]
                if n >= FRONT_SLOTS:
                    sp.wait_ge(z_done, 2 * (n - FRONT_SLOTS + 1))
                w = w_o[0] if kind == "wo" else w_in[0]
                c0 = zcol[kind] + f * P
                sp.dma_start(by_col[n % FRONT_SLOTS], w[:, c0:c0 + 2 * P].rearrange("(k p) f -> p k f", p=P))\
                    .then_inc(slot_loaded[n % FRONT_SLOTS], 16)

            def load(m):
                sp.dma_start(by_k[m % SLOTS], chunk_source(m // PER_EXPERT, m % PER_EXPERT))\
                    .then_inc(slot_loaded[m % SLOTS], 16)

            for m in range(SLOTS):
                if m < FRONT_SLOTS:
                    sp.wait_ge(z_done, 2 * (max(range(m, NFRONT, FRONT_SLOTS)) + 1))
                elif m == FRONT_SLOTS:
                    sp.wait_ge(misc_done, mcount(("so", NS - 1)))
                    sp.wait_ge(sp_stored, 16)
                    sp.wait_ge(o_ready, 1)
                elif m == SLOTS - LATE_SLOTS:
                    sp.wait_ge(a_done, KT)
                    sp.wait_ge(st_stored[0], 16 * NS // 2)
                    sp.wait_ge(st_stored[1], 16 * NS // 2)
                load(m)
            TURN = UNROLL * PER_EXPERT
            with sp.Fori(0, ROUNDS - 1) as i:
                for r in range(SLOTS, SLOTS + TURN):
                    sp.wait_ge(chunk_used, i * TURN + (r - SLOTS + 1))
                    sp.dma_start(by_k[r % SLOTS], chunk_source(i * UNROLL + r // PER_EXPERT, r % PER_EXPERT))\
                        .then_inc(slot_loaded[r % SLOTS], 16)
            for m in range(SLOTS + TURN * (ROUNDS - 1), LAST):
                sp.wait_ge(chunk_used, m - SLOTS + 1)
                load(m)

            sp.wait_ge(table_ready, 1)
            n_extra = sp.value_load(ov_table_i[0:1, 2 * MAX_OV:2 * MAX_OV + 1], min_val=0, max_val=MAX_OV)
            with sp.If(n_extra > 0):
                sp.wait_ge(chunk_used, LAST)
                with sp.Fori(0, n_extra) as i:
                    e = sp.value_load(ov_table_i[0:1, bass.ds(i, 1)], min_val=0, max_val=E - 1)
                    for c in range(PER_EXPERT):
                        sp.wait_ge(extra.used, i * PER_EXPERT + 1)
                        sp.dma_start(by_k[c], chunk_source(e, c)).then_inc(extra_loaded[c], 16)
            sp.wait_ge(extra.used, n_extra * PER_EXPERT + 1)

            for m in range(LAST, LAST + 5):
                sp.wait_ge(chunk_used, m - SLOTS + 1)
                src = w_ple_gate[0, :, (m - LAST) * 2 * P:(m - LAST + 1) * 2 * P].rearrange("(k p) f -> p k f", p=P) \
                    if m < LAST + 4 else w_ple_proj[0].rearrange("(k p) f -> p k f", p=P)
                dst = by_col[m % SLOTS] if m < LAST + 4 else by_k[m % SLOTS]
                sp.dma_start(dst, src).then_inc(slot_loaded[m % SLOTS], 16)

            for b, rows, t0 in BLOCKS:
                sp.wait_ge(yrow_ready["vector"], b + 1)
                sp.wait_ge(yrow_ready["scalar"], b + 1)
                dst = y_prompt[0, t0:t0 + rows, :] if b < NB else y_sample[:, 0, :]
                sp.dma_start(dst, x2[0:rows, b, :]).then_inc(y_stored, 16)
            sp.wait_ge(y_stored, 16 * len(BLOCKS))

        @block.gpsimd
        def _(pool):
            link = chained(pool, pool_step)
            pool.memset(ident[:, :], 0.0)
            pool.memset(before[:, :], 1.0)
            pool.memset(upto[:, :], 1.0)
            pool.memset(ones[:, :], 1.0)
            pool.memset(scanmask, 1.0)
            link(pool.memset(vrows, 0.0))
            pool.affine_select(out=ident[:, :], in_=ident[:, :], compare_op=ALU.not_equal, fill=1.0, base=0,
                               pattern=[[-1, P]], channel_multiplier=1)
            pool.affine_select(out=before[:, :], in_=before[:, :], compare_op=ALU.is_gt, fill=0.0, base=0,
                               pattern=[[1, P]], channel_multiplier=-1)
            pool.affine_select(out=upto[:, :], in_=upto[:, :], compare_op=ALU.is_ge, fill=0.0, base=0,
                               pattern=[[1, P]], channel_multiplier=-1)
            pool.memset(scanmask[:, 0:L:GLA_CHUNK], 0.0)
            link(pool.memset(scanmask[:, L:T], 0.0))
            link(pool.tensor_copy(attmask, upto[:, :]))
            link(pool.memset(attmask[0:GLA_CHUNK, GLA_CHUNK:P], 0.0))
            pool.iota(iota_c[:, :], [[1, CAP]], base=0, channel_multiplier=0, allow_small_or_imprecise_dtypes=True)
            link(pool.iota(iota_e[:, :], [[1, E]], base=0, channel_multiplier=0, allow_small_or_imprecise_dtypes=True))
            pool.memset(rank[:, :], -1.0)
            pool.memset(wts[:, :], 0.0).then_inc(consts_ready, 1)
            for b in range(2):
                pool.dma_start(st[:, b, :].rearrange("p (h v) -> p h v", h=H),
                               state_gla[0, b].rearrange("h k v -> k h v")).then_inc(st_loaded[b], 16)
            pool.wait_ge(ld_rows, 16 * 3)
            link(pool.tensor_copy(bspT[:, :, P:2 * P], bspT[:, :, 0:P]))
            pool.tensor_copy(bspT[:, :, L:T], bspT[:, :, 0:1].to_broadcast([P, H, NS])).then_inc(bsp_ready, 1)
            for b, rows, _ in BLOCKS:
                pool.wait_ge(vn_scaled, b + 1)
                link(pool.tensor_tensor(vn[0:rows, b, :], vn[0:rows, b, :], vngrow[0:rows, :], ALU.mult))
                pool.tensor_tensor(vn[0:rows, b, :], vn[0:rows, b, :], vnbrow[0:rows, :], ALU.add)\
                    .then_inc(vn_ready, 1)
            pool.wait_ge(vn_ready, NB + 1)
            pool.dma_start(mix_v_sample[0, :, 0, :], vn[0:NS, NB, :]).then_inc(vn_stored, 16)
            pool.wait_ge(state_ready, 2 * NCH)
            pool.dma_start(st_prompt[0, 0].rearrange("h k v -> k h v"),
                           S_last.rearrange("p (h v) -> p h v", h=H)).then_inc(sp_stored, 16)
            for b in range(NS):
                pool.wait_ge(st_ready, 2 * (b + 1))
                pool.dma_start(st_sample[0, b].rearrange("h k v -> k h v"),
                               st[:, b % 2, :].rearrange("p (h v) -> p h v", h=H)).then_inc(st_stored[b % 2], 16)
                if b + 2 < NS:
                    pool.wait_ge(st_stored[b % 2], 16 * (b // 2 + 1))
                    pool.wait_ge(misc_done, mcount(("so", b)))
                    pool.dma_start(st[:, b % 2, :].rearrange("p (h v) -> p h v", h=H),
                                   state_gla[0, b + 2].rearrange("h k v -> k h v")).then_inc(st_loaded[b % 2], 16)
            pool.wait_ge(z_done, zcount(("ga", KT - 1)))
            pool.memset(view(regA, 0, KT * T), 0.0)
            pool.wait_ge(misc_done, mcount(("oT", KT - 1)))
            pool.memset(x2[:, NB, :], 0.0)
            pool.wait_ge(b_done, KT)
            pool.memset(SWT[1], 0.0)
            pool.wait_ge(z_done, zcount(("wo", KT - 1)))
            pool.memset(view(regD, 0, EC), 0.0).then_inc(zeros_ready, 1)
            pool.wait_ge(vn_stored, 16)
            pool.wait_ge(sp_stored, 16)
            pool.wait_ge(st_stored[0], 16 * NS // 2)
            pool.wait_ge(st_stored[1], 16 * NS // 2)

        @block.tensor
        def _(pe):
            mm = nc.tensor.matmul
            turn = nc.tensor.transpose

            def z_tile(kind, f):
                n = zpos[(kind, f)]
                if n >= ZBANKS:
                    pe.wait_ge(*freed(zby, z_free, n - ZBANKS))
                chunk, half = n // 2, n % 2
                s = chunk % FRONT_SLOTS
                if half == 0:
                    pe.wait_ge(slot_loaded[s], 16 * (chunk // FRONT_SLOTS + 1))
                if (kind, f) == ("k", 0):
                    pe.wait_ge(misc_free["vector"], mby[:mcount(("nT", KT - 1))].count("vector"))
                if (kind, f) == ("wo", 0):
                    pe.wait_ge(a_done, KT)
                rhs = mixT if kind == "wo" else nT
                for k in range(KT):
                    ins = mm(zbank((kind, f))[:, 0:T], by_col[s][:, k, half * P:(half + 1) * P], rhs[:, k, :],
                             start=(k == 0), stop=(k == KT - 1))
                ins.then_inc(z_done, 1)

            def misc_step(x):
                n = mpos[x]
                if n >= ZBANKS:
                    pe.wait_ge(*freed(mby, misc_free, n - ZBANKS))
                out = mbank(x)
                kind, *at = x if isinstance(x, tuple) else (x,)
                f = at[0] if at else None
                if kind == "vec":
                    pe.wait_ge(consts_ready, 1)
                    pe.wait_ge(ld_vec, 16 * 6)
                    ins = turn(out[:, 0:40], vrows[0:40, :], ident[0:40, 0:40])
                elif kind in ("nT", "xT"):
                    src = xn if kind == "nT" else x_tok
                    if f == 0 and kind == "nT":
                        pe.wait_ge(xn_ready, 1)
                    for b, rows, t0 in BLOCKS:
                        ins = turn(out[:, t0:t0 + rows], src[0:rows, b, f * P:(f + 1) * P], ident[0:rows, 0:rows])
                elif kind == "gk":
                    pe.wait_ge(ld_gk, 32)
                    pe.wait_ge(misc_free["vector"], mby[:mcount(("nT", KT - 1))].count("vector"))
                    for k in range(KT):
                        ins = mm(out[0:RANK, 0:T], wgk[:, k, :], nT[:, k, :], start=(k == 0), stop=(k == KT - 1))
                elif kind == "bias":
                    pe.wait_ge(ld_bias, 48)
                    for j in range(12):
                        m, ff = divmod(12 * f + j, KT)
                        ins = turn(out[:, j * E:(j + 1) * E], bias_rows[0:E, m, ff * P:(ff + 1) * P], ident[0:E, 0:E])
                elif kind == "pT":
                    pe.wait_ge(ld_p, 48)
                    for b, rows, t0 in BLOCKS:
                        ins = turn(out[:, t0:t0 + rows], p_tok[0:rows, b, f * P:(f + 1) * P], ident[0:rows, 0:rows])
                elif kind == "wsp":
                    pe.wait_ge(ld_wsp, 32)
                    for h in range(MH):
                        ins = turn(out[:, h * P:(h + 1) * P], wsp[:, h, :], ident[:, :])
                elif kind == "la":
                    pe.wait_ge(*freed(mby, misc_free, mpos["gk"]))
                    ins = mm(out[:, 0:T], wgk2[0:RANK, f * P:(f + 1) * P], gkT[0:RANK, :], start=True, stop=True)
                elif kind in ("vT", "vgT"):
                    tile = ("v" if kind == "vT" else "vg", f)
                    pe.wait_ge(*freed(zby, z_free, zpos[tile]))
                    src = t[f % 2 + (2 if kind == "vgT" else 0)]
                    for b, rows, t0 in BLOCKS:
                        ins = turn(out[0:rows, b * P:(b + 1) * P], src[:, t0:t0 + rows], ident[:, :])
                elif kind == "kdT":
                    pe.wait_ge(gla_in_ready, 1)
                    b, rows, t0 = BLOCKS[f]
                    src = kdT if f < NB else kT
                    for h in range(H):
                        ins = turn(out[0:rows, h * DK:(h + 1) * DK], src[:, h, t0:t0 + rows], ident[:, :])
                elif kind == "att":
                    t0 = f * P
                    for h in range(H):
                        ins = mm(out[:, h * P:(h + 1) * P], keT[:, h, t0:t0 + P], qT[:, h, t0:t0 + P],
                                 start=True, stop=True)
                elif kind == "dS":
                    c, i = at
                    b, r0 = c * GLA_CHUNK // P, c * GLA_CHUNK % P
                    pe.wait_ge(*freed(mby, misc_free, mpos[("kdT", b)]))
                    pe.wait_ge(*freed(mby, misc_free, mpos[("vT", KT - 1)]))
                    for h in (2 * i, 2 * i + 1):
                        ins = mm(out[:, (h % 2) * DV:(h % 2 + 1) * DV],
                                 kd_tok[r0:r0 + GLA_CHUNK, b, h * DK:(h + 1) * DK],
                                 v_tok[r0:r0 + GLA_CHUNK, b, h * DV:(h + 1) * DV], start=True, stop=True)
                elif kind == "o":
                    b, i = at
                    pe.wait_ge(att_ready, b + 1)
                    pe.wait_ge(state_ready, 2 * min(2 * b + 1, NCH - 1))
                    for h in (2 * i, 2 * i + 1):
                        o0 = (h % 2) * DV
                        ins = mm(out[:, o0:o0 + DV], att[:, b, h, :], v_tok[:, b, h * DV:(h + 1) * DV],
                                 start=True, stop=False, skip_group_check=True)
                        for c in (2 * b, 2 * b + 1):
                            if c > 0:
                                r0, t0 = c * GLA_CHUNK % P, c * GLA_CHUNK
                                ins = mm(out[r0:r0 + GLA_CHUNK, o0:o0 + DV], qT[:, h, t0:t0 + GLA_CHUNK],
                                         S_ver[:, c - 1, h * DV:(h + 1) * DV], start=False, stop=True,
                                         skip_group_check=True)
                elif kind == "kv":
                    b, i = at
                    if i == 0:
                        pe.wait_ge(kmask_ready, b + 1)
                    for h in (2 * i, 2 * i + 1):
                        ins = mm(out[:, (h % 2) * DV:(h % 2 + 1) * DV], kmask[0:NS, b % 2, h * DK:(h + 1) * DK],
                                 v_tok[0:NS, NB, h * DV:(h + 1) * DV], start=True, stop=True)
                elif kind == "so":
                    pe.wait_ge(st_ready, 2 * (f + 1))
                    for j in range(2 * H):
                        ins = mm(out[:, j:j + 1], st[:, f % 2, j * P:(j + 1) * P], qT[:, j // 2, L + f:L + f + 1],
                                 start=True, stop=True)
                elif kind == "soT":
                    if f == 0:
                        pe.wait_ge(*freed(mby, misc_free, mpos[("so", NS - 1)]))
                    for j in range(4):
                        ins = turn(out[0:NS, j * P:(j + 1) * P], oST[:, 4 * f + j, :], ident[:, :])
                elif kind == "mix":
                    if f == 0:
                        pe.wait_ge(vn_ready, NB + 1)
                        pe.wait_ge(dw_ready, 1)
                    h = f * MH // KT
                    for b in range(NB):
                        mm(out[:, b * P:(b + 1) * P], vn[:, b, f * P:(f + 1) * P], WT[:, h, :], start=True, stop=True)
                    ins = mm(out[:, L:T], vn[0:NS, NB, f * P:(f + 1) * P], dw[:, h * NS:(h + 1) * NS],
                             start=True, stop=True)
                elif kind == "oT":
                    pe.wait_ge(o_ready, 2)
                    for b, rows, t0 in BLOCKS:
                        ins = turn(out[:, t0:t0 + rows], o_tok[0:rows, b, f * P:(f + 1) * P], ident[0:rows, 0:rows])
                ins.then_inc(misc_done, 1)

            for x in plan:
                if x[0] == "z":
                    z_tile(*x[1:])
                else:
                    misc_step(x)

            pe.wait_ge(h_ready, KT)
            for n in range(len(misc) - ZBANKS, len(misc)):
                pe.wait_ge(*freed(mby, misc_free, n))
            for b, rows, t0 in BLOCKS:
                for i in range(2):
                    for j in range(HALF):
                        f = i * HALF + j
                        ins = turn(bank[2 + 2 * b + i][0:rows, j * P:(j + 1) * P], hTv[:, f, t0:t0 + rows], ident[:, :])
                    ins.then_inc(hrow_done, 1)
            pe.wait_ge(hg_ready, KT)
            pe.wait_ge(ld_router, 48)
            for b, rows, t0 in BLOCKS:
                for k in range(KT):
                    ins = mm(bank[0][0:rows, b * E:(b + 1) * E], hgT[:, k, t0:t0 + rows], wrtv[:, k, :],
                             start=(k == 0), stop=(k == KT - 1))
            ins.then_inc(router_done, 1)
            pe.wait_ge(sel_ready, 1)
            for b in range(NB + 1):
                for c in range(b + 1):
                    mm(bank[1][:, b * E:(b + 1) * E], (before if c == b else ones)[:, :], selm[:, c, :],
                       start=(c == 0), stop=(c == b))
            for c in range(NB + 1):
                ins = mm(bank[1][:, (NB + 1) * E:(NB + 2) * E], ones[:, :], selm[:, c, :],
                         start=(c == 0), stop=(c == NB))
            ins.then_inc(rank_done, 1)

            GB, UB, DB, XB = (0, 1), (2, 3), (4, 5), (6, 7)

            def cols_of(f):
                return slice((f % HALF) * CAP, (f % HALF + 1) * CAP)

            def weights_step(ps, banks, rhs, chunks):
                for s, loaded, value, k0 in chunks:
                    pe.wait_ge(loaded, value)
                    for k in (k0, k0 + 1):
                        for f in range(KT):
                            ins = mm(bank[banks[f // HALF]][:, cols_of(f)], by_k[s][:, k % 2, f * P:(f + 1) * P],
                                     rhs[:, k, :], start=(k == 0 and f % HALF == 0), stop=(k == KT - 1),
                                     skip_group_check=True)
                    ins.then_inc(ps.used, 1)

            def gather(ps, item):
                pe.wait_ge(ps.selected, item + 1)
                for f in range(KT):
                    for b in range(NB + 1):
                        mm(bank[XB[f // HALF]][:, cols_of(f)], x2[:, b, f * P:(f + 1) * P], Ssel[:, b, :],
                           start=(b == 0), stop=(b == NB))
                for b, rows, t0 in BLOCKS:
                    o0 = HALF * CAP + (P if b == NB else 0)
                    ins = turn(bank[XB[b % 2]][0:CAP, o0:o0 + rows], Swt[0:rows, b, :], ident[0:rows, 0:rows])
                ins.then_inc(ps.gathered, 1)

            def turn_y(ps, n):
                pe.wait_ge(ps.y_biased, n)
                for f in range(KT):
                    ins = turn(bank[XB[f // HALF]][0:CAP, (f % HALF) * P:(f % HALF + 1) * P], yT[:, f, :], ident[:, :])
                ins.then_inc(ps.turned, 1)

            def scatter(ps, n, parity):
                pe.wait_ge(ps.ye_ready, n + 1)
                for f in range(KT):
                    if f >= 2:
                        pe.wait_ge(ps.added, n * KT + f - 1)
                    mm(bank[DB[f % 2]][:, 0:T], ye[0:CAP, f * P:(f + 1) * P], SWT[parity][0:CAP, :],
                       start=True, stop=True).then_inc(ps.scattered, 1)

            def main_chunks(u, i, c):
                r = u * PER_EXPERT + c
                loads = 16 * UNROLL * PER_EXPERT // SLOTS
                return (r % SLOTS, slot_loaded[r % SLOTS], i * loads + expert_loads(r), 2 * (c % 4))

            pe.wait_ge(x2_ready, 1)
            pe.wait_ge(zeros_ready, 1)
            pe.sem_inc(extra.used, 1)
            gather(main, 0)
            with pe.Fori(0, ROUNDS) as i:
                for u in range(UNROLL):
                    j = i * UNROLL + u
                    pe.wait_ge(main.xe_ready, j + 1)
                    weights_step(main, GB, xe, [main_chunks(u, i, c) for c in range(0, 4)])
                    turn_y(main, j + 1)
                    weights_step(main, UB, xe, [main_chunks(u, i, c) for c in range(4, 6)])
                    scatter(main, j, (u + 1) % 2)
                    weights_step(main, UB, xe, [main_chunks(u, i, c) for c in range(6, 8)])
                    gather(main, j + 1)
                    pe.wait_ge(main.mid_ready, j + 1)
                    pe.wait_ge(main.added, j * KT + KT)
                    weights_step(main, DB, gs, [main_chunks(u, i, c) for c in range(8, 12)])
            pe.wait_ge(main.xe_ready, E + 1)
            turn_y(main, E + 1)
            scatter(main, E, 1)

            pe.wait_ge(table_ready, 1)
            n_extra = pe.value_load(ov_table_i[0:1, 2 * MAX_OV:2 * MAX_OV + 1], min_val=0, max_val=MAX_OV)
            with pe.If(n_extra > 0):
                pe.wait_ge(main.added, (E + 1) * KT)
                with pe.Fori(0, n_extra) as i:
                    def extra_chunks(c0, c1):
                        return [(c, extra_loaded[c], i * 16 + 16, 2 * (c % 4)) for c in range(c0, c1)]
                    gather(extra, i)
                    pe.wait_ge(extra.xe_ready, i + 1)
                    weights_step(extra, GB, xe, extra_chunks(0, 4))
                    weights_step(extra, UB, xe, extra_chunks(4, 8))
                    pe.wait_ge(extra.mid_ready, i + 1)
                    weights_step(extra, DB, gs, extra_chunks(8, 12))
                    turn_y(extra, i + 1)
                    scatter(extra, i, 0)
                    pe.wait_ge(extra.added, i * KT + KT)

            loaded5 = slot_loaded[(LAST + 4) % SLOTS]
            pe.wait_ge(loaded5, expert_loads(LAST + 4))
            wpp = by_k[(LAST + 4) % SLOTS]
            for f in range(KT):
                if f >= 4:
                    pe.wait_ge(pw_ready, f - 3)
                for k in range(PK):
                    ins = mm(bank[f % 4][:, 0:T], wpp[:, k, f * P:(f + 1) * P], pTv[:, k, :],
                             start=(k == 0), stop=(k == PK - 1))
                ins.then_inc(pw_done, 1)
            pe.wait_ge(pw_ready, KT)
            pe.wait_ge(h2_ready, KT)
            for k in range(KT):
                pe.wait_ge(sq_ready, k + 1)
                ins = mm(bank[4][:, 0:T], ones[:, :], sqT[:, k, :], start=(k == 0), stop=(k == KT - 1))
            ins.then_inc(rms_done, 1)
            for f in range(KT):
                s = (LAST + f // 2) % SLOTS
                if f % 2 == 0:
                    pe.wait_ge(slot_loaded[s], expert_loads(LAST + f // 2))
                if f >= 4:
                    pe.wait_ge(gate_pre, f - 3)
                for k in range(KT):
                    ins = mm(bank[f % 4][:, 0:T], by_col[s][:, k, (f % 2) * P:(f % 2 + 1) * P], n3T[:, k, :],
                             start=(k == 0), stop=(k == KT - 1))
                ins.then_inc(gate_done, 1)
            pe.wait_ge(ysq_ready, KT)
            for b, rows, t0 in BLOCKS:
                for k in range(KT):
                    ins = mm(bank[5][0:rows, b:b + 1], sqT[:, k, t0:t0 + rows], ones[:, 0:1],
                             start=(k == 0), stop=(k == KT - 1))
            ins.then_inc(y_stat, 1)
            pe.wait_ge(h3_ready, KT)
            for b, rows, t0 in BLOCKS:
                for i in range(2):
                    n = 2 * b + i
                    if n >= 4:
                        pe.wait_ge(yrow_ready["scalar" if i else "vector"], b - 1)
                    for j in range(HALF):
                        f = i * HALF + j
                        ins = turn(bank[n % 4][0:rows, j * P:(j + 1) * P], y3T[:, f, t0:t0 + rows], ident[:, :])
                    ins.then_inc(yrow_done, 1)

        @block.vector
        def _(dve):
            v = nc.vector
            link = chained(dve, dve_step)

            def vec(row, rows=P):
                return vecT[0:rows, row:row + 1]

            def empty(x):
                assert mby[mpos[x]] == "vector"
                return misc_free["vector"]

            dve.wait_ge(misc_done, mcount("vec"))
            v.tensor_copy(vecT[:, 0:40], mbank("vec")[:, 0:40]).then_inc(empty("vec"), 1)
            dve.wait_ge(misc_free["vector"], 1)
            dve.wait_ge(x_squares, NB + 1)
            for b, rows, _ in BLOCKS:
                ins = v.tensor_scalar(xrs[0:rows, b:b + 1], xss[0:rows, b:b + 1], 1.0 / D, EPS, ALU.mult, ALU.add)
            ins.then_inc(x_scale_sum, 1)
            dve.wait_ge(x_root, 1)
            for b, rows, _ in BLOCKS:
                ins = v.reciprocal(xrs[0:rows, b:b + 1], xrs[0:rows, b:b + 1])
            link(ins)
            for b, rows, _ in BLOCKS:
                ins = v.tensor_scalar(xn[0:rows, b, :], x_tok[0:rows, b, :], xrs[0:rows, b:b + 1], None, ALU.mult)
            ins.then_inc(xn_ready, 1)
            for f in range(KT):
                dve.wait_ge(misc_done, mcount(("nT", f)))
                v.tensor_scalar(nT[:, f, :], mbank(("nT", f))[:, 0:T], vec(f), None, ALU.mult)\
                    .then_inc(empty(("nT", f)), 1)
            for i in range(2):
                dve.wait_ge(misc_done, mcount(("bias", i)))
                v.tensor_copy(biasT[:, i * 12 * E:(i + 1) * 12 * E], mbank(("bias", i))[:, 0:12 * E])\
                    .then_inc(empty(("bias", i)), 1)
            dve.wait_ge(misc_done, mcount("wsp"))
            v.tensor_tensor(WT, mbank("wsp")[:, 0:MH * P].rearrange("p (h t) -> p h t", h=MH),
                            upto[:, :].unsqueeze(1).to_broadcast([P, MH, P]), ALU.mult).then_inc(empty("wsp"), 1)
            for h in range(MH):
                ins = v.tensor_scalar(dw[:, h * NS:(h + 1) * NS], ident[0:NS, 0:NS], w00[:, h:h + 1], None, ALU.mult)
            ins.then_inc(dw_ready, 1)

            for h in range(H):
                dve.wait_ge(misc_done, mcount(("la", h)))
                ins = v.tensor_scalar(keT[:, h, :], mbank(("la", h))[:, 0:T], vec(32 + h), None, ALU.add)
                ins.then_inc(empty(("la", h)), 1)
            dve.wait_ge(*freed(mby, misc_free, mpos[("la", H - 1)]))
            v.scalar_tensor_tensor(e1, keT, -1.0, keT, ALU.mult, ALU.max).then_inc(abs_ready, 1)
            dve.wait_ge(la_ready, 1)
            link(v.scalar_tensor_tensor(kdT, keT, 0.0, e1, ALU.min, ALU.subtract))
            for h in range(H):
                ins = v.tensor_tensor_scan(bT[:, h, :], scanmask, kdT[:, h, :], 0.0, ALU.mult, ALU.add)
            ins.then_inc(cum_ready, 1)
            dve.wait_ge(cum_ready, 1)
            by_chunk = lambda a: a[:, :, 0:L].rearrange("p h (c s) -> p h c s", c=NCH)
            for h in range(H):
                bh = bT[:, h, 0:L].rearrange("p (c s) -> p c s", c=NCH)
                ins = v.tensor_tensor(kdT[:, h, 0:L].rearrange("p (c s) -> p c s", c=NCH),
                                      bh[:, :, GLA_CHUNK - 1:GLA_CHUNK].to_broadcast([P, NCH, GLA_CHUNK]), bh,
                                      ALU.subtract)
            ins.then_inc(back_ready, 1)
            dve.wait_ge(decays_ready, 3)
            dve.wait_ge(*freed(zby, z_free, zpos[("q", H - 1)]))
            for h in range(H):
                v.tensor_copy(decay[:, h, :], e1[:, h, GLA_CHUNK - 1:L:GLA_CHUNK])
            v.tensor_copy(sdecay, e1[:, :, L:T])
            v.scalar_tensor_tensor(qT[:, :, 0:L], qT[:, :, 0:L], float(DK) ** -0.5, e1[:, :, 0:L], ALU.mult, ALU.mult)
            v.tensor_scalar(qT[:, :, L:T], qT[:, :, L:T], float(DK) ** -0.5, None, ALU.mult)
            v.tensor_tensor(keT[:, :, 0:L], keT[:, :, 0:L], kT[:, :, 0:L], ALU.mult)
            v.memset(att, 0.0)
            v.tensor_tensor(kdT[:, :, 0:L], kdT[:, :, 0:L], kT[:, :, 0:L], ALU.mult).then_inc(gla_in_ready, 1)
            dve.wait_ge(gla_in_ready, 1)

            def rows_from(kind, f, out):
                x = (kind, f)
                dve.wait_ge(misc_done, mcount(x))
                v.tensor_copy(out[:, 0:NB, f * P:(f + 1) * P],
                              mbank(x)[:, 0:NB * P].rearrange("p (b f) -> p b f", b=NB))
                v.tensor_copy(out[0:NS, NB, f * P:(f + 1) * P], mbank(x)[0:NS, NB * P:(NB + 1) * P])\
                    .then_inc(empty(x), 1)

            def att_step(b):
                x = ("att", b)
                dve.wait_ge(misc_done, mcount(x))
                for h in range(H):
                    ins = v.copy_predicated(att[:, b, h, :], attmask.bitcast(I32), mbank(x)[:, h * P:(h + 1) * P])
                ins.then_inc(empty(x), 1)
                dve.wait_ge(*freed(mby, misc_free, mpos[x]))
                dve.sem_inc(att_ready, 1)

            def state_of(c):
                return S_ver[:, c, :] if c < NCH - 1 else S_last

            def state_step(c, i):
                x = ("dS", c, i)
                dve.wait_ge(misc_done, mcount(x))
                if c == 0:
                    ins = v.tensor_copy(state_of(0)[:, 2 * i * DV:(2 * i + 2) * DV], mbank(x)[:, :])
                else:
                    for h in (2 * i, 2 * i + 1):
                        hs = slice(h * DV, (h + 1) * DV)
                        ins = v.scalar_tensor_tensor(state_of(c)[:, hs], state_of(c - 1)[:, hs], decay[:, h, c:c + 1],
                                                     mbank(x)[:, (h % 2) * DV:(h % 2 + 1) * DV], ALU.mult, ALU.add)
                ins.then_inc(empty(x), 1)
                dve.wait_ge(*freed(mby, misc_free, mpos[x]))
                dve.sem_inc(state_ready, 1)

            def sample_state(b, i):
                x = ("kv", b, i)
                dve.wait_ge(misc_done, mcount(x))
                if i == 0:
                    dve.wait_ge(st_loaded[b % 2], 16 * (b // 2 + 1))
                for h in (2 * i, 2 * i + 1):
                    s = st[:, b % 2, h * DV:(h + 1) * DV]
                    ins = v.scalar_tensor_tensor(s, s, sdecay[:, h, b:b + 1], mbank(x)[:, (h % 2) * DV:(h % 2 + 1) * DV],
                                                 ALU.mult, ALU.add)
                ins.then_inc(empty(x), 1)
                dve.wait_ge(*freed(mby, misc_free, mpos[x]))
                dve.sem_inc(st_ready, 1)

            def o_norm(part, sample):
                r = slice(NB * H, (NB + 1) * H) if sample else slice(0, NB * H)
                rows = NS if sample else P
                dve.wait_ge(o_squares, part)
                v.tensor_scalar(ors[0:rows, r], oss[0:rows, r], 1.0 / DV, EPS, ALU.mult, ALU.add).then_inc(o_sum, 1)
                dve.wait_ge(o_root, 1 + sample)
                link(v.reciprocal(ors[0:rows, r], ors[0:rows, r]))
                for b in ([NB] if sample else range(NB)):
                    for h in range(H):
                        hs = slice(h * DV, (h + 1) * DV)
                        ins = v.tensor_scalar(o_tok[0:rows, b, hs], o_tok[0:rows, b, hs],
                                              ors[0:rows, b * H + h:b * H + h + 1], None, ALU.mult)
                ins.then_inc(o_ready, 1)

            def v_norm():
                for b, rows, _ in BLOCKS:
                    for i in range(2):
                        ins = v.bn_stats(vstat[0:rows, 6 * i:6 * i + 6], vn[0:rows, b, i * 512:(i + 1) * 512])
                    link(ins)
                    link(v.bn_aggr(vmv[0:rows, 2 * b:2 * b + 2], vstat[0:rows, :]))
                    ins = v.tensor_scalar(vrs[0:rows, b:b + 1], vmv[0:rows, 2 * b + 1:2 * b + 2], EPS, None, ALU.add)
                ins.then_inc(vn_var, 1)
                dve.wait_ge(vn_root, 1)
                for b, rows, _ in BLOCKS:
                    ins = v.reciprocal(vrs[0:rows, b:b + 1], vrs[0:rows, b:b + 1])
                link(ins)
                for b, rows, _ in BLOCKS:
                    v.tensor_scalar(vn[0:rows, b, :], vn[0:rows, b, :], vmv[0:rows, 2 * b:2 * b + 1],
                                    vrs[0:rows, b:b + 1], ALU.subtract, ALU.mult).then_inc(vn_scaled, 1)

            def b_step(f):
                x = ("mix", f)
                dve.wait_ge(misc_done, mcount(x))
                dve.wait_ge(*freed(zby, z_free, zpos[("gb", f)]))
                if f > 0:
                    dve.wait_ge(b_done, f)
                ins = v.tensor_tensor(t[4], mbank(x)[:, 0:T], bspT[:, f * MH // KT, :], ALU.add)
                ins.then_inc(empty(x), 1)
                dve.wait_ge(*freed(mby, misc_free, mpos[x]))
                link(v.tensor_tensor(t[4], t[4], t[f % 2], ALU.mult))
                v.tensor_tensor(mixT[:, f, :], t[4], t[2 + f % 2], ALU.mult).then_inc(b_done, 1)

            def r_step(f):
                dve.wait_ge(r_sig, f + 1)
                v.tensor_tensor(t[f % 2], t[f % 2], zbank(("r", f))[:, 0:T], ALU.mult).then_inc(z_free["vector"], 1)

            def a_step(f):
                x = ("oT", f)
                dve.wait_ge(*freed(zby, z_free, zpos[("ga", f)]))
                dve.wait_ge(*freed(zby, z_free, zpos[("r", f)]))
                link(v.tensor_tensor(t[2 + f % 2], t[f % 2], t[2 + f % 2], ALU.mult))
                if f == 0:
                    dve.wait_ge(b_done, KT)
                else:
                    dve.wait_ge(a_done, f)
                dve.wait_ge(misc_done, mcount(x))
                ins = v.scalar_tensor_tensor(t[4], mbank(x)[:, 0:T], vec(36 + f % 2), t[2 + f % 2], ALU.mult, ALU.mult)
                ins.then_inc(empty(x), 1)
                dve.wait_ge(*freed(mby, misc_free, mpos[x]))
                v.tensor_tensor(mixT[:, f, :], mixT[:, f, :], t[4], ALU.add).then_inc(a_done, 1)

            for x in misc:
                if mby[mpos[x]] == "vector" or x in (("soT", 1),):
                    kind, *at = x if isinstance(x, tuple) else (x,)
                    if kind == "vT":
                        rows_from("vT", at[0], v_tok)
                    elif kind == "vgT":
                        rows_from("vgT", at[0], vn)
                        if at[0] == KT - 1:
                            dve.wait_ge(*freed(mby, misc_free, mpos[x]))
                            v_norm()
                            o_norm(NB * H, False)
                    elif kind == "att":
                        att_step(*at)
                    elif kind == "dS":
                        state_step(*at)
                    elif kind == "kv":
                        sample_state(*at)
                    elif kind == "mix":
                        if at[0] == 0:
                            dve.wait_ge(bsp_ready, 1)
                        b_step(*at)
                    elif kind == "soT":
                        o_norm(NB * H + 1, True)
                    elif kind == "oT":
                        if at[0] % 2 == 0:
                            r_step(at[0])
                            r_step(at[0] + 1)
                        a_step(*at)

            dve.wait_ge(vn_stored, 16)
            for f in range(KT):
                dve.wait_ge(z_done, zcount(("wo", f)))
                if f == 0:
                    dve.wait_ge(*freed(mby, misc_free, mpos[("xT", KT - 1)]))
                v.tensor_tensor(hTv[:, f, :], hTv[:, f, :], zbank(("wo", f))[:, 0:T], ALU.add).then_inc(h_ready, 1)
                dve.wait_ge(h_ready, f + 1)
                v.tensor_scalar(hgT[:, f, :], hTv[:, f, :], vec(KT + f), None, ALU.mult).then_inc(hg_ready, 1)
                dve.sem_inc(z_free["vector"], 1)
            dve.wait_ge(h_squares, 2 * (NB + 1))
            for b, rows, _ in BLOCKS:
                ins = v.tensor_tensor(hrs[0:rows, b:b + 1], hss[0:rows, 2 * b:2 * b + 1], hss[0:rows, 2 * b + 1:2 * b + 2],
                                      ALU.add)
            link(ins)
            for b, rows, _ in BLOCKS:
                ins = v.tensor_scalar(hrs[0:rows, b:b + 1], hrs[0:rows, b:b + 1], 1.0 / D, EPS, ALU.mult, ALU.add)
            ins.then_inc(h_sum, 1)
            v.memset(selm, 0.0)
            dve.wait_ge(h_root, 1)
            for b, rows, _ in BLOCKS:
                ins = v.reciprocal(hrs[0:rows, b:b + 1], hrs[0:rows, b:b + 1])
            link(ins)
            dve.wait_ge(router_done, 1)
            dve.wait_ge(ld_router, 48)
            for b, rows, _ in BLOCKS:
                ins = v.scalar_tensor_tensor(lg[0:rows, b, :], bank[0][0:rows, b * E:(b + 1) * E],
                                             hrs[0:rows, b:b + 1], brrow[0:rows, :], ALU.mult, ALU.add)
            link(ins)
            for b, rows, _ in BLOCKS:
                ins = v.max(m8[0:rows, b, :], lg[0:rows, b, :])
            link(ins)
            for b, rows, _ in BLOCKS:
                v.tensor_scalar(negm[0:rows, b:b + 1], m8[0:rows, b, 0:1], -1.0, None, ALU.mult).then_inc(top_ready, 1)
            for b, rows, _ in BLOCKS:
                ins = v.max_index(idx[0:rows, b, :].bitcast(U32), m8[0:rows, b, :], lg[0:rows, b, :])
            link(ins)
            for b, rows, _ in BLOCKS:
                ins = v.tensor_copy(idx_f[0:rows, b, :], idx[0:rows, b, 0:TOP_K].bitcast(U32))
            link(ins)
            dve.wait_ge(top_exp, NB + 1)
            for b, rows, _ in BLOCKS:
                ins = v.reciprocal(esum[0:rows, b:b + 1], esum[0:rows, b:b + 1])
            link(ins)
            for b, rows, _ in BLOCKS:
                ins = v.tensor_scalar(ew[0:rows, b, :], ew[0:rows, b, :], esum[0:rows, b:b + 1], None, ALU.mult)
            link(ins)
            for b, rows, _ in BLOCKS:
                r = slice(0, rows)
                link(v.tensor_tensor(hit[r], iota_e[r, :].unsqueeze(1).to_broadcast([rows, TOP_K, E]),
                                     idx_f[r, b, :].unsqueeze(2).to_broadcast([rows, TOP_K, E]), ALU.is_equal))
                link(v.tensor_reduce(selm[r, b, :], hit[r].rearrange("p k e -> p e k"), AX.X, ALU.add))
                link(v.tensor_tensor(hit[r], hit[r], ew[r, b, :].unsqueeze(2).to_broadcast([rows, TOP_K, E]), ALU.mult))
                ins = v.tensor_reduce(wtsv[r, b, 0:E], hit[r].rearrange("p k e -> p e k"), AX.X, ALU.add)
                link(ins)
            dve.sem_inc(sel_ready, 1)
            dve.wait_ge(rank_done, 1)
            v.tensor_copy(cnt, bank[1][:, (NB + 1) * E:(NB + 2) * E])
            placed = rankv[:, :, 0:E]
            link(v.scalar_tensor_tensor(placed, bank[1][:, 0:(NB + 1) * E].rearrange("p (b e) -> p b e", b=NB + 1),
                                        1.0, selm, ALU.add, ALU.mult))
            link(v.tensor_scalar(placed, placed, -1.0, None, ALU.add))

            def select(ps, item, col, w_col, offset=None):
                if offset is None:
                    at_rank = lambda b: rankv[:, b, col]
                else:
                    vlink(v.tensor_scalar(rk[:, :], rankv[:, :, col].rearrange("p b e -> p (b e)"), offset, None,
                                          ALU.subtract))
                    at_rank = lambda b: rk[:, b:b + 1]
                for b in range(NB + 1):
                    v.tensor_scalar(Ssel[:, b, :], iota_c[:, :], at_rank(b), None, ALU.is_equal)
                for b in range(NB + 1):
                    ins = v.tensor_scalar(Swt[:, b, :], iota_c[:, :], at_rank(b), wtsv[:, b, w_col],
                                          ALU.is_equal, ALU.mult)
                ins.then_inc(ps.selected, 1)

            def through(ps, item, chunks):
                return item * PER_EXPERT + (chunks + (ps is extra))

            def halves(banks):
                for i in range(2):
                    yield slice(i * HALF, (i + 1) * HALF), \
                        bank[banks[i]][:, 0:HALF * CAP].rearrange("p (f c) -> p f c", f=HALF)

            def bias_of(m, fs, col):
                return biasv[:, m, fs, col].to_broadcast([P, HALF, CAP])

            def gate_half(ps, item, col):
                dve.wait_ge(ps.used, through(ps, item, 4))
                for fs, p in halves((0, 1)):
                    ins = v.tensor_tensor(gs[:, fs, :], p, bias_of(0, fs, col), ALU.add)
                vlink(ins)
                v.tensor_scalar(gs, gs, LIMIT, None, ALU.min).then_inc(ps.g_ready, 1)

            def up_half(ps, item, col):
                dve.wait_ge(ps.used, through(ps, item, 8))
                for fs, p in halves((2, 3)):
                    ins = v.tensor_tensor(us[:, fs, :], p, bias_of(1, fs, col), ALU.add)
                vlink(ins)
                vlink(v.tensor_scalar(us, us, LIMIT, -LIMIT, ALU.min, ALU.max))
                vlink(v.scalar_tensor_tensor(us, us, 1.0, gs, ALU.add, ALU.mult))
                dve.wait_ge(ps.sig_ready, item + 1)
                v.tensor_tensor(gs, us, sg, ALU.mult).then_inc(ps.mid_ready, 1)

            def y_bias(ps, item, col):
                dve.wait_ge(ps.used, through(ps, item, 12))
                for fs, p in halves((4, 5)):
                    ins = v.tensor_tensor(yT[:, fs, :], p, bias_of(2, fs, col), ALU.add)
                ins.then_inc(ps.y_biased, 1)

            def add_y(ps, n):
                for f in range(KT):
                    dve.wait_ge(ps.scattered, n * KT + f + 1)
                    v.tensor_tensor(acc[:, f, :], acc[:, f, :], bank[4 + f % 2][:, 0:T], ALU.add)\
                        .then_inc(ps.added, 1)

            STEPS = 4
            vlink = chained(dve, main.vector_step)
            select(main, 0, bass.ds(0, 1), bass.ds(0, 1))
            for b, rows, _ in BLOCKS:
                for i in range(2):
                    c = slice(i * 512, (i + 1) * 512)
                    if b == 0 and i == 0:
                        dve.wait_ge(zeros_ready, 1)
                    ins = v.scalar_tensor_tensor(x2[0:rows, b, c], bank[2 + 2 * b + i][0:rows, :], hrs[0:rows, b:b + 1],
                                                 g2row[0:rows, c], ALU.mult, ALU.mult)
            ins.then_inc(x2_ready, 1)
            link(v.tensor_scalar(nov, cnt, float(CAP), None, ALU.is_gt))
            for n in range(2, LEVELS + 1):
                link(v.scalar_tensor_tensor(nov, cnt, float(n * CAP), nov, ALU.is_gt, ALU.add))
            link(v.tensor_tensor_scan(nov_end, ones[:, 0:E], nov, 0.0, ALU.mult, ALU.add))
            ends = nov_end.unsqueeze(1).to_broadcast([P, MAX_OV, E])
            link(v.tensor_tensor(ovt, ends, iota_c[:, 0:MAX_OV].unsqueeze(2).to_broadcast([P, MAX_OV, E]), ALU.is_le))
            link(v.tensor_reduce(ov_table[:, 0:MAX_OV], ovt, AX.X, ALU.add))
            link(v.tensor_tensor(ovt, ovt, nov.unsqueeze(1).to_broadcast([P, MAX_OV, E]), ALU.mult))
            link(v.tensor_reduce(ov_table[:, MAX_OV:2 * MAX_OV], ovt, AX.X, ALU.add))
            link(v.scalar_tensor_tensor(ov_table[:, MAX_OV:2 * MAX_OV], iota_c[:, 0:MAX_OV], 1.0,
                                        ov_table[:, MAX_OV:2 * MAX_OV], ALU.add, ALU.subtract))
            link(v.tensor_scalar(ov_table[:, MAX_OV:2 * MAX_OV], ov_table[:, MAX_OV:2 * MAX_OV], float(CAP), None,
                                 ALU.mult))
            link(v.tensor_copy(ov_table[:, 2 * MAX_OV:2 * MAX_OV + 1], nov_end[:, E - 1:E]))
            v.tensor_copy(ov_table_i[:, :], ov_table[:, :]).then_inc(table_ready, 1)
            dve.sem_inc(main.y_biased, 1)

            with dve.Fori(0, ROUNDS) as i:
                for u in range(UNROLL):
                    j = i * UNROLL + u
                    vlink = chained(dve, main.vector_step, base=j * STEPS)
                    gate_half(main, j, bass.ds(j, 1))
                    select(main, j + 1, bass.ds(j + 1, 1), bass.ds(j + 1, 1))
                    add_y(main, j)
                    up_half(main, j, bass.ds(j, 1))
                    y_bias(main, j, bass.ds(j, 1))
                    assert vlink.count[0] == STEPS
            add_y(main, E)

            n_extra = dve.value_load(ov_table_i[0:1, 2 * MAX_OV:2 * MAX_OV + 1], min_val=0, max_val=MAX_OV)
            with dve.If(n_extra > 0):
                with dve.Fori(0, n_extra) as i:
                    e = dve.value_load(ov_table_i[0:1, bass.ds(i, 1)], min_val=0, max_val=E - 1)
                    vlink = chained(dve, extra.vector_step, base=i * (STEPS + 1))
                    select(extra, i, bass.ds(e, 1), bass.ds(e, 1), ov_table[:, bass.ds(i + MAX_OV, 1)])
                    gate_half(extra, i, bass.ds(e, 1))
                    up_half(extra, i, bass.ds(e, 1))
                    y_bias(extra, i, bass.ds(e, 1))
                    assert vlink.count[0] == STEPS + 1
                    add_y(extra, i)
                    dve.wait_ge(extra.added, i * KT + KT)

            link = chained(dve, tail_step)
            dve.wait_ge(main.added, (E + 1) * KT)
            for f in range(KT):
                ins = v.tensor_tensor(hTv[:, f, :], hTv[:, f, :], acc[:, f, :], ALU.add)
            link(ins)
            for f in range(KT):
                v.tensor_scalar(n3T[:, f, :], hTv[:, f, :], vec(2 * KT + f), None, ALU.mult).then_inc(h2_ready, 1)
            dve.wait_ge(rms_done, 1)
            v.tensor_scalar(rb, bank[4][:, 0:T], 1.0 / D, EPS, ALU.mult, ALU.add).then_inc(rms_sum, 1)
            dve.wait_ge(rms_root, 1)
            link(v.reciprocal(rb, rb))

            def third(f):
                g = gt[f % 3]
                dve.wait_ge(gate_act, f + 1)
                dve.wait_ge(pw_ready, KT)
                link(v.tensor_tensor(g, g, pwT[:, f, :], ALU.mult))
                v.tensor_tensor(hTv[:, f, :], hTv[:, f, :], g, ALU.add).then_inc(h3_sum, 1)
                dve.wait_ge(h3_sum, f + 1)
                v.tensor_scalar(y3T[:, f, :], hTv[:, f, :], vec(3 * KT + f), None, ALU.mult).then_inc(h3_ready, 1)

            for f in range(KT):
                dve.wait_ge(gate_done, f + 1)
                v.tensor_tensor(gt[f % 3], bank[f % 4][:, 0:T], rb, ALU.mult).then_inc(gate_pre, 1)
                if f > 0:
                    third(f - 1)
            third(KT - 1)
            dve.wait_ge(y_stat, 1)
            for b, rows, _ in BLOCKS:
                ins = v.tensor_scalar(yss[0:rows, b:b + 1], bank[5][0:rows, b:b + 1], 1.0 / D, EPS, ALU.mult, ALU.add)
            ins.then_inc(y_sum, 1)
            dve.wait_ge(y_root, 1)
            for b, rows, _ in BLOCKS:
                ins = v.reciprocal(yss[0:rows, b:b + 1], yss[0:rows, b:b + 1])
            ins.then_inc(y_scale, 1)
            dve.wait_ge(y_scale, 1)
            for b, rows, _ in BLOCKS:
                dve.wait_ge(yrow_done, 2 * b + 1)
                v.tensor_scalar(x2[0:rows, b, 0:512], bank[2 * b % 4][0:rows, :], yss[0:rows, b:b + 1], None, ALU.mult)\
                    .then_inc(yrow_ready["vector"], 1)

        @block.scalar
        def _(act):
            a = nc.scalar.activation
            link = chained(act, act_step)

            for i, (x, n) in enumerate(((norm1_g[0], KT), (norm2_g[0], KT), (norm3_g[0], KT), (final_g, KT),
                                        (b_gk[0], H), (gla_norm_g[0], DV // P))):
                if i == 0:
                    act.wait_ge(pool_step, 1)
                r0 = [0, KT, 2 * KT, 3 * KT, 4 * KT, 4 * KT + H][i]
                act.dma_start(vrows[r0:r0 + n, :], x.rearrange("(k p) -> k p", p=P)).then_inc(ld_vec, 16)
            act.dma_start(wgk, w_in[0][:, CGK:CGK + RANK].rearrange("(k p) n -> p k n", p=P)).then_inc(ld_gk, 16)
            act.dma_start(wgk2[0:RANK, :], w_gk2[0]).then_inc(ld_gk, 16)
            act.dma_start(w00[:, :], w_sp[0, :, 0, 0].unsqueeze(0).to_broadcast([NS, MH]),
                          allow_slow_non_contiguous=True).then_inc(ld_wsp, 16)
            act.dma_start(wsp, w_sp[0].rearrange("h t s -> t h s")).then_inc(ld_wsp, 16)
            for b, rows, t0 in BLOCKS:
                src = p_prompt[0, 0, t0:t0 + rows, :] if b < NB else p_sample[0, :, 0, :]
                act.dma_start(p_tok[0:rows, b, :], src).then_inc(ld_p, 16)
            for m, x in enumerate((b_gate, b_up, b_down)):
                act.dma_start(bias_rows[0:E, m, :], x[0]).then_inc(ld_bias, 16)
            act.dma_start(vngrow, v_norm_g.to_broadcast([P, D])).then_inc(ld_rows, 16)
            act.dma_start(vnbrow, v_norm_b.to_broadcast([P, D])).then_inc(ld_rows, 16)
            act.dma_start(bspT[:, :, 0:P], b_sp.to_broadcast([P, MH, P])).then_inc(ld_rows, 16)
            act.dma_start(g2row[:, :], norm2_g.to_broadcast([P, D])).then_inc(ld_router, 16)
            act.dma_start(brrow[:, :], b_router.to_broadcast([P, E])).then_inc(ld_router, 16)
            act.dma_start(wrtv, w_router[0].rearrange("(k p) n -> p k n", p=P)).then_inc(ld_router, 16)

            act.wait_ge(ld_x, 16 * len(BLOCKS))
            for b, rows, _ in BLOCKS:
                if b > 0:
                    act.wait_ge(x_squares, b)
                a(junk[0:rows, :], x_tok[0:rows, b, :], ACT.Square, accum_out=xss[0:rows, b:b + 1])\
                    .then_inc(x_squares, 1)
            act.wait_ge(x_scale_sum, 1)
            for b, rows, _ in BLOCKS:
                ins = a(xrs[0:rows, b:b + 1], xrs[0:rows, b:b + 1], ACT.Sqrt)
            ins.then_inc(x_root, 1)

            def z_out(kind, f):
                tile = (kind, f)
                p, free = zbank(tile)[:, 0:T], z_free["scalar"]
                act.wait_ge(z_done, zcount(tile))
                if kind in ("k", "q"):
                    a((kT if kind == "k" else qT)[:, f, :], p, ACT.Copy).then_inc(free, 1)
                elif kind == "v":
                    if f >= 2:
                        act.wait_ge(misc_done, mcount(("vT", f - 2)))
                    a(t[f % 2], p, ACT.Copy).then_inc(free, 1)
                elif kind == "vg":
                    if f >= 2:
                        act.wait_ge(misc_done, mcount(("vgT", f - 2)))
                    a(t[2 + f % 2], p, ACT.Gelu).then_inc(free, 1)
                elif kind in ("u", "gb"):
                    if f >= 2:
                        act.wait_ge(b_done, f - 1)
                    else:
                        act.wait_ge(misc_done, mcount(("vT" if kind == "u" else "vgT", KT - 1)))
                    if kind == "u":
                        a(t[f % 2], p, ACT.Gelu).then_inc(free, 1)
                    else:
                        a(t[2 + f % 2], p, ACT.Sigmoid).then_inc(free, 1)
                elif kind in ("r", "ga"):
                    if f >= 2:
                        act.wait_ge(a_done, f - 1)
                    else:
                        act.wait_ge(b_done, KT - 1 + f)
                    if kind == "r":
                        a(t[f % 2], p, ACT.Sigmoid).then_inc(r_sig, 1)
                    else:
                        a(t[2 + f % 2], p, ACT.Sigmoid).then_inc(free, 1)

            def mask_keys(b):
                a(kmask[0:NS, b % 2, :], kd_tok[0:NS, NB, :], ACT.Copy, scale=ident[0:NS, b:b + 1])\
                    .then_inc(kmask_ready, 1)

            def misc_out(x):
                kind, *at = x if isinstance(x, tuple) else (x,)
                p, free = mbank(x), misc_free["scalar"]
                act.wait_ge(misc_done, mcount(x))
                f = at[0] if at else None
                if kind == "gk":
                    a(gkT[0:RANK, :], p[0:RANK, 0:T], ACT.Copy).then_inc(free, 1)
                elif kind == "xT":
                    a(hTv[:, f, :], p[:, 0:T], ACT.Copy).then_inc(free, 1)
                elif kind == "pT":
                    a(pTv[:, f, :], p[:, 0:T], ACT.Copy).then_inc(free, 1)
                elif kind == "kdT":
                    rows = BLOCKS[f][1]
                    a(kd_tok[0:rows, f, :], p[0:rows, :], ACT.Copy).then_inc(free, 1)
                    if f == NB:
                        act.wait_ge(*freed(mby, misc_free, mpos[x]))
                        mask_keys(0)
                        mask_keys(1)
                elif kind == "o":
                    b, i = at
                    a(o_tok[:, b, i * 512:(i + 1) * 512], p[:, :], ACT.Copy).then_inc(free, 1)
                    act.wait_ge(*freed(mby, misc_free, mpos[x]))
                    for h in (2 * i, 2 * i + 1):
                        a(ojunk[h % 2], o_tok[:, b, h * DV:(h + 1) * DV], ACT.Square,
                          accum_out=oss[:, b * H + h:b * H + h + 1]).then_inc(o_squares, 1)
                    act.wait_ge(o_squares, 2 * (2 * b + i + 1))
                elif kind == "so":
                    a(oST[:, :, f], p[:, 0:2 * H], ACT.Copy).then_inc(free, 1)
                    if f + 2 < NS:
                        mask_keys(f + 2)
                elif kind == "soT":
                    a(o_tok[0:NS, NB, f * 512:(f + 1) * 512], p[0:NS, :], ACT.Copy).then_inc(free, 1)
                    if f == 1:
                        act.wait_ge(*freed(mby, misc_free, mpos[x]))
                        for h in range(H):
                            ins = a(hjunk[h][0:NS, 0:DV], o_tok[0:NS, NB, h * DV:(h + 1) * DV], ACT.Square,
                                    accum_out=oss[0:NS, NB * H + h:NB * H + h + 1])
                        ins.then_inc(o_squares, 1)
                        act.wait_ge(o_sum, 2)
                        a(ors[0:NS, NB * H:], ors[0:NS, NB * H:], ACT.Sqrt).then_inc(o_root, 1)

            for x in plan:
                if x[0] == "z":
                    if zby[zpos[x[1:]]] == "scalar" or x[1] == "r":
                        z_out(*x[1:])
                elif mby[mpos[x]] == "scalar":
                    misc_out(x)
                if x == ("z", "q", 0):
                    act.wait_ge(abs_ready, 1)
                    link(a(e1, e1, ACT.Exp, scale=-1.0))
                    a(e1, e1, ACT.Ln, bias=1.0).then_inc(la_ready, 1)
                if x == ("z", "v", 0):
                    act.wait_ge(cum_ready, 1)
                    a(e1, bT, ACT.Exp, scale=1.0 / GATE_NORMALIZER).then_inc(decays_ready, 1)
                    a(keT[:, :, 0:L], bT[:, :, 0:L], ACT.Exp, scale=-1.0 / GATE_NORMALIZER).then_inc(decays_ready, 1)
                    act.wait_ge(back_ready, 1)
                    a(kdT[:, :, 0:L], kdT[:, :, 0:L], ACT.Exp, scale=1.0 / GATE_NORMALIZER).then_inc(decays_ready, 1)
                if x == ("z", "u", 0):
                    act.wait_ge(vn_var, 1)
                    for b, rows, _ in BLOCKS:
                        ins = a(vrs[0:rows, b:b + 1], vrs[0:rows, b:b + 1], ACT.Sqrt)
                    ins.then_inc(vn_root, 1)
                    act.wait_ge(o_sum, 1)
                    a(ors[:, 0:NB * H], ors[:, 0:NB * H], ACT.Sqrt).then_inc(o_root, 1)

            for b, rows, _ in BLOCKS:
                for i in range(2):
                    act.wait_ge(hrow_done, 2 * b + i + 1)
                    if b == 2:
                        act.wait_ge(h_squares, 4)
                    a(hjunk[(2 * b + i) % 4][0:rows, :], bank[2 + 2 * b + i][0:rows, :], ACT.Square,
                      accum_out=hss[0:rows, 2 * b + i:2 * b + i + 1]).then_inc(h_squares, 1)
            act.wait_ge(h_sum, 1)
            for b, rows, _ in BLOCKS:
                ins = a(hrs[0:rows, b:b + 1], hrs[0:rows, b:b + 1], ACT.Sqrt)
            ins.then_inc(h_root, 1)
            for b, rows, _ in BLOCKS:
                act.wait_ge(top_ready, b + 1)
                a(ew[0:rows, b, :], m8[0:rows, b, 0:TOP_K], ACT.Exp, bias=negm[0:rows, b:b + 1],
                  accum_out=esum[0:rows, b:b + 1]).then_inc(top_exp, 1)

            def gathered_out(ps, item, parity):
                act.wait_ge(ps.gathered, item + 1)
                for i in range(2):
                    a(xe[:, i * HALF:(i + 1) * HALF, :],
                      bank[6 + i][:, 0:HALF * CAP].rearrange("p (f c) -> p f c", f=HALF), ACT.Copy)
                for b, rows, t0 in BLOCKS:
                    o0 = HALF * CAP + (P if b == NB else 0)
                    ins = a(SWT[parity][0:CAP, t0:t0 + rows], bank[6 + b % 2][0:CAP, o0:o0 + rows], ACT.Copy)
                ins.then_inc(ps.xe_ready, 1)

            def turned_out(ps, n):
                act.wait_ge(ps.turned, n + 1)
                for i in range(2):
                    ins = a(ye[0:CAP, i * 512:(i + 1) * 512], bank[6 + i][0:CAP, :], ACT.Copy)
                ins.then_inc(ps.ye_ready, 1)

            def sigmoid(ps, item):
                act.wait_ge(ps.g_ready, item + 1)
                a(sg, gs, ACT.Sigmoid, scale=ALPHA).then_inc(ps.sig_ready, 1)

            gathered_out(main, 0, 0)
            with act.Fori(0, ROUNDS) as i:
                for u in range(UNROLL):
                    j = i * UNROLL + u
                    turned_out(main, j)
                    sigmoid(main, j)
                    gathered_out(main, j + 1, (u + 1) % 2)
            turned_out(main, E)

            act.wait_ge(table_ready, 1)
            n_extra = act.value_load(ov_table_i[0:1, 2 * MAX_OV:2 * MAX_OV + 1], min_val=0, max_val=MAX_OV)
            with act.If(n_extra > 0):
                with act.Fori(0, n_extra) as i:
                    gathered_out(extra, i, 0)
                    sigmoid(extra, i)
                    turned_out(extra, i)

            for f in range(KT):
                act.wait_ge(pw_done, f + 1)
                a(pwT[:, f, :], bank[f % 4][:, 0:T], ACT.Copy).then_inc(pw_ready, 1)
            for f in range(KT):
                act.wait_ge(h2_ready, f + 1)
                a(sqT[:, f, :], hTv[:, f, :], ACT.Square).then_inc(sq_ready, 1)
            act.wait_ge(rms_sum, 1)
            a(rb, rb, ACT.Sqrt).then_inc(rms_root, 1)

            def gate_sigmoid(f):
                act.wait_ge(gate_pre, f + 1)
                a(gt[f % 3], gt[f % 3], ACT.Sigmoid).then_inc(gate_act, 1)

            for f in range(KT):
                gate_sigmoid(f)
                if f > 0:
                    act.wait_ge(h3_sum, f)
                    a(sqT[:, f - 1, :], hTv[:, f - 1, :], ACT.Square).then_inc(ysq_ready, 1)
            act.wait_ge(h3_sum, KT)
            a(sqT[:, KT - 1, :], hTv[:, KT - 1, :], ACT.Square).then_inc(ysq_ready, 1)
            act.wait_ge(y_sum, 1)
            for b, rows, _ in BLOCKS:
                ins = a(yss[0:rows, b:b + 1], yss[0:rows, b:b + 1], ACT.Sqrt)
            ins.then_inc(y_root, 1)
            act.wait_ge(y_scale, 1)
            for b, rows, _ in BLOCKS:
                act.wait_ge(yrow_done, 2 * b + 2)
                a(x2[0:rows, b, 512:1024], bank[(2 * b + 1) % 4][0:rows, :], ACT.Copy, scale=yss[0:rows, b:b + 1])\
                    .then_inc(yrow_ready["scalar"], 1)


_INS = ["x_prompt", "x_sample", "state_gla", "p_prompt", "p_sample", "norm1_g", "w_in", "w_gk2", "b_gk", "gla_norm_g",
        "v_norm_g", "v_norm_b", "w_sp", "b_sp", "w_o", "norm2_g", "w_router", "b_router", "w_gate", "b_gate", "w_up",
        "b_up", "w_down", "b_down", "norm3_g", "w_ple_gate", "w_ple_proj", "final_g"]
_OUTS = [(1, 256, 1024), (8, 1, 1024), (1, 1, 4, 128, 256), (1, 8, 4, 128, 256), (1, 8, 1, 1024)]


def kernel(**inputs):
    import numpy as _np
    import concourse.bacc as _bacc
    from concourse import mybir as _mybir
    from concourse.bass_utils import run_bass_kernel_spmd as _run

    nc = _bacc.Bacc("TRN2", target_bir_lowering=False, num_devices=1)
    arrays, args = {}, []
    for name in _INS:
        a = _np.ascontiguousarray(inputs[name])
        arrays[f"in_{name}_dram"] = a
        args.append(nc.dram_tensor(f"in_{name}_dram", a.shape, _mybir.dt.from_np(a.dtype), kind="ExternalInput").ap())
    for i, shape in enumerate(_OUTS):
        args.append(nc.dram_tensor(f"out_{i}_dram", shape, _mybir.dt.float32, kind="ExternalOutput").ap())
    hybrid_step(nc, *args)
    r = _run(nc, [arrays], core_ids=[0])
    return tuple(r.results[0][f"out_{i}_dram"] for i in range(len(_OUTS)))
```

```python
from contextlib import ExitStack

import numpy as np

import concourse.bass as bass
from concourse import mybir

F32 = mybir.dt.float32
I32 = mybir.dt.int32
U32 = mybir.dt.uint32
ALU = mybir.AluOpType
ACT = mybir.ActivationFunctionType
AX = mybir.AxisListType

P = 128
EPS = 1e-6
GLA_CHUNK = 64
TOP_K = 4
LIMIT, ALPHA = 7.0, 1.702
CAP = P // 2
GATE_NORMALIZER = 16.0

SLOT = 2048
SLOTS = 16
FRONT_SLOTS = 6
LATE_SLOTS = 2
PER_EXPERT = 12
UNROLL = 4
EXTRA_SLOT = 4


def hybrid_step(nc, x_prompt, x_sample, state_gla, p_prompt, p_sample, norm1_g, w_in, w_gk2, b_gk, gla_norm_g,
                v_norm_g, v_norm_b, w_sp, b_sp, w_o, norm2_g, w_router, b_router, w_gate, b_gate, w_up, b_up,
                w_down, b_down, norm3_g, w_ple_gate, w_ple_proj, final_g,
                y_prompt, y_sample, st_prompt, st_sample, mix_v_sample):
    L, D = x_prompt.shape[1:]
    NS = x_sample.shape[0]
    T = L + NS
    NB = L // P
    KT = D // P
    H, DK, DV = state_gla.shape[2:]
    RANK = w_gk2.shape[1]
    E = w_gate.shape[1]
    MH = w_sp.shape[1]
    DP = p_prompt.shape[3]
    PK = DP // P
    NCH = L // GLA_CHUNK
    HALF = KT // 2
    MAX_OV = T * TOP_K // CAP + 1
    LEVELS = (T - 1) // CAP
    ROUNDS = E // UNROLL
    BLOCKS = [(b, P, b * P) for b in range(NB)] + [(NB, NS, L)]

    CQ, CK, CV, CR = 0, H * DK, 2 * H * DK, 2 * H * DK + H * DV
    CGK = CR + H * DV
    CU, CVG, CGA, CGB = CGK + RANK, CGK + RANK + D, CGK + RANK + 2 * D, CGK + RANK + 3 * D

    def in_turn(a, b):
        return [(k, f) for c in range(0, KT, 2) for k in (a, b) for f in (c, c + 1)]

    ztiles = [("k", f) for f in range(H)] + [("q", f) for f in range(H)] + [("v", f) for f in range(KT)] + \
        [("vg", f) for f in range(KT)] + in_turn("u", "gb") + in_turn("r", "ga") + [("wo", f) for f in range(KT)]
    zcol = {"k": CK, "q": CQ, "v": CV, "vg": CVG, "u": CU, "gb": CGB, "r": CR, "ga": CGA, "wo": 0}
    zpos = {tile: n for n, tile in enumerate(ztiles)}
    NFRONT = len(ztiles) // 2
    ZBANKS = 4
    zby = ["vector" if kind in ("r", "wo") else "scalar" for kind, _ in ztiles]

    def z(kind, *fs):
        return [("z", kind, f) for f in fs]

    plan = ["vec"] + [("nT", f) for f in range(KT)] + ["gk"] + z("k", *range(H)) + [("la", h) for h in range(H)] + \
        z("q", *range(H)) + [("xT", f) for f in range(KT)] + [("bias", 0), ("bias", 1)] + \
        [("pT", k) for k in range(PK)] + ["wsp"] + z("v", 0)
    for f in range(1, KT):
        plan += z("v", f) + [("vT", f - 1)]
    between = [[("kdT", 0), ("kdT", 1), ("kdT", 2)], [("att", 0), ("att", 1)]] + \
        [[("dS", c, 0), ("dS", c, 1)] for c in range(NCH)] + [[("o", b, 0), ("o", b, 1)] for b in range(NB)]
    for f in range(KT):
        plan += z("vg", f) + [("vT", KT - 1) if f == 0 else ("vgT", f - 1)] + between[f]
    for c in range(0, KT, 2):
        plan += z("u", c) + ([("vgT", KT - 1)] if c == 0 else []) + [("kv", c, 0), ("kv", c, 1)] + z("u", c + 1) + \
            [("kv", c + 1, 0), ("kv", c + 1, 1), ("so", c)] + z("gb", c) + [("so", c + 1)] + z("gb", c + 1) + \
            [("mix", c), ("mix", c + 1)]
    plan += [("soT", 0), ("soT", 1)]
    for c in range(0, KT, 2):
        plan += z("r", c, c + 1) + z("ga", c, c + 1) + [("oT", c), ("oT", c + 1)]
    plan += z("wo", *range(KT))
    assert [x[1:] for x in plan if x[0] == "z"] == ztiles

    misc = [x for x in plan if x[0] != "z"]
    mpos = {x: n for n, x in enumerate(misc)}
    mby = ["scalar" if x[0] in ("gk", "xT", "pT", "kdT", "o", "so", "soT") or x == "gk" else "vector" for x in misc]

    ctx = ExitStack()
    with ctx:
        def sb(name, shape, dt=F32):
            return ctx.enter_context(nc.sbuf_tensor(name, shape, dt))

        def sem(name):
            return ctx.enter_context(nc.semaphore(name))

        bank = [ctx.enter_context(nc.psum_tensor(f"bank{i}", [P, 512], F32)) for i in range(8)]

        def view(tensor, at, *shape):
            n = int(np.prod(shape))
            v = tensor[:, at:at + n]
            if len(shape) == 1:
                return v
            names = "abcd"[:len(shape)]
            return v.rearrange("p (%s) -> p %s" % (" ".join(names), " ".join(names)),
                               **dict(zip(names[1:], shape[1:])))

        ring = sb("ring", [P, SLOTS * SLOT])
        hT = sb("hT", [P, KT * T])
        ident = sb("ident", [P, P])
        ones = sb("ones", [P, P])
        two_eyes = sb("two_eyes", [P, CAP])
        before = sb("before", [P, P])
        upto = sb("upto", [P, P])
        vecT = sb("vecT", [P, 40])
        biasT = sb("biasT", [P, 2 * KT * E])
        iota_c = sb("iota_c", [P, P])
        iota_e = sb("iota_e", [P, E])
        rank = sb("rank", [P, (NB + 1) * (E + 2)])
        wts = sb("wts", [P, (NB + 1) * (E + 2)])
        small = sb("small", [P, 128])
        ov_table = sb("ov_table", [P, 2 * MAX_OV + 1])
        ov_table_i = sb("ov_table_i", [P, 2 * MAX_OV + 1], I32)
        wrt = sb("wrt", [P, KT * E])
        brrow = sb("brrow", [P, E])
        pT = sb("pT", [P, PK * T])
        g2row = sb("g2row", [P, D])
        regA = sb("regA", [P, KT * T])
        regB = sb("regB", [P, (NB + 1) * D])
        regC = sb("regC", [P, (NB + 1) * D])
        regD = sb("regD", [P, KT * T])
        regE = sb("regE", [P, max(2 * D + H * T, (KT + 2) * T + MAX_OV * E)])
        w00 = sb("w00", [NS, MH])
        dw = sb("dw", [NS, MH * NS])
        rk = sb("rk", [P, NB + 1])

        hTv = view(hT, 0, KT, T)
        slot = [view(ring, s * SLOT, SLOT) for s in range(SLOTS)]
        by_k = [s.rearrange("p (k f) -> p k f", k=2) for s in slot]
        by_col = [s.rearrange("p (k f) -> p k f", k=KT) for s in slot]
        biasv = view(biasT, 0, 2, KT, E)
        rankv, wtsv = view(rank, 0, NB + 1, E + 2), view(wts, 0, NB + 1, E + 2)
        wrtv, pTv = view(wrt, 0, KT, E), view(pT, 0, PK, T)

        place = [FRONT_SLOTS * SLOT, (SLOTS - LATE_SLOTS) * SLOT]

        def front_buffer(*shape, late=False):
            at = place[late]
            place[late] += int(np.prod(shape))
            assert place[late] <= (SLOTS - LATE_SLOTS + late * LATE_SLOTS) * SLOT
            return view(ring, at, *shape)

        x_tok = front_buffer(NB + 1, D)
        S_ver = view(ring, FRONT_SLOTS * SLOT, NCH - 1, H * DV)
        S_last = front_buffer(H * DV)
        at_b = place[0]
        bT = front_buffer(H, T)
        att = view(ring, at_b, NB, H, P)
        e1 = front_buffer(H, T)
        qT = front_buffer(H, T)
        kT = front_buffer(H, T)
        at_junk = place[0]
        keT = front_buffer(H, T)
        kdT = front_buffer(H, T)
        v_tok = front_buffer(NB + 1, D)
        kd_tok = front_buffer(NB + 1, H * DK)
        kmask = front_buffer(2, H * DK)
        t = [front_buffer(T, late=True) for _ in range(5)]
        WT = front_buffer(MH, P, late=True)
        st = front_buffer(2, H * DV, late=True)
        attmask = front_buffer(P, late=True)
        scanmask = t[4]

        nT = view(regA, 0, KT, T)
        bias_rows = view(regB, 0, 2, D)
        o_tok, x2 = view(regB, 0, NB + 1, D), view(regB, 0, NB + 1, D)
        xn, vn, hgT = view(regC, 0, NB + 1, D), view(regC, 0, NB + 1, D), view(regC, 0, KT, T)
        mixT = view(regD, 0, KT, T)
        wgk, wgk2, gkT = view(regD, 0, KT, RANK), view(regD, P, H * DK), view(regD, P + H * DK, T)
        vrows, wsp = view(regD, 1024, P), view(regD, 1024 + P, MH, P)
        p_tok = view(sb("p_tok", [P, (NB + 1) * DP]), 0, NB + 1, DP)
        vngrow, vnbrow, bspT = view(regE, 0, D), view(regE, D, D), view(regE, 2 * D, H, T)
        junk = view(ring, at_junk, D)

        EC = KT * CAP
        gs, us, sg = (view(regC, i * EC, KT, CAP) for i in range(3))
        xe = view(regC, 3 * EC, KT, P)
        Ssel, Swt = view(regC, 3 * EC + KT * P, NB + 1, P), view(regA, 0, NB + 1, P)
        y_rows, rows_sb = view(regD, 0, D), view(regD, D, D)
        pwT = view(regE, 0, KT, T)
        SWT = [view(regE, KT * T + i * T, T) for i in range(2)]
        cols = [0]

        def small_tile(n):
            cols[0] += n
            assert cols[0] <= 128
            return small[:, cols[0] - n:cols[0]]

        xss, xrs = small_tile(NB + 1), small_tile(NB + 1)
        decay, sdecay = small_tile(H * NCH).rearrange("p (h c) -> p h c", h=H), \
            sb("sdecay", [P, H * NS])[:].rearrange("p (h s) -> p h s", h=H)
        oss, ors = small_tile((NB + 1) * H), small_tile((NB + 1) * H)
        vstat, vmv, vrs = small_tile(12), small_tile(2 * (NB + 1)), small_tile(NB + 1)
        hss, hrs = small_tile(2 * (NB + 1)), small_tile(NB + 1)
        yss = small_tile(NB + 1)
        oST = sb("oST", [P, 2 * H * NS])[:].rearrange("p (j s) -> p j s", s=NS)

        rt = [KT * T]

        def route_tile(*shape):
            rt[0] += int(np.prod(shape))
            assert rt[0] <= (NB + 1) * D
            return view(regC, rt[0] - int(np.prod(shape)), *shape)

        lg = route_tile(NB + 1, E)
        m8, ew = route_tile(NB + 1, 8), route_tile(NB + 1, TOP_K)
        idx = route_tile(NB + 1, 8)
        idx_f = route_tile(NB + 1, TOP_K)
        esum = route_tile(NB + 1)
        negm = route_tile(NB + 1)
        hit = route_tile(NB + 1, TOP_K, E)
        selm = route_tile(NB + 1, E)
        cnt, nov, nov_end = sb("cnt", [P, E])[:], sb("nov", [P, E])[:], sb("nov_end", [P, E])[:]
        ovt = view(regE, (KT + 2) * T, MAX_OV, E)

        sqT, n3T, y3T = view(regC, 0, KT, T), view(regD, 0, KT, T), view(regA, 0, KT, T)
        gt = [view(regC, (KT + i) * T, T) for i in range(3)]
        rb = view(regE, KT * T, T)

        ld_x = [sem(f"ld_x{b}") for b in range(NB + 1)]
        ld_vec, ld_gk, ld_bias, ld_p = sem("ld_vec"), sem("ld_gk"), sem("ld_bias"), sem("ld_p")
        ld_wsp, ld_rows, ld_router = sem("ld_wsp"), sem("ld_rows"), sem("ld_router")
        slot_loaded = [sem(f"slot_loaded{s}") for s in range(SLOTS)]
        st_loaded = [sem(f"st_loaded{s}") for s in range(2)]
        st_stored = [sem(f"st_stored{s}") for s in range(2)]
        sp_stored, vn_stored, y_stored = sem("sp_stored"), sem("vn_stored"), sem("y_stored")
        consts_ready = sem("consts_ready")
        pool_step, dve_step, act_step = sem("pool_step"), sem("dve_step"), sem("act_step")
        z_done, misc_done, chunk_used = sem("z_done"), sem("misc_done"), sem("chunk_used")
        z_free = {"scalar": sem("z_free_scalar"), "vector": sem("z_free_vector")}
        misc_free = {"scalar": sem("misc_free_scalar"), "vector": sem("misc_free_vector")}
        x_squares, x_scale_sum, x_root = sem("x_squares"), sem("x_scale_sum"), sem("x_root")
        xn_ready = sem("xn_ready")
        abs_ready, exp_ready, la_ready, cum_ready, back_ready = (
            sem(n) for n in ("abs_ready", "exp_ready", "la_ready", "cum_ready", "back_ready"))
        decays_ready, gla_in_ready = sem("decays_ready"), sem("gla_in_ready")
        att_ready, state_ready = sem("att_ready"), sem("state_ready")
        o_squares, o_sum, o_root, o_ready = sem("o_squares"), sem("o_sum"), sem("o_root"), sem("o_ready")
        vn_var, vn_root, vn_scaled, vn_ready = sem("vn_var"), sem("vn_root"), sem("vn_scaled"), sem("vn_ready")
        dw_ready, bsp_ready = sem("dw_ready"), sem("bsp_ready")
        kmask_ready, st_ready = sem("kmask_ready"), sem("st_ready")
        b_done, a_done = sem("b_done"), sem("a_done")
        r_sig = sem("r_sig")
        h_ready, hg_ready, hrow_done, router_done = sem("h_ready"), sem("hg_ready"), sem("hrow_done"), sem("router_done")
        h_squares, h_sum, h_root, hrs_ready = sem("h_squares"), sem("h_sum"), sem("h_root"), sem("hrs_ready")
        top_ready, top_exp, sel_ready, rank_done = sem("top_ready"), sem("top_exp"), sem("sel_ready"), sem("rank_done")
        zeros_ready, x2_ready, table_ready = sem("zeros_ready"), sem("x2_ready"), sem("table_ready")
        pw_done, pw_ready = sem("pw_done"), sem("pw_ready")
        ld_bdown, wT_done, wts_ready, x2_scaled = sem("ld_bdown"), sem("wT_done"), sem("wts_ready"), sem("x2_scaled")
        h2_ready, sq_ready, rms_done, rms_sum, rms_root = (
            sem(n) for n in ("h2_ready", "sq_ready", "rms_done", "rms_sum", "rms_root"))
        gate_done, gate_free, gate_pre, gate_act, h3_ready = (
            sem(n) for n in ("gate_done", "gate_free", "gate_pre", "gate_act", "h3_ready"))
        ysq_ready, y_stat, y_sum, y_root, yrow_done = (
            sem(n) for n in ("ysq_ready", "y_stat", "y_sum", "y_root", "yrow_done"))
        yrow_ready = {"vector": sem("yrow_ready_vector"), "scalar": sem("yrow_ready_scalar")}
        h3_sum, y_scale = sem("h3_sum"), sem("y_scale")
        ojunk, hjunk = [kT[:, h, 0:DV] for h in range(H)], [rows_sb[:, i * 512:(i + 1) * 512] for i in range(2)]
        tail_step = sem("tail_step")

        class Pass:
            def __init__(self, kind):
                self.selected = sem(f"{kind}_selected")
                self.gathered = sem(f"{kind}_gathered")
                self.xe_ready = sem(f"{kind}_xe_ready")
                self.rows_scalar = sem(f"{kind}_rows_scalar")
                self.rows_vector = sem(f"{kind}_rows_vector")
                self.turned = sem(f"{kind}_turned")
                self.g_ready = sem(f"{kind}_g_ready")
                self.sig_ready = sem(f"{kind}_sig_ready")
                self.mid_ready = sem(f"{kind}_mid_ready")
                self.y_ready = sem(f"{kind}_y_ready")
                self.scattered = sem(f"{kind}_scattered")
                self.added = sem(f"{kind}_added")
                self.vector_step = sem(f"{kind}_vector_step")

        main, extra = Pass("main"), Pass("extra")
        main.used, extra.used = chunk_used, sem("extra_used")
        extra_loaded = [sem(f"extra_loaded{s}") for s in range(PER_EXPERT)]

        def freed(by, free, n):
            return free[by[n]], by[:n + 1].count(by[n])

        def zcount(tile):
            return zpos[tile] + 1

        def mcount(x):
            return mpos[x] + 1

        def zbank(tile):
            return bank[zpos[tile] % ZBANKS]

        def mbank(x):
            return bank[ZBANKS + mpos[x] % ZBANKS]

        FRONT_LOADS = [len(range(s, NFRONT + 1, FRONT_SLOTS)) for s in range(FRONT_SLOTS)] + [0] * (SLOTS - FRONT_SLOTS)

        def expert_loads(m):
            return 16 * (FRONT_LOADS[m % SLOTS] + m // SLOTS + 1)

        RANKS = (NB + 1) * E
        PW_EARLY = 5
        SCATTER = (4, 5, 6, 7, 2, 3, 6, 7)
        LAST = E * PER_EXPERT
        K3 = [(w_gate, "gate"), (w_up, "up"), (w_down, "down")]

        def chunk_source(e, c):
            w = K3[c // 4][0]
            return w[0, e, (c % 4) * 2 * P:(c % 4 + 1) * 2 * P, :].rearrange("(k p) f -> p k f", p=P)

        def chained(eng, s, base=0):
            n = [0]

            def link(ins):
                ins.then_inc(s, 1)
                n[0] += 1
                eng.wait_ge(s, base + n[0])
            link.count = n
            return link

        block = ctx.enter_context(nc.Block())

        @block.sync
        def _(sp):
            for b, rows, t0 in BLOCKS:
                src = x_prompt[0, t0:t0 + rows, :] if b < NB else x_sample[:, 0, :]
                sp.dma_start(x_tok[0:rows, b, :], src).then_inc(ld_x[b], 16)
            sp.wait_ge(ld_vec, 16 * 6)
            sp.wait_ge(ld_gk, 32)
            def load(m):
                sp.dma_start(by_k[m % SLOTS], chunk_source(m // PER_EXPERT, m % PER_EXPERT))\
                    .then_inc(slot_loaded[m % SLOTS], 16)

            EARLY = zpos[("r", 0)] // 2 + FRONT_SLOTS
            for n in range(NFRONT):
                kind, f = ztiles[2 * n]
                if n >= FRONT_SLOTS:
                    sp.wait_ge(z_done, 2 * (n - FRONT_SLOTS + 1))
                w = w_o[0] if kind == "wo" else w_in[0]
                c0 = zcol[kind] + f * P
                sp.dma_start(by_col[n % FRONT_SLOTS], w[:, c0:c0 + 2 * P].rearrange("(k p) f -> p k f", p=P))\
                    .then_inc(slot_loaded[n % FRONT_SLOTS], 16)
                if n == EARLY:
                    sp.wait_ge(misc_done, mcount(("so", NS - 1)))
                    sp.wait_ge(sp_stored, 16)
                    sp.wait_ge(o_ready, 2)
                if EARLY <= n < EARLY + 4:
                    load(FRONT_SLOTS + 2 * (n - EARLY))
                    load(FRONT_SLOTS + 2 * (n - EARLY) + 1)

            sp.wait_ge(z_done, 2 * (NFRONT - FRONT_SLOTS + 1))
            sp.dma_start(by_k[NFRONT % FRONT_SLOTS], w_ple_proj[0].rearrange("(k p) f -> p k f", p=P))\
                .then_inc(slot_loaded[NFRONT % FRONT_SLOTS], 16)

            sp.wait_ge(a_done, KT)
            sp.wait_ge(st_stored[0], 16 * NS // 2)
            sp.wait_ge(st_stored[1], 16 * NS // 2)
            for m in range(SLOTS - LATE_SLOTS, SLOTS):
                load(m)
            for n in range(NFRONT - FRONT_SLOTS + 1, NFRONT):
                sp.wait_ge(z_done, 2 * (n + 1))
                load(n % FRONT_SLOTS)
            sp.wait_ge(pw_done, KT)
            load(NFRONT % FRONT_SLOTS)
            TURN = UNROLL * PER_EXPERT
            with sp.Fori(0, ROUNDS - 1) as i:
                for r in range(SLOTS, SLOTS + TURN):
                    sp.wait_ge(chunk_used, i * TURN + (r - SLOTS + 1))
                    sp.dma_start(by_k[r % SLOTS], chunk_source(i * UNROLL + r // PER_EXPERT, r % PER_EXPERT))\
                        .then_inc(slot_loaded[r % SLOTS], 16)
            for m in range(SLOTS + TURN * (ROUNDS - 1), LAST):
                sp.wait_ge(chunk_used, m - SLOTS + 1)
                load(m)

            sp.wait_ge(table_ready, 1)
            n_extra = sp.value_load(ov_table_i[0:1, 2 * MAX_OV:2 * MAX_OV + 1], min_val=0, max_val=MAX_OV)
            with sp.If(n_extra > 0):
                with sp.Fori(0, n_extra) as i:
                    e = sp.value_load(ov_table_i[0:1, bass.ds(i, 1)], min_val=0, max_val=E - 1)
                    for c in range(PER_EXPERT):
                        s = EXTRA_SLOT + c
                        sp.wait_ge(chunk_used, LAST - SLOTS + s + 1)
                        sp.wait_ge(extra.used, i * PER_EXPERT + (c + 1))
                        sp.dma_start(by_k[s], chunk_source(e, c)).then_inc(extra_loaded[c], 16)

            for m in range(LAST, LAST + KT // 2):
                sp.wait_ge(chunk_used, m - SLOTS + 1)
                sp.dma_start(by_col[m % SLOTS], w_ple_gate[0, :, (m - LAST) * 2 * P:(m - LAST + 1) * 2 * P]
                             .rearrange("(k p) f -> p k f", p=P)).then_inc(slot_loaded[m % SLOTS], 16)

            for b, rows, t0 in BLOCKS:
                sp.wait_ge(yrow_ready["vector"], b + 1)
                sp.wait_ge(yrow_ready["scalar"], b + 1)
                dst = y_prompt[0, t0:t0 + rows, :] if b < NB else y_sample[:, 0, :]
                sp.dma_start(dst, x2[0:rows, b, :]).then_inc(y_stored, 16)
            sp.wait_ge(y_stored, 16 * len(BLOCKS))

        @block.gpsimd
        def _(pool):
            link = chained(pool, pool_step)
            pool.memset(ident[:, :], 0.0)
            pool.memset(before[:, :], 1.0)
            pool.memset(upto[:, :], 1.0)
            pool.memset(ones[:, :], 1.0)
            pool.memset(scanmask, 1.0)
            link(pool.memset(vrows, 0.0))
            pool.affine_select(out=ident[:, :], in_=ident[:, :], compare_op=ALU.not_equal, fill=1.0, base=0,
                               pattern=[[-1, P]], channel_multiplier=1)
            pool.affine_select(out=before[:, :], in_=before[:, :], compare_op=ALU.is_gt, fill=0.0, base=0,
                               pattern=[[1, P]], channel_multiplier=-1)
            pool.affine_select(out=upto[:, :], in_=upto[:, :], compare_op=ALU.is_ge, fill=0.0, base=0,
                               pattern=[[1, P]], channel_multiplier=-1)
            pool.memset(scanmask[:, 0:L:GLA_CHUNK], 0.0)
            link(pool.memset(scanmask[:, L:T], 0.0))
            pool.tensor_tensor(two_eyes[:, :], ident[:, 0:CAP], ident[:, CAP:P], ALU.add)
            link(pool.tensor_copy(attmask, upto[:, :]))
            link(pool.memset(attmask[0:GLA_CHUNK, GLA_CHUNK:P], 0.0))
            pool.iota(iota_c[:, :], [[0, 2], [1, CAP]], base=0, channel_multiplier=0, allow_small_or_imprecise_dtypes=True)
            link(pool.iota(iota_e[:, :], [[1, E]], base=0, channel_multiplier=0, allow_small_or_imprecise_dtypes=True))
            pool.memset(rank[:, :], -1.0)
            pool.memset(wts[:, :], 0.0).then_inc(consts_ready, 1)
            pool.wait_ge(ld_rows, 16 * 3)
            link(pool.tensor_copy(bspT[:, :, P:2 * P], bspT[:, :, 0:P]))
            pool.tensor_copy(bspT[:, :, L:T], bspT[:, :, 0:1].to_broadcast([P, H, NS])).then_inc(bsp_ready, 1)
            for b in range(2):
                pool.dma_start(st[:, b, :].rearrange("p (h v) -> p h v", h=H),
                               state_gla[0, b].rearrange("h k v -> k h v")).then_inc(st_loaded[b], 16)
            for b, rows, _ in BLOCKS:
                pool.wait_ge(vn_scaled, b + 1)
                link(pool.tensor_tensor(vn[0:rows, b, :], vn[0:rows, b, :], vngrow[0:rows, :], ALU.mult))
                pool.tensor_tensor(vn[0:rows, b, :], vn[0:rows, b, :], vnbrow[0:rows, :], ALU.add)\
                    .then_inc(vn_ready, 1)
            pool.wait_ge(vn_ready, NB + 1)
            pool.dma_start(mix_v_sample[0, :, 0, :], vn[0:NS, NB, :]).then_inc(vn_stored, 16)
            pool.wait_ge(state_ready, 2 * NCH)
            pool.dma_start(st_prompt[0, 0].rearrange("h k v -> k h v"),
                           S_last.rearrange("p (h v) -> p h v", h=H)).then_inc(sp_stored, 16)
            for b in range(NS):
                pool.wait_ge(st_ready, 2 * (b + 1))
                pool.dma_start(st_sample[0, b].rearrange("h k v -> k h v"),
                               st[:, b % 2, :].rearrange("p (h v) -> p h v", h=H)).then_inc(st_stored[b % 2], 16)
                if b + 2 < NS:
                    pool.wait_ge(st_stored[b % 2], 16 * (b // 2 + 1))
                    pool.wait_ge(misc_done, mcount(("so", b)))
                    pool.dma_start(st[:, b % 2, :].rearrange("p (h v) -> p h v", h=H),
                                   state_gla[0, b + 2].rearrange("h k v -> k h v")).then_inc(st_loaded[b % 2], 16)
            pool.wait_ge(misc_done, mcount(("oT", KT - 1)))
            pool.memset(x2[:, NB, :], 0.0)
            pool.wait_ge(b_done, KT)
            pool.memset(SWT[1], 0.0)
            pool.wait_ge(z_done, zcount(("wo", KT - 1)))
            pool.memset(y_rows, 0.0).then_inc(zeros_ready, 1)
            pool.wait_ge(zeros_ready, 1)
            pool.dma_start(y_rows[0:E, :], b_down[0]).then_inc(ld_bdown, 16)
            pool.wait_ge(ld_router, 48)
            for b in range(NB):
                pool.wait_ge(x2_scaled, b + 1)
                pool.tensor_tensor(x2[:, b, :], x2[:, b, :], g2row[:, :], ALU.mult).then_inc(x2_ready, 1)
            pool.wait_ge(vn_stored, 16)
            pool.wait_ge(sp_stored, 16)
            pool.wait_ge(st_stored[0], 16 * NS // 2)
            pool.wait_ge(st_stored[1], 16 * NS // 2)

        @block.tensor
        def _(pe):
            mm = nc.tensor.matmul
            turn = nc.tensor.transpose

            def z_tile(kind, f):
                n = zpos[(kind, f)]
                if n >= ZBANKS:
                    pe.wait_ge(*freed(zby, z_free, n - ZBANKS))
                chunk, half = n // 2, n % 2
                s = chunk % FRONT_SLOTS
                if half == 0:
                    pe.wait_ge(slot_loaded[s], 16 * (chunk // FRONT_SLOTS + 1))
                if (kind, f) == ("k", 0):
                    pe.wait_ge(misc_free["vector"], mby[:mcount(("nT", KT - 1))].count("vector"))
                if (kind, f) == ("wo", 0):
                    pe.wait_ge(a_done, KT)
                rhs = mixT if kind == "wo" else nT
                for k in range(KT):
                    ins = mm(zbank((kind, f))[:, 0:T], by_col[s][:, k, half * P:(half + 1) * P], rhs[:, k, :],
                             start=(k == 0), stop=(k == KT - 1))
                ins.then_inc(z_done, 1)

            def misc_step(x):
                n = mpos[x]
                if n >= ZBANKS:
                    pe.wait_ge(*freed(mby, misc_free, n - ZBANKS))
                out = mbank(x)
                kind, *at = x if isinstance(x, tuple) else (x,)
                f = at[0] if at else None
                if kind == "vec":
                    pe.wait_ge(consts_ready, 1)
                    pe.wait_ge(ld_vec, 16 * 6)
                    ins = turn(out[:, 0:40], vrows[0:40, :], ident[0:40, 0:40])
                elif kind in ("nT", "xT"):
                    src = xn if kind == "nT" else x_tok
                    if f == 0 and kind == "nT":
                        pe.wait_ge(xn_ready, 1)
                    for b, rows, t0 in BLOCKS:
                        ins = turn(out[:, t0:t0 + rows], src[0:rows, b, f * P:(f + 1) * P], ident[0:rows, 0:rows])
                elif kind == "gk":
                    pe.wait_ge(ld_gk, 32)
                    pe.wait_ge(misc_free["vector"], mby[:mcount(("nT", KT - 1))].count("vector"))
                    for k in range(KT):
                        ins = mm(out[0:RANK, 0:T], wgk[:, k, :], nT[:, k, :], start=(k == 0), stop=(k == KT - 1))
                elif kind == "bias":
                    pe.wait_ge(ld_bias, 32)
                    for j in range(KT):
                        ins = turn(out[:, j * E:(j + 1) * E], bias_rows[0:E, f, j * P:(j + 1) * P], ident[0:E, 0:E])
                elif kind == "pT":
                    pe.wait_ge(ld_p, 48)
                    for b, rows, t0 in BLOCKS:
                        ins = turn(out[:, t0:t0 + rows], p_tok[0:rows, b, f * P:(f + 1) * P], ident[0:rows, 0:rows])
                elif kind == "wsp":
                    pe.wait_ge(ld_wsp, 32)
                    for h in range(MH):
                        ins = turn(out[:, h * P:(h + 1) * P], wsp[:, h, :], ident[:, :])
                elif kind == "la":
                    pe.wait_ge(*freed(mby, misc_free, mpos["gk"]))
                    ins = mm(out[:, 0:T], wgk2[0:RANK, f * P:(f + 1) * P], gkT[0:RANK, :], start=True, stop=True)
                elif kind in ("vT", "vgT"):
                    tile = ("v" if kind == "vT" else "vg", f)
                    pe.wait_ge(*freed(zby, z_free, zpos[tile]))
                    src = t[f % 2 + (2 if kind == "vgT" else 0)]
                    for b, rows, t0 in BLOCKS:
                        ins = turn(out[0:rows, b * P:(b + 1) * P], src[:, t0:t0 + rows], ident[:, :])
                elif kind == "kdT":
                    pe.wait_ge(gla_in_ready, 1)
                    b, rows, t0 = BLOCKS[f]
                    src = kdT if f < NB else kT
                    for h in range(H):
                        ins = turn(out[0:rows, h * DK:(h + 1) * DK], src[:, h, t0:t0 + rows], ident[:, :])
                elif kind == "att":
                    t0 = f * P
                    for h in range(H):
                        ins = mm(out[:, h * P:(h + 1) * P], keT[:, h, t0:t0 + P], qT[:, h, t0:t0 + P],
                                 start=True, stop=True)
                elif kind == "dS":
                    c, i = at
                    b, r0 = c * GLA_CHUNK // P, c * GLA_CHUNK % P
                    pe.wait_ge(*freed(mby, misc_free, mpos[("kdT", b)]))
                    pe.wait_ge(*freed(mby, misc_free, mpos[("vT", KT - 1)]))
                    for h in (2 * i, 2 * i + 1):
                        ins = mm(out[:, (h % 2) * DV:(h % 2 + 1) * DV],
                                 kd_tok[r0:r0 + GLA_CHUNK, b, h * DK:(h + 1) * DK],
                                 v_tok[r0:r0 + GLA_CHUNK, b, h * DV:(h + 1) * DV], start=True, stop=True)
                elif kind == "o":
                    b, i = at
                    pe.wait_ge(att_ready, b + 1)
                    pe.wait_ge(state_ready, 2 * min(2 * b + 1, NCH - 1))
                    for h in (2 * i, 2 * i + 1):
                        o0 = (h % 2) * DV
                        ins = mm(out[:, o0:o0 + DV], att[:, b, h, :], v_tok[:, b, h * DV:(h + 1) * DV],
                                 start=True, stop=False, skip_group_check=True)
                        for c in (2 * b, 2 * b + 1):
                            if c > 0:
                                r0, t0 = c * GLA_CHUNK % P, c * GLA_CHUNK
                                ins = mm(out[r0:r0 + GLA_CHUNK, o0:o0 + DV], qT[:, h, t0:t0 + GLA_CHUNK],
                                         S_ver[:, c - 1, h * DV:(h + 1) * DV], start=False, stop=True,
                                         skip_group_check=True)
                elif kind == "kv":
                    b, i = at
                    if i == 0:
                        pe.wait_ge(kmask_ready, b + 1)
                    for h in (2 * i, 2 * i + 1):
                        ins = mm(out[:, (h % 2) * DV:(h % 2 + 1) * DV], kmask[0:NS, b % 2, h * DK:(h + 1) * DK],
                                 v_tok[0:NS, NB, h * DV:(h + 1) * DV], start=True, stop=True)
                elif kind == "so":
                    pe.wait_ge(st_ready, 2 * (f + 1))
                    for j in range(2 * H):
                        ins = mm(out[:, j:j + 1], st[:, f % 2, j * P:(j + 1) * P], qT[:, j // 2, L + f:L + f + 1],
                                 start=True, stop=True)
                elif kind == "soT":
                    if f == 0:
                        pe.wait_ge(*freed(mby, misc_free, mpos[("so", NS - 1)]))
                    for j in range(4):
                        ins = turn(out[0:NS, j * P:(j + 1) * P], oST[:, 4 * f + j, :], ident[:, :])
                elif kind == "mix":
                    if f == 0:
                        pe.wait_ge(vn_ready, NB + 1)
                        pe.wait_ge(dw_ready, 1)
                    h = f * MH // KT
                    for b in range(NB):
                        mm(out[:, b * P:(b + 1) * P], vn[:, b, f * P:(f + 1) * P], WT[:, h, :], start=True, stop=True)
                    ins = mm(out[:, L:T], vn[0:NS, NB, f * P:(f + 1) * P], dw[:, h * NS:(h + 1) * NS],
                             start=True, stop=True)
                elif kind == "oT":
                    pe.wait_ge(o_ready, 2)
                    for b, rows, t0 in BLOCKS:
                        ins = turn(out[:, t0:t0 + rows], o_tok[0:rows, b, f * P:(f + 1) * P], ident[0:rows, 0:rows])
                ins.then_inc(misc_done, 1)

            for x in plan:
                if x[0] == "z":
                    z_tile(*x[1:])
                else:
                    misc_step(x)

            def pw_tile(f):
                if f > 0:
                    pe.wait_ge(pw_ready, f)
                for k in range(PK):
                    ins = mm(bank[0][:, 0:T], by_k[s_pw][:, k, f * P:(f + 1) * P], pTv[:, k, :],
                             start=(k == 0), stop=(k == PK - 1))
                ins.then_inc(pw_done, 1)

            pe.wait_ge(h_ready, KT)
            for n in range(len(misc) - ZBANKS, len(misc)):
                pe.wait_ge(*freed(mby, misc_free, n))
            for b, rows, t0 in BLOCKS:
                for i in range(2):
                    for j in range(HALF):
                        f = i * HALF + j
                        ins = turn(bank[2 + 2 * b + i][0:rows, j * P:(j + 1) * P], hTv[:, f, t0:t0 + rows], ident[:, :])
                    ins.then_inc(hrow_done, 1)
            pe.wait_ge(hg_ready, KT)
            pe.wait_ge(ld_router, 48)
            for b, rows, t0 in BLOCKS:
                for k in range(KT):
                    ins = mm(bank[1][0:rows, b * E:(b + 1) * E], hgT[:, k, t0:t0 + rows], wrtv[:, k, :],
                             start=(k == 0), stop=(k == KT - 1))
            ins.then_inc(router_done, 1)
            s_pw = NFRONT % FRONT_SLOTS
            pe.wait_ge(slot_loaded[s_pw], 16 * FRONT_LOADS[s_pw])
            for f in range(PW_EARLY):
                pw_tile(f)
            pe.wait_ge(sel_ready, 1)
            for b in range(NB + 1):
                for c in range(b + 1):
                    mm(bank[1][:, RANKS + b * E:RANKS + (b + 1) * E], (before if c == b else ones)[:, :], selm[:, c, :],
                       start=(c == 0), stop=(c == b))
            for c in range(NB + 1):
                ins = mm(bank[1][:, RANKS + (NB + 1) * E:RANKS + (NB + 2) * E], ones[:, :], selm[:, c, :],
                         start=(c == 0), stop=(c == NB))
            ins.then_inc(rank_done, 1)
            for f in range(PW_EARLY, KT):
                pw_tile(f)

            def weights_step(ps, banks, lhs, chunks):
                for s, loaded, value, k in chunks:
                    pe.wait_ge(loaded, value)
                    for n in range(2):
                        for i in range(2):
                            ins = mm(bank[banks[n]][i * CAP:(i + 1) * CAP, :], lhs[:, k + i, :],
                                     by_k[s][:, i, n * 512:(n + 1) * 512], start=(k == 0), stop=(k == KT - 2))
                    ins.then_inc(ps.used, 1)

            def turn_rows(ps, count, b):
                pe.wait_ge(ps.rows_scalar, count)
                pe.wait_ge(ps.rows_vector, count)
                for f in range(KT):
                    ins = mm(bank[b][:, f * CAP:(f + 1) * CAP], rows_sb[:, f * P:(f + 1) * P], two_eyes[:, :],
                             start=True, stop=True)
                ins.then_inc(ps.turned, 1)

            def gather(width):
                for f in range(KT):
                    for b in range(NB + 1):
                        mm(bank[6 + f // HALF][:, (f % HALF) * width:(f % HALF + 1) * width],
                           x2[:, b, f * P:(f + 1) * P], Ssel[:, b, 0:width], start=(b == 0), stop=(b == NB))

            def turn_selection(ps):
                for b, rows, t0 in BLOCKS:
                    ins = turn(bank[1][:, t0:t0 + rows], Swt[0:rows, b, :], ident[0:rows, 0:rows])
                ins.then_inc(ps.gathered, 1)

            def scatter(ps, n, parity, rows_copied=None, fs=range(KT)):
                if fs[0] == 0:
                    pe.wait_ge(ps.y_ready, n + 1)
                for f in fs:
                    if f == HALF and rows_copied is not None:
                        pe.wait_ge(ps.rows_scalar, rows_copied)
                        pe.wait_ge(ps.rows_vector, rows_copied)
                    if f >= 6:
                        pe.wait_ge(ps.added, n * KT + f - 3)
                    mm(bank[SCATTER[f]][:, 0:T], y_rows[:, f * P:(f + 1) * P], SWT[parity][:, :],
                       start=True, stop=True).then_inc(ps.scattered, 1)

            def main_chunks(u, i, c0, c1):
                loads = 16 * UNROLL * PER_EXPERT // SLOTS
                return [(r % SLOTS, slot_loaded[r % SLOTS], i * loads + expert_loads(r), 2 * (r % 4))
                        for r in range(u * PER_EXPERT + c0, u * PER_EXPERT + c1)]

            pe.wait_ge(pw_ready, KT)
            pe.wait_ge(zeros_ready, 1)
            pe.wait_ge(wts_ready, 1)
            for b, rows, t0 in BLOCKS:
                ins = turn(bank[0][0:E, t0:t0 + rows], wtsv[0:rows, b, 0:E], ident[0:rows, 0:rows])
            ins.then_inc(wT_done, 1)
            pe.sem_inc(extra.used, PER_EXPERT)
            pe.wait_ge(x2_ready, NB + 1)
            pe.wait_ge(main.selected, 1)
            gather(P)
            turn_selection(main)
            with pe.Fori(0, ROUNDS) as i:
                for u in range(UNROLL):
                    j = i * UNROLL + u
                    own = slice(u % 2 * CAP, (u % 2 + 1) * CAP)
                    pe.wait_ge(main.xe_ready, j + 1)
                    weights_step(main, (0, 1), xe[:, :, own], main_chunks(u, i, 0, 4))
                    weights_step(main, (2, 3), xe[:, :, own], main_chunks(u, i, 4, 6))
                    turn_rows(main, 2 * j + 1, 6)
                    weights_step(main, (2, 3), xe[:, :, own], main_chunks(u, i, 6, 8))
                    pe.wait_ge(main.g_ready, j + 1)
                    if u % 2 == 0:
                        scatter(main, j, (u + 1) % 2, fs=range(HALF))
                        turn_rows(main, 2 * j + 2, 0)
                        scatter(main, j, (u + 1) % 2, 2 * j + 2, fs=range(HALF, KT))
                        pe.wait_ge(main.selected, j + 2)
                    else:
                        scatter(main, j, (u + 1) % 2, 2 * j + 2)
                        turn_rows(main, 2 * j + 2, 0)
                        pe.wait_ge(main.selected, j + 2)
                        pe.wait_ge(main.added, j * KT + KT)
                        gather(P)
                    turn_selection(main)
                    pe.wait_ge(main.mid_ready, j + 1)
                    weights_step(main, (4, 5), gs, main_chunks(u, i, 8, 12))
                    pe.wait_ge(main.added, j * KT + KT)
            pe.wait_ge(main.xe_ready, E + 1)
            scatter(main, E, 1)

            pe.wait_ge(table_ready, 1)
            n_extra = pe.value_load(ov_table_i[0:1, 2 * MAX_OV:2 * MAX_OV + 1], min_val=0, max_val=MAX_OV)
            with pe.If(n_extra > 0):
                pe.wait_ge(main.added, (E + 1) * KT)
                with pe.Fori(0, n_extra) as i:
                    def extra_chunks(c0, c1):
                        return [(EXTRA_SLOT + c, extra_loaded[c], i * 16 + 16, 2 * (c % 4)) for c in range(c0, c1)]
                    own = slice(0, CAP)
                    pe.wait_ge(extra.selected, i + 1)
                    gather(CAP)
                    turn_selection(extra)
                    pe.wait_ge(extra.xe_ready, i + 1)
                    weights_step(extra, (0, 1), xe[:, :, own], extra_chunks(0, 4))
                    weights_step(extra, (2, 3), xe[:, :, own], extra_chunks(4, 6))
                    turn_rows(extra, i * 2 + 1, 6)
                    weights_step(extra, (2, 3), xe[:, :, own], extra_chunks(6, 8))
                    turn_rows(extra, i * 2 + 2, 0)
                    pe.wait_ge(extra.mid_ready, i + 1)
                    weights_step(extra, (4, 5), gs, extra_chunks(8, 12))
                    scatter(extra, i, 0)
                    pe.wait_ge(extra.added, i * KT + KT)

            for f in range(KT):
                s = (LAST + f // 2) % SLOTS
                if f % 2 == 0:
                    pe.wait_ge(slot_loaded[s], expert_loads(LAST + f // 2))
                if f >= 4:
                    pe.wait_ge(gate_pre, f - 3)
                for k in range(KT):
                    if f == 0:
                        pe.wait_ge(h2_ready, k + 1)
                    ins = mm(bank[f % 4][:, 0:T], by_col[s][:, k, (f % 2) * P:(f % 2 + 1) * P], n3T[:, k, :],
                             start=(k == 0), stop=(k == KT - 1))
                ins.then_inc(gate_done, 1)
                if f == 0:
                    for k in range(KT):
                        pe.wait_ge(sq_ready, k + 1)
                        ins = mm(bank[4][:, 0:T], ones[:, :], sqT[:, k, :], start=(k == 0), stop=(k == KT - 1))
                    ins.then_inc(rms_done, 1)
            pe.wait_ge(ysq_ready, KT)
            for b, rows, t0 in BLOCKS:
                for k in range(KT):
                    ins = mm(bank[5][0:rows, b:b + 1], sqT[:, k, t0:t0 + rows], ones[:, 0:1],
                             start=(k == 0), stop=(k == KT - 1))
            ins.then_inc(y_stat, 1)
            pe.wait_ge(h3_ready, KT)
            for b, rows, t0 in BLOCKS:
                for i in range(2):
                    n = 2 * b + i
                    if n >= 4:
                        pe.wait_ge(yrow_ready["scalar" if i else "vector"], b - 1)
                    for j in range(HALF):
                        f = i * HALF + j
                        ins = turn(bank[n % 4][0:rows, j * P:(j + 1) * P], y3T[:, f, t0:t0 + rows], ident[:, :])
                    ins.then_inc(yrow_done, 1)

        @block.vector
        def _(dve):
            v = nc.vector
            link = chained(dve, dve_step)

            def vec(row, rows=P):
                return vecT[0:rows, row:row + 1]

            def empty(x):
                assert mby[mpos[x]] == "vector"
                return misc_free["vector"]

            dve.wait_ge(misc_done, mcount("vec"))
            v.tensor_copy(vecT[:, 0:40], mbank("vec")[:, 0:40]).then_inc(empty("vec"), 1)
            dve.wait_ge(misc_free["vector"], 1)
            dve.wait_ge(x_squares, NB + 1)
            for b, rows, _ in BLOCKS:
                ins = v.tensor_scalar(xrs[0:rows, b:b + 1], xss[0:rows, b:b + 1], 1.0 / D, EPS, ALU.mult, ALU.add)
            ins.then_inc(x_scale_sum, 1)
            dve.wait_ge(x_root, 1)
            for b, rows, _ in BLOCKS:
                ins = v.reciprocal(xrs[0:rows, b:b + 1], xrs[0:rows, b:b + 1])
            link(ins)
            for b, rows, _ in BLOCKS:
                ins = v.tensor_scalar(xn[0:rows, b, :], x_tok[0:rows, b, :], xrs[0:rows, b:b + 1], None, ALU.mult)
            ins.then_inc(xn_ready, 1)
            for f in range(KT):
                dve.wait_ge(misc_done, mcount(("nT", f)))
                v.tensor_scalar(nT[:, f, :], mbank(("nT", f))[:, 0:T], vec(f), None, ALU.mult)\
                    .then_inc(empty(("nT", f)), 1)
            for h in range(H):
                dve.wait_ge(misc_done, mcount(("la", h)))
                ins = v.tensor_scalar(keT[:, h, :], mbank(("la", h))[:, 0:T], vec(32 + h), None, ALU.add)
                ins.then_inc(empty(("la", h)), 1)
            dve.wait_ge(*freed(mby, misc_free, mpos[("la", H - 1)]))
            v.scalar_tensor_tensor(e1, keT, -1.0, keT, ALU.mult, ALU.max).then_inc(abs_ready, 1)
            dve.wait_ge(la_ready, 1)
            link(v.scalar_tensor_tensor(kdT, keT, 0.0, e1, ALU.min, ALU.subtract))
            for h in range(H):
                ins = v.tensor_tensor_scan(bT[:, h, :], scanmask, kdT[:, h, :], 0.0, ALU.mult, ALU.add)
            ins.then_inc(cum_ready, 1)
            dve.wait_ge(cum_ready, 1)
            by_chunk = lambda a: a[:, :, 0:L].rearrange("p h (c s) -> p h c s", c=NCH)
            for h in range(H):
                bh = bT[:, h, 0:L].rearrange("p (c s) -> p c s", c=NCH)
                ins = v.tensor_tensor(kdT[:, h, 0:L].rearrange("p (c s) -> p c s", c=NCH),
                                      bh[:, :, GLA_CHUNK - 1:GLA_CHUNK].to_broadcast([P, NCH, GLA_CHUNK]), bh,
                                      ALU.subtract)
            ins.then_inc(back_ready, 1)
            for i in range(2):
                dve.wait_ge(misc_done, mcount(("bias", i)))
                v.tensor_copy(biasT[:, i * KT * E:(i + 1) * KT * E], mbank(("bias", i))[:, 0:KT * E])\
                    .then_inc(empty(("bias", i)), 1)
            dve.wait_ge(misc_done, mcount("wsp"))
            v.tensor_tensor(WT, mbank("wsp")[:, 0:MH * P].rearrange("p (h t) -> p h t", h=MH),
                            upto[:, :].unsqueeze(1).to_broadcast([P, MH, P]), ALU.mult).then_inc(empty("wsp"), 1)
            for h in range(MH):
                ins = v.tensor_scalar(dw[:, h * NS:(h + 1) * NS], ident[0:NS, 0:NS], w00[:, h:h + 1], None, ALU.mult)
            ins.then_inc(dw_ready, 1)
            dve.wait_ge(decays_ready, 3)
            dve.wait_ge(*freed(zby, z_free, zpos[("q", H - 1)]))
            for h in range(H):
                v.tensor_copy(decay[:, h, :], e1[:, h, GLA_CHUNK - 1:L:GLA_CHUNK])
            v.tensor_copy(sdecay, e1[:, :, L:T])
            v.scalar_tensor_tensor(qT[:, :, 0:L], qT[:, :, 0:L], float(DK) ** -0.5, e1[:, :, 0:L], ALU.mult, ALU.mult)
            v.tensor_scalar(qT[:, :, L:T], qT[:, :, L:T], float(DK) ** -0.5, None, ALU.mult)
            v.tensor_tensor(keT[:, :, 0:L], keT[:, :, 0:L], kT[:, :, 0:L], ALU.mult)
            v.memset(att, 0.0)
            v.tensor_tensor(kdT[:, :, 0:L], kdT[:, :, 0:L], kT[:, :, 0:L], ALU.mult).then_inc(gla_in_ready, 1)
            dve.wait_ge(gla_in_ready, 1)

            def rows_from(kind, f, out):
                x = (kind, f)
                dve.wait_ge(misc_done, mcount(x))
                v.tensor_copy(out[:, 0:NB, f * P:(f + 1) * P],
                              mbank(x)[:, 0:NB * P].rearrange("p (b f) -> p b f", b=NB))
                v.tensor_copy(out[0:NS, NB, f * P:(f + 1) * P], mbank(x)[0:NS, NB * P:(NB + 1) * P])\
                    .then_inc(empty(x), 1)

            def att_step(b):
                x = ("att", b)
                dve.wait_ge(misc_done, mcount(x))
                for h in range(H):
                    ins = v.copy_predicated(att[:, b, h, :], attmask.bitcast(I32), mbank(x)[:, h * P:(h + 1) * P])
                ins.then_inc(empty(x), 1)
                dve.wait_ge(*freed(mby, misc_free, mpos[x]))
                dve.sem_inc(att_ready, 1)

            def state_of(c):
                return S_ver[:, c, :] if c < NCH - 1 else S_last

            def state_step(c, i):
                x = ("dS", c, i)
                dve.wait_ge(misc_done, mcount(x))
                if c == 0:
                    ins = v.tensor_copy(state_of(0)[:, 2 * i * DV:(2 * i + 2) * DV], mbank(x)[:, :])
                else:
                    for h in (2 * i, 2 * i + 1):
                        hs = slice(h * DV, (h + 1) * DV)
                        ins = v.scalar_tensor_tensor(state_of(c)[:, hs], state_of(c - 1)[:, hs], decay[:, h, c:c + 1],
                                                     mbank(x)[:, (h % 2) * DV:(h % 2 + 1) * DV], ALU.mult, ALU.add)
                ins.then_inc(empty(x), 1)
                dve.wait_ge(*freed(mby, misc_free, mpos[x]))
                dve.sem_inc(state_ready, 1)

            def sample_state(b, i):
                x = ("kv", b, i)
                dve.wait_ge(misc_done, mcount(x))
                if i == 0:
                    dve.wait_ge(st_loaded[b % 2], 16 * (b // 2 + 1))
                for h in (2 * i, 2 * i + 1):
                    s = st[:, b % 2, h * DV:(h + 1) * DV]
                    ins = v.scalar_tensor_tensor(s, s, sdecay[:, h, b:b + 1], mbank(x)[:, (h % 2) * DV:(h % 2 + 1) * DV],
                                                 ALU.mult, ALU.add)
                ins.then_inc(empty(x), 1)
                dve.wait_ge(*freed(mby, misc_free, mpos[x]))
                dve.sem_inc(st_ready, 1)

            def o_norm(part, sample):
                r = slice(NB * H, (NB + 1) * H) if sample else slice(0, NB * H)
                rows = NS if sample else P
                dve.wait_ge(o_squares, part)
                v.tensor_scalar(ors[0:rows, r], oss[0:rows, r], 1.0 / DV, EPS, ALU.mult, ALU.add).then_inc(o_sum, 1)
                dve.wait_ge(o_root, 1 + sample)
                link(v.reciprocal(ors[0:rows, r], ors[0:rows, r]))
                for b in ([NB] if sample else range(NB)):
                    for h in range(H):
                        hs = slice(h * DV, (h + 1) * DV)
                        ins = v.tensor_scalar(o_tok[0:rows, b, hs], o_tok[0:rows, b, hs],
                                              ors[0:rows, b * H + h:b * H + h + 1], None, ALU.mult)
                ins.then_inc(o_ready, 1)

            def v_norm():
                for b, rows, _ in BLOCKS:
                    for i in range(2):
                        ins = v.bn_stats(vstat[0:rows, 6 * i:6 * i + 6], vn[0:rows, b, i * 512:(i + 1) * 512])
                    link(ins)
                    link(v.bn_aggr(vmv[0:rows, 2 * b:2 * b + 2], vstat[0:rows, :]))
                    ins = v.tensor_scalar(vrs[0:rows, b:b + 1], vmv[0:rows, 2 * b + 1:2 * b + 2], EPS, None, ALU.add)
                ins.then_inc(vn_var, 1)
                dve.wait_ge(vn_root, 1)
                for b, rows, _ in BLOCKS:
                    ins = v.reciprocal(vrs[0:rows, b:b + 1], vrs[0:rows, b:b + 1])
                link(ins)
                for b, rows, _ in BLOCKS:
                    v.tensor_scalar(vn[0:rows, b, :], vn[0:rows, b, :], vmv[0:rows, 2 * b:2 * b + 1],
                                    vrs[0:rows, b:b + 1], ALU.subtract, ALU.mult).then_inc(vn_scaled, 1)

            def b_step(f):
                x = ("mix", f)
                dve.wait_ge(misc_done, mcount(x))
                dve.wait_ge(*freed(zby, z_free, zpos[("gb", f)]))
                if f > 0:
                    dve.wait_ge(b_done, f)
                ins = v.tensor_tensor(t[4], mbank(x)[:, 0:T], bspT[:, f * MH // KT, :], ALU.add)
                ins.then_inc(empty(x), 1)
                dve.wait_ge(*freed(mby, misc_free, mpos[x]))
                link(v.tensor_tensor(t[4], t[4], t[f % 2], ALU.mult))
                v.tensor_tensor(mixT[:, f, :], t[4], t[2 + f % 2], ALU.mult).then_inc(b_done, 1)

            def r_step(f):
                dve.wait_ge(r_sig, f + 1)
                v.tensor_tensor(t[f % 2], t[f % 2], zbank(("r", f))[:, 0:T], ALU.mult).then_inc(z_free["vector"], 1)

            def a_step(f):
                x = ("oT", f)
                dve.wait_ge(*freed(zby, z_free, zpos[("ga", f)]))
                dve.wait_ge(*freed(zby, z_free, zpos[("r", f)]))
                link(v.tensor_tensor(t[2 + f % 2], t[f % 2], t[2 + f % 2], ALU.mult))
                if f == 0:
                    dve.wait_ge(b_done, KT)
                else:
                    dve.wait_ge(a_done, f)
                dve.wait_ge(misc_done, mcount(x))
                ins = v.scalar_tensor_tensor(t[4], mbank(x)[:, 0:T], vec(36 + f % 2), t[2 + f % 2], ALU.mult, ALU.mult)
                ins.then_inc(empty(x), 1)
                dve.wait_ge(*freed(mby, misc_free, mpos[x]))
                v.tensor_tensor(mixT[:, f, :], mixT[:, f, :], t[4], ALU.add).then_inc(a_done, 1)

            for x in misc:
                if mby[mpos[x]] == "vector" or x in (("soT", 1),):
                    kind, *at = x if isinstance(x, tuple) else (x,)
                    if kind == "vT":
                        rows_from("vT", at[0], v_tok)
                    elif kind == "vgT":
                        rows_from("vgT", at[0], vn)
                        if at[0] == KT - 1:
                            dve.wait_ge(*freed(mby, misc_free, mpos[x]))
                            v_norm()
                            o_norm(NB * H, False)
                    elif kind == "att":
                        att_step(*at)
                    elif kind == "dS":
                        state_step(*at)
                    elif kind == "kv":
                        sample_state(*at)
                    elif kind == "mix":
                        if at[0] == 0:
                            dve.wait_ge(bsp_ready, 1)
                        b_step(*at)
                    elif kind == "soT":
                        o_norm(NB * H + 1, True)
                    elif kind == "oT":
                        if at[0] % 2 == 0:
                            r_step(at[0])
                            r_step(at[0] + 1)
                        a_step(*at)

            dve.wait_ge(vn_stored, 16)
            for f in range(KT):
                dve.wait_ge(z_done, zcount(("wo", f)))
                if f == 0:
                    dve.wait_ge(*freed(mby, misc_free, mpos[("xT", KT - 1)]))
                v.tensor_tensor(hTv[:, f, :], hTv[:, f, :], zbank(("wo", f))[:, 0:T], ALU.add).then_inc(h_ready, 1)
                dve.wait_ge(h_ready, f + 1)
                v.tensor_scalar(hgT[:, f, :], hTv[:, f, :], vec(KT + f), None, ALU.mult).then_inc(hg_ready, 1)
                dve.sem_inc(z_free["vector"], 1)
            dve.wait_ge(h_squares, 2 * (NB + 1))
            for b, rows, _ in BLOCKS:
                ins = v.tensor_tensor(hrs[0:rows, b:b + 1], hss[0:rows, 2 * b:2 * b + 1], hss[0:rows, 2 * b + 1:2 * b + 2],
                                      ALU.add)
            link(ins)
            for b, rows, _ in BLOCKS:
                ins = v.tensor_scalar(hrs[0:rows, b:b + 1], hrs[0:rows, b:b + 1], 1.0 / D, EPS, ALU.mult, ALU.add)
            ins.then_inc(h_sum, 1)
            v.memset(selm, 0.0)
            dve.wait_ge(zeros_ready, 1)
            dve.wait_ge(h_root, 1)
            for b, rows, _ in BLOCKS:
                ins = v.reciprocal(hrs[0:rows, b:b + 1], hrs[0:rows, b:b + 1])
            ins.then_inc(hrs_ready, 1)
            dve.wait_ge(hrs_ready, 1)
            dve.wait_ge(router_done, 1)
            dve.wait_ge(ld_router, 48)
            for b, rows, _ in BLOCKS:
                ins = v.scalar_tensor_tensor(lg[0:rows, b, :], bank[1][0:rows, b * E:(b + 1) * E],
                                             hrs[0:rows, b:b + 1], brrow[0:rows, :], ALU.mult, ALU.add)
            link(ins)
            for b, rows, _ in BLOCKS:
                ins = v.max(m8[0:rows, b, :], lg[0:rows, b, :])
            link(ins)
            for b, rows, _ in BLOCKS:
                v.tensor_scalar(negm[0:rows, b:b + 1], m8[0:rows, b, 0:1], -1.0, None, ALU.mult).then_inc(top_ready, 1)
            for b, rows, _ in BLOCKS:
                ins = v.max_index(idx[0:rows, b, :].bitcast(U32), m8[0:rows, b, :], lg[0:rows, b, :])
            link(ins)
            for b, rows, _ in BLOCKS:
                ins = v.tensor_copy(idx_f[0:rows, b, :], idx[0:rows, b, 0:TOP_K].bitcast(U32))
            link(ins)
            for b, rows, _ in BLOCKS:
                r = slice(0, rows)
                ins = v.tensor_tensor(hit[r, b], iota_e[r, :].unsqueeze(1).to_broadcast([rows, TOP_K, E]),
                                      idx_f[r, b, :].unsqueeze(2).to_broadcast([rows, TOP_K, E]), ALU.is_equal)
            link(ins)
            for b, rows, _ in BLOCKS:
                r = slice(0, rows)
                ins = v.tensor_reduce(selm[r, b, :], hit[r, b].rearrange("p k e -> p e k"), AX.X, ALU.add)
            ins.then_inc(sel_ready, 1)
            dve.wait_ge(top_exp, NB + 1)
            for b, rows, _ in BLOCKS:
                ins = v.reciprocal(esum[0:rows, b:b + 1], esum[0:rows, b:b + 1])
            link(ins)
            for b, rows, _ in BLOCKS:
                ins = v.tensor_scalar(ew[0:rows, b, :], ew[0:rows, b, :], esum[0:rows, b:b + 1], None, ALU.mult)
            link(ins)
            for b, rows, _ in BLOCKS:
                r = slice(0, rows)
                ins = v.tensor_tensor(hit[r, b], hit[r, b], ew[r, b, :].unsqueeze(2).to_broadcast([rows, TOP_K, E]),
                                      ALU.mult)
            link(ins)
            for b, rows, _ in BLOCKS:
                r = slice(0, rows)
                ins = v.tensor_reduce(wtsv[r, b, 0:E], hit[r, b].rearrange("p k e -> p e k"), AX.X, ALU.add)
            ins.then_inc(wts_ready, 1)
            for c in (slice(0, 512), slice(512, 1024)):
                ins = v.scalar_tensor_tensor(x2[0:NS, NB, c], bank[2 + 2 * NB + c.start // 512][0:NS, :], hrs[0:NS, NB:NB + 1],
                                             g2row[0:NS, c], ALU.mult, ALU.mult)
            ins.then_inc(x2_ready, 1)
            dve.wait_ge(rank_done, 1)
            v.tensor_copy(cnt, bank[1][:, RANKS + (NB + 1) * E:RANKS + (NB + 2) * E])
            placed = rankv[:, :, 0:E]
            link(v.scalar_tensor_tensor(placed, bank[1][:, RANKS:RANKS + (NB + 1) * E].rearrange("p (b e) -> p b e", b=NB + 1),
                                        1.0, selm, ALU.add, ALU.mult))
            link(v.tensor_scalar(placed, placed, -1.0, None, ALU.add))

            def select_pair(e):
                for i in range(2):
                    for b in range(NB + 1):
                        v.tensor_scalar(Ssel[:, b, i * CAP:(i + 1) * CAP], iota_c[:, 0:CAP],
                                        rankv[:, b, bass.ds(e + i, 1)], None, ALU.is_equal)

            def select(ps, col, w_col, offset=None, columns=None):
                if offset is None:
                    at_rank = lambda b: rankv[:, b, col]
                else:
                    vlink(v.tensor_scalar(rk[:, :], rankv[:, :, col].rearrange("p b e -> p (b e)"), offset, None,
                                          ALU.subtract))
                    at_rank = lambda b: rk[:, b:b + 1]
                if columns is not None:
                    for b in range(NB + 1):
                        v.tensor_scalar(Ssel[:, b, columns], iota_c[:, 0:CAP], at_rank(b), None, ALU.is_equal)
                for b in range(NB + 1):
                    ins = v.tensor_scalar(Swt[:, b, :], iota_c[:, :], at_rank(b), wtsv[:, b, w_col],
                                          ALU.is_equal, ALU.mult)
                ins.then_inc(ps.selected, 1)

            def through(ps, item, chunks):
                return item * PER_EXPERT + (chunks + (PER_EXPERT if ps is extra else 0))

            def rows_out(ps, item, chunks, b):
                dve.wait_ge(ps.used, through(ps, item, chunks))
                v.tensor_copy(rows_sb[:, 512:1024], bank[b][:, :]).then_inc(ps.rows_vector, 1)

            def biased(out, b, m, col):
                v_in = bank[b][:, 0:EC].rearrange("p (f c) -> p f c", f=KT)
                return v.tensor_tensor(out, v_in, biasv[:, m, :, col].to_broadcast([P, KT, CAP]), ALU.add)

            def gate_step(ps, item, col):
                rows_out(ps, item, 4, 1)
                dve.wait_ge(ps.turned, 2 * item + 1)
                vlink(biased(gs, 6, 0, col))
                v.tensor_scalar(gs, gs, LIMIT, None, ALU.min).then_inc(ps.g_ready, 1)

            def silu_step(ps, item):
                dve.wait_ge(ps.sig_ready, item + 1)
                vlink(v.tensor_tensor(sg, gs, sg, ALU.mult))

            def up_step(ps, item, col):
                dve.wait_ge(ps.turned, 2 * item + 2)
                vlink(biased(us, 0, 1, col))
                vlink(v.tensor_scalar(us, us, LIMIT, -LIMIT, ALU.min, ALU.max))
                v.scalar_tensor_tensor(gs, us, 1.0, sg, ALU.add, ALU.mult).then_inc(ps.mid_ready, 1)

            def add_y(ps, n, fs=range(KT)):
                for f in fs:
                    dve.wait_ge(ps.scattered, n * KT + f + 1)
                    v.tensor_tensor(hTv[:, f, :], hTv[:, f, :], bank[SCATTER[f]][:, 0:T], ALU.add)\
                        .then_inc(ps.added, 1)

            STEPS = 4
            vlink = chained(dve, main.vector_step)
            select_pair(0)
            select(main, bass.ds(0, 1), bass.ds(0, 1))
            link(v.tensor_scalar(nov, cnt, float(CAP), None, ALU.is_gt))
            for n in range(2, LEVELS + 1):
                link(v.scalar_tensor_tensor(nov, cnt, float(n * CAP), nov, ALU.is_gt, ALU.add))
            link(v.tensor_tensor_scan(nov_end, ones[:, 0:E], nov, 0.0, ALU.mult, ALU.add))
            ends = nov_end.unsqueeze(1).to_broadcast([P, MAX_OV, E])
            link(v.tensor_tensor(ovt, ends, iota_c[:, 0:MAX_OV].unsqueeze(2).to_broadcast([P, MAX_OV, E]), ALU.is_le))
            link(v.tensor_reduce(ov_table[:, 0:MAX_OV], ovt, AX.X, ALU.add))
            link(v.tensor_tensor(ovt, ovt, nov.unsqueeze(1).to_broadcast([P, MAX_OV, E]), ALU.mult))
            link(v.tensor_reduce(ov_table[:, MAX_OV:2 * MAX_OV], ovt, AX.X, ALU.add))
            link(v.scalar_tensor_tensor(ov_table[:, MAX_OV:2 * MAX_OV], iota_c[:, 0:MAX_OV], 1.0,
                                        ov_table[:, MAX_OV:2 * MAX_OV], ALU.add, ALU.subtract))
            link(v.tensor_scalar(ov_table[:, MAX_OV:2 * MAX_OV], ov_table[:, MAX_OV:2 * MAX_OV], float(CAP), None,
                                 ALU.mult))
            link(v.tensor_copy(ov_table[:, 2 * MAX_OV:2 * MAX_OV + 1], nov_end[:, E - 1:E]))
            v.tensor_copy(ov_table_i[:, :], ov_table[:, :]).then_inc(table_ready, 1)

            with dve.Fori(0, ROUNDS) as i:
                for u in range(UNROLL):
                    j = i * UNROLL + u
                    vlink = chained(dve, main.vector_step, base=j * STEPS)
                    gate_step(main, j, bass.ds(j, 1))
                    if u % 2 == 1:
                        select_pair(j + 1)
                    select(main, bass.ds(j + 1, 1), bass.ds(j + 1, 1))
                    silu_step(main, j)
                    rows_out(main, j, 8, 3)
                    if u % 2 == 0:
                        add_y(main, j, range(HALF))
                        up_step(main, j, bass.ds(j, 1))
                        add_y(main, j, range(HALF, KT))
                    else:
                        add_y(main, j)
                        up_step(main, j, bass.ds(j, 1))
                    assert vlink.count[0] == STEPS
            add_y(main, E)

            n_extra = dve.value_load(ov_table_i[0:1, 2 * MAX_OV:2 * MAX_OV + 1], min_val=0, max_val=MAX_OV)
            with dve.If(n_extra > 0):
                with dve.Fori(0, n_extra) as i:
                    e = dve.value_load(ov_table_i[0:1, bass.ds(i, 1)], min_val=0, max_val=E - 1)
                    vlink = chained(dve, extra.vector_step, base=i * (STEPS + 1))
                    select(extra, bass.ds(e, 1), bass.ds(e, 1), ov_table[:, bass.ds(i + MAX_OV, 1)], slice(0, CAP))
                    gate_step(extra, i, bass.ds(e, 1))
                    silu_step(extra, i)
                    rows_out(extra, i, 8, 3)
                    up_step(extra, i, bass.ds(e, 1))
                    assert vlink.count[0] == STEPS + 1
                    add_y(extra, i)
                    dve.wait_ge(extra.added, i * KT + KT)

            link = chained(dve, tail_step)
            dve.wait_ge(main.added, (E + 1) * KT)
            for f in range(KT):
                v.tensor_scalar(n3T[:, f, :], hTv[:, f, :], vec(2 * KT + f), None, ALU.mult).then_inc(h2_ready, 1)
            dve.wait_ge(rms_done, 1)
            v.tensor_scalar(rb, bank[4][:, 0:T], 1.0 / D, EPS, ALU.mult, ALU.add).then_inc(rms_sum, 1)
            dve.wait_ge(rms_root, 1)
            link(v.reciprocal(rb, rb))

            def third(f):
                g = gt[f % 3]
                dve.wait_ge(gate_act, f + 1)
                dve.wait_ge(pw_ready, KT)
                link(v.tensor_tensor(g, g, pwT[:, f, :], ALU.mult))
                v.tensor_tensor(hTv[:, f, :], hTv[:, f, :], g, ALU.add).then_inc(h3_sum, 1)
                dve.wait_ge(h3_sum, f + 1)
                v.tensor_scalar(y3T[:, f, :], hTv[:, f, :], vec(3 * KT + f), None, ALU.mult).then_inc(h3_ready, 1)

            for f in range(KT):
                dve.wait_ge(gate_done, f + 1)
                v.tensor_tensor(gt[f % 3], bank[f % 4][:, 0:T], rb, ALU.mult).then_inc(gate_pre, 1)
                if f > 0:
                    third(f - 1)
            third(KT - 1)
            dve.wait_ge(y_stat, 1)
            for b, rows, _ in BLOCKS:
                ins = v.tensor_scalar(yss[0:rows, b:b + 1], bank[5][0:rows, b:b + 1], 1.0 / D, EPS, ALU.mult, ALU.add)
            ins.then_inc(y_sum, 1)
            dve.wait_ge(y_root, 1)
            for b, rows, _ in BLOCKS:
                ins = v.reciprocal(yss[0:rows, b:b + 1], yss[0:rows, b:b + 1])
            ins.then_inc(y_scale, 1)
            dve.wait_ge(y_scale, 1)
            for b, rows, _ in BLOCKS:
                dve.wait_ge(yrow_done, 2 * b + 1)
                v.tensor_scalar(x2[0:rows, b, 0:512], bank[2 * b % 4][0:rows, :], yss[0:rows, b:b + 1], None, ALU.mult)\
                    .then_inc(yrow_ready["vector"], 1)

        @block.scalar
        def _(act):
            a = nc.scalar.activation
            link = chained(act, act_step)

            for i, (x, n) in enumerate(((norm1_g[0], KT), (norm2_g[0], KT), (norm3_g[0], KT), (final_g, KT),
                                        (b_gk[0], H), (gla_norm_g[0], DV // P))):
                if i == 0:
                    act.wait_ge(pool_step, 1)
                r0 = [0, KT, 2 * KT, 3 * KT, 4 * KT, 4 * KT + H][i]
                act.dma_start(vrows[r0:r0 + n, :], x.rearrange("(k p) -> k p", p=P)).then_inc(ld_vec, 16)
            act.dma_start(wgk, w_in[0][:, CGK:CGK + RANK].rearrange("(k p) n -> p k n", p=P)).then_inc(ld_gk, 16)
            act.dma_start(wgk2[0:RANK, :], w_gk2[0]).then_inc(ld_gk, 16)
            for b, rows, _ in BLOCKS:
                act.wait_ge(ld_x[b], 16)
                if b > 0:
                    act.wait_ge(x_squares, b)
                a(junk[0:rows, :], x_tok[0:rows, b, :], ACT.Square, accum_out=xss[0:rows, b:b + 1])\
                    .then_inc(x_squares, 1)
            act.wait_ge(x_scale_sum, 1)
            for b, rows, _ in BLOCKS:
                ins = a(xrs[0:rows, b:b + 1], xrs[0:rows, b:b + 1], ACT.Sqrt)
            ins.then_inc(x_root, 1)
            act.dma_start(w00[:, :], w_sp[0, :, 0, 0].unsqueeze(0).to_broadcast([NS, MH]),
                          allow_slow_non_contiguous=True).then_inc(ld_wsp, 16)
            act.dma_start(wsp, w_sp[0].rearrange("h t s -> t h s")).then_inc(ld_wsp, 16)
            for b, rows, t0 in BLOCKS:
                src = p_prompt[0, 0, t0:t0 + rows, :] if b < NB else p_sample[0, :, 0, :]
                act.dma_start(p_tok[0:rows, b, :], src).then_inc(ld_p, 16)
            for m, x in enumerate((b_gate, b_up)):
                act.dma_start(bias_rows[0:E, m, :], x[0]).then_inc(ld_bias, 16)
            act.dma_start(vngrow, v_norm_g.to_broadcast([P, D])).then_inc(ld_rows, 16)
            act.dma_start(vnbrow, v_norm_b.to_broadcast([P, D])).then_inc(ld_rows, 16)
            act.dma_start(bspT[:, :, 0:P], b_sp.to_broadcast([P, MH, P])).then_inc(ld_rows, 16)
            act.dma_start(g2row[:, :], norm2_g.to_broadcast([P, D])).then_inc(ld_router, 16)
            act.dma_start(brrow[:, :], b_router.to_broadcast([P, E])).then_inc(ld_router, 16)
            act.dma_start(wrtv, w_router[0].rearrange("(k p) n -> p k n", p=P)).then_inc(ld_router, 16)

            def z_out(kind, f):
                tile = (kind, f)
                p, free = zbank(tile)[:, 0:T], z_free["scalar"]
                act.wait_ge(z_done, zcount(tile))
                if kind in ("k", "q"):
                    a((kT if kind == "k" else qT)[:, f, :], p, ACT.Copy).then_inc(free, 1)
                elif kind == "v":
                    if f >= 2:
                        act.wait_ge(misc_done, mcount(("vT", f - 2)))
                    a(t[f % 2], p, ACT.Copy).then_inc(free, 1)
                elif kind == "vg":
                    if f >= 2:
                        act.wait_ge(misc_done, mcount(("vgT", f - 2)))
                    a(t[2 + f % 2], p, ACT.Gelu).then_inc(free, 1)
                elif kind in ("u", "gb"):
                    if f >= 2:
                        act.wait_ge(b_done, f - 1)
                    else:
                        act.wait_ge(misc_done, mcount(("vT" if kind == "u" else "vgT", KT - 1)))
                    if kind == "u":
                        a(t[f % 2], p, ACT.Gelu).then_inc(free, 1)
                    else:
                        a(t[2 + f % 2], p, ACT.Sigmoid).then_inc(free, 1)
                elif kind in ("r", "ga"):
                    if f >= 2:
                        act.wait_ge(a_done, f - 1)
                    else:
                        act.wait_ge(b_done, KT - 1 + f)
                    if kind == "r":
                        a(t[f % 2], p, ACT.Sigmoid).then_inc(r_sig, 1)
                    else:
                        a(t[2 + f % 2], p, ACT.Sigmoid).then_inc(free, 1)

            def mask_keys(b):
                a(kmask[0:NS, b % 2, :], kd_tok[0:NS, NB, :], ACT.Copy, scale=ident[0:NS, b:b + 1])\
                    .then_inc(kmask_ready, 1)

            def misc_out(x):
                kind, *at = x if isinstance(x, tuple) else (x,)
                p, free = mbank(x), misc_free["scalar"]
                act.wait_ge(misc_done, mcount(x))
                f = at[0] if at else None
                if kind == "gk":
                    a(gkT[0:RANK, :], p[0:RANK, 0:T], ACT.Copy).then_inc(free, 1)
                elif kind == "xT":
                    a(hTv[:, f, :], p[:, 0:T], ACT.Copy).then_inc(free, 1)
                elif kind == "pT":
                    a(pTv[:, f, :], p[:, 0:T], ACT.Copy).then_inc(free, 1)
                elif kind == "kdT":
                    rows = BLOCKS[f][1]
                    a(kd_tok[0:rows, f, :], p[0:rows, :], ACT.Copy).then_inc(free, 1)
                    if f == NB:
                        act.wait_ge(*freed(mby, misc_free, mpos[x]))
                        mask_keys(0)
                        mask_keys(1)
                elif kind == "o":
                    b, i = at
                    a(o_tok[:, b, i * 512:(i + 1) * 512], p[:, :], ACT.Copy).then_inc(free, 1)
                    act.wait_ge(*freed(mby, misc_free, mpos[x]))
                    for h in (2 * i, 2 * i + 1):
                        a(ojunk[h % 2], o_tok[:, b, h * DV:(h + 1) * DV], ACT.Square,
                          accum_out=oss[:, b * H + h:b * H + h + 1]).then_inc(o_squares, 1)
                    act.wait_ge(o_squares, 2 * (2 * b + i + 1))
                elif kind == "so":
                    a(oST[:, :, f], p[:, 0:2 * H], ACT.Copy).then_inc(free, 1)
                    if f + 2 < NS:
                        mask_keys(f + 2)
                elif kind == "soT":
                    a(o_tok[0:NS, NB, f * 512:(f + 1) * 512], p[0:NS, :], ACT.Copy).then_inc(free, 1)
                    if f == 1:
                        act.wait_ge(*freed(mby, misc_free, mpos[x]))
                        for h in range(H):
                            ins = a(ojunk[h][0:NS, :], o_tok[0:NS, NB, h * DV:(h + 1) * DV], ACT.Square,
                                    accum_out=oss[0:NS, NB * H + h:NB * H + h + 1])
                        ins.then_inc(o_squares, 1)
                        act.wait_ge(o_sum, 2)
                        a(ors[0:NS, NB * H:], ors[0:NS, NB * H:], ACT.Sqrt).then_inc(o_root, 1)

            for x in plan:
                if x[0] == "z":
                    if zby[zpos[x[1:]]] == "scalar" or x[1] == "r":
                        z_out(*x[1:])
                elif mby[mpos[x]] == "scalar":
                    misc_out(x)
                if x == ("z", "q", 0):
                    act.wait_ge(abs_ready, 1)
                    link(a(e1, e1, ACT.Exp, scale=-1.0))
                    a(e1, e1, ACT.Ln, bias=1.0).then_inc(la_ready, 1)
                if x == ("z", "v", 0):
                    act.wait_ge(cum_ready, 1)
                    a(e1, bT, ACT.Exp, scale=1.0 / GATE_NORMALIZER).then_inc(decays_ready, 1)
                    a(keT[:, :, 0:L], bT[:, :, 0:L], ACT.Exp, scale=-1.0 / GATE_NORMALIZER).then_inc(decays_ready, 1)
                    act.wait_ge(back_ready, 1)
                    a(kdT[:, :, 0:L], kdT[:, :, 0:L], ACT.Exp, scale=1.0 / GATE_NORMALIZER).then_inc(decays_ready, 1)
                if x == ("z", "u", 0):
                    act.wait_ge(vn_var, 1)
                    for b, rows, _ in BLOCKS:
                        ins = a(vrs[0:rows, b:b + 1], vrs[0:rows, b:b + 1], ACT.Sqrt)
                    ins.then_inc(vn_root, 1)
                    act.wait_ge(o_sum, 1)
                    a(ors[:, 0:NB * H], ors[:, 0:NB * H], ACT.Sqrt).then_inc(o_root, 1)

            def pw_out(f):
                act.wait_ge(pw_done, f + 1)
                a(pwT[:, f, :], bank[0][:, 0:T], ACT.Copy).then_inc(pw_ready, 1)

            for b, rows, _ in BLOCKS:
                for i in range(2):
                    act.wait_ge(hrow_done, 2 * b + i + 1)
                    if b > 0:
                        act.wait_ge(h_squares, 2 * b + i - 1)
                    a(hjunk[(2 * b + i) % 2][0:rows, :], bank[2 + 2 * b + i][0:rows, :], ACT.Square,
                      accum_out=hss[0:rows, 2 * b + i:2 * b + i + 1]).then_inc(h_squares, 1)
            act.wait_ge(h_sum, 1)
            for b, rows, _ in BLOCKS:
                ins = a(hrs[0:rows, b:b + 1], hrs[0:rows, b:b + 1], ACT.Sqrt)
            ins.then_inc(h_root, 1)
            act.wait_ge(hrs_ready, 1)
            for b in range(NB):
                for i in range(2):
                    ins = a(x2[:, b, i * 512:(i + 1) * 512], bank[2 + 2 * b + i][:, :], ACT.Copy, scale=hrs[:, b:b + 1])
                ins.then_inc(x2_scaled, 1)
            pw_out(0)
            for b, rows, _ in BLOCKS:
                act.wait_ge(top_ready, b + 1)
                a(ew[0:rows, b, :], m8[0:rows, b, 0:TOP_K], ACT.Exp, bias=negm[0:rows, b:b + 1],
                  accum_out=esum[0:rows, b:b + 1]).then_inc(top_exp, 1)
            for f in range(1, KT):
                pw_out(f)

            def gathered_out(ps, item, parity, width=0):
                act.wait_ge(ps.gathered, item + 1)
                if width:
                    for i in range(2):
                        a(xe[:, i * HALF:(i + 1) * HALF, 0:width],
                          bank[6 + i][:, 0:HALF * width].rearrange("p (f c) -> p f c", f=HALF), ACT.Copy)
                a(SWT[parity], bank[1][:, 0:T], ACT.Copy).then_inc(ps.xe_ready, 1)

            def rows_out(ps, item, chunks, b):
                base = PER_EXPERT if ps is extra else 0
                act.wait_ge(ps.used, item * PER_EXPERT + (chunks + base))
                a(rows_sb[:, 0:512], bank[b][:, :], ACT.Copy).then_inc(ps.rows_scalar, 1)

            def sigmoid(ps, item):
                act.wait_ge(ps.g_ready, item + 1)
                a(sg, gs, ACT.Sigmoid, scale=ALPHA).then_inc(ps.sig_ready, 1)

            def y_out(ps, item):
                base = PER_EXPERT if ps is extra else 0
                act.wait_ge(ps.used, item * PER_EXPERT + (PER_EXPERT + base))
                for i in range(2):
                    ins = a(y_rows[:, i * 512:(i + 1) * 512], bank[4 + i][:, :], ACT.Copy)
                ins.then_inc(ps.y_ready, 1)

            act.wait_ge(wT_done, 1)
            link(a(SWT[1][0:E, :], bank[0][0:E, 0:T], ACT.Copy))
            act.wait_ge(ld_bdown, 16)
            act.sem_inc(main.y_ready, 1)
            gathered_out(main, 0, 0, P)
            with act.Fori(0, ROUNDS) as i:
                for u in range(UNROLL):
                    j = i * UNROLL + u
                    rows_out(main, j, 4, 0)
                    sigmoid(main, j)
                    rows_out(main, j, 8, 2)
                    gathered_out(main, j + 1, (u + 1) % 2, P if u % 2 else 0)
                    y_out(main, j)

            act.wait_ge(table_ready, 1)
            n_extra = act.value_load(ov_table_i[0:1, 2 * MAX_OV:2 * MAX_OV + 1], min_val=0, max_val=MAX_OV)
            with act.If(n_extra > 0):
                with act.Fori(0, n_extra) as i:
                    gathered_out(extra, i, 0, CAP)
                    rows_out(extra, i, 4, 0)
                    sigmoid(extra, i)
                    rows_out(extra, i, 8, 2)
                    y_out(extra, i)

            for f in range(KT):
                act.wait_ge(h2_ready, f + 1)
                a(sqT[:, f, :], hTv[:, f, :], ACT.Square).then_inc(sq_ready, 1)
            act.wait_ge(rms_sum, 1)
            a(rb, rb, ACT.Sqrt).then_inc(rms_root, 1)

            def gate_sigmoid(f):
                act.wait_ge(gate_pre, f + 1)
                a(gt[f % 3], gt[f % 3], ACT.Sigmoid).then_inc(gate_act, 1)

            for f in range(KT):
                gate_sigmoid(f)
                if f > 0:
                    act.wait_ge(h3_sum, f)
                    a(sqT[:, f - 1, :], hTv[:, f - 1, :], ACT.Square).then_inc(ysq_ready, 1)
            act.wait_ge(h3_sum, KT)
            a(sqT[:, KT - 1, :], hTv[:, KT - 1, :], ACT.Square).then_inc(ysq_ready, 1)
            act.wait_ge(y_sum, 1)
            for b, rows, _ in BLOCKS:
                ins = a(yss[0:rows, b:b + 1], yss[0:rows, b:b + 1], ACT.Sqrt)
            ins.then_inc(y_root, 1)
            act.wait_ge(y_scale, 1)
            for b, rows, _ in BLOCKS:
                act.wait_ge(yrow_done, 2 * b + 2)
                a(x2[0:rows, b, 512:1024], bank[(2 * b + 1) % 4][0:rows, :], ACT.Copy, scale=yss[0:rows, b:b + 1])\
                    .then_inc(yrow_ready["scalar"], 1)


_INS = ["x_prompt", "x_sample", "state_gla", "p_prompt", "p_sample", "norm1_g", "w_in", "w_gk2", "b_gk", "gla_norm_g",
        "v_norm_g", "v_norm_b", "w_sp", "b_sp", "w_o", "norm2_g", "w_router", "b_router", "w_gate", "b_gate", "w_up",
        "b_up", "w_down", "b_down", "norm3_g", "w_ple_gate", "w_ple_proj", "final_g"]
_OUTS = [(1, 256, 1024), (8, 1, 1024), (1, 1, 4, 128, 256), (1, 8, 4, 128, 256), (1, 8, 1, 1024)]


def kernel(**inputs):
    import numpy as _np
    import concourse.bacc as _bacc
    from concourse import mybir as _mybir
    from concourse.bass_utils import run_bass_kernel_spmd as _run

    nc = _bacc.Bacc("TRN2", target_bir_lowering=False, num_devices=1)
    arrays, args = {}, []
    for name in _INS:
        a = _np.ascontiguousarray(inputs[name])
        arrays[f"in_{name}_dram"] = a
        args.append(nc.dram_tensor(f"in_{name}_dram", a.shape, _mybir.dt.from_np(a.dtype), kind="ExternalInput").ap())
    for i, shape in enumerate(_OUTS):
        args.append(nc.dram_tensor(f"out_{i}_dram", shape, _mybir.dt.float32, kind="ExternalOutput").ap())
    hybrid_step(nc, *args)
    r = _run(nc, [arrays], core_ids=[0])
    return tuple(r.results[0][f"out_{i}_dram"] for i in range(len(_OUTS)))
```

```python
from contextlib import ExitStack

import numpy as np

import concourse.bass as bass
from concourse import mybir

F32 = mybir.dt.float32
I32 = mybir.dt.int32
U32 = mybir.dt.uint32
ALU = mybir.AluOpType
ACT = mybir.ActivationFunctionType
AX = mybir.AxisListType

P = 128
EPS = 1e-6
GLA_CHUNK = 64
TOP_K = 4
LIMIT, ALPHA = 7.0, 1.702
CAP = P // 2
GATE_NORMALIZER = 16.0

SLOT = 2048
SLOTS = 16
FRONT_SLOTS = 6
LATE_SLOTS = 2
PER_EXPERT = 12
UNROLL = 4
EXTRA_SLOT = 4


def hybrid_step(nc, x_prompt, x_sample, state_gla, p_prompt, p_sample, norm1_g, w_in, w_gk2, b_gk, gla_norm_g,
                v_norm_g, v_norm_b, w_sp, b_sp, w_o, norm2_g, w_router, b_router, w_gate, b_gate, w_up, b_up,
                w_down, b_down, norm3_g, w_ple_gate, w_ple_proj, final_g,
                y_prompt, y_sample, st_prompt, st_sample, mix_v_sample):
    L, D = x_prompt.shape[1:]
    NS = x_sample.shape[0]
    T = L + NS
    NB = L // P
    KT = D // P
    H, DK, DV = state_gla.shape[2:]
    RANK = w_gk2.shape[1]
    E = w_gate.shape[1]
    MH = w_sp.shape[1]
    DP = p_prompt.shape[3]
    PK = DP // P
    NCH = L // GLA_CHUNK
    HALF = KT // 2
    MAX_OV = T * TOP_K // CAP + 1
    LEVELS = (T - 1) // CAP
    ROUNDS = E // UNROLL
    BLOCKS = [(b, P, b * P) for b in range(NB)] + [(NB, NS, L)]

    CQ, CK, CV, CR = 0, H * DK, 2 * H * DK, 2 * H * DK + H * DV
    CGK = CR + H * DV
    CU, CVG, CGA, CGB = CGK + RANK, CGK + RANK + D, CGK + RANK + 2 * D, CGK + RANK + 3 * D

    def in_turn(a, b):
        return [(k, f) for c in range(0, KT, 2) for k in (a, b) for f in (c, c + 1)]

    ztiles = [("k", f) for f in range(H)] + [("q", f) for f in range(H)] + [("v", f) for f in range(KT)] + \
        [("vg", f) for f in range(KT)] + in_turn("u", "gb") + in_turn("r", "ga") + [("wo", f) for f in range(KT)]
    zcol = {"k": CK, "q": CQ, "v": CV, "vg": CVG, "u": CU, "gb": CGB, "r": CR, "ga": CGA, "wo": 0}
    zpos = {tile: n for n, tile in enumerate(ztiles)}
    NFRONT = len(ztiles) // 2
    ZBANKS = 3
    SO_BANK = 3
    MBANK, MBANKS = 4, 4
    zby = ["vector" if kind in ("r", "wo") else "scalar" for kind, _ in ztiles]

    def z(kind, *fs):
        return [("z", kind, f) for f in fs]

    plan = [("xT", f) for f in range(KT)] + ["vec"] + [("nT", f) for f in range(KT)] + ["gk"] + \
        z("k", *range(H)) + [("la", h) for h in range(H)] + \
        z("q", *range(H)) + [("bias", 0), ("bias", 1)] + \
        [("pT", k) for k in range(PK)] + ["wsp"] + z("v", 0)
    for f in range(1, KT):
        plan += z("v", f) + [("vT", f - 1)]
    between = [[("kdT", 0), ("kdT", 1), ("kdT", 2)], [("att", 0), ("att", 1)]] + \
        [[("dS", c, 0), ("dS", c, 1)] for c in range(NCH)] + [[("o", b, 0), ("o", b, 1)] for b in range(NB)]
    for f in range(KT):
        plan += z("vg", f) + [("vT", KT - 1) if f == 0 else ("vgT", f - 1)] + between[f]
    for c in range(0, KT, 2):
        plan += z("u", c) + ([("vgT", KT - 1)] if c == 0 else []) + [("kv", c, 0), ("kv", c, 1)] + z("u", c + 1) + \
            [("kv", c + 1, 0), ("kv", c + 1, 1), ("so", c)] + z("gb", c) + [("so", c + 1)] + z("gb", c + 1) + \
            [("mix", c), ("mix", c + 1)]
    for c in range(0, KT, 2):
        plan += z("r", c, c + 1) + z("ga", c, c + 1) + [("oT", c), ("oT", c + 1)]
    plan += z("wo", *range(KT))
    assert [x[1:] for x in plan if x[0] == "z"] == ztiles

    misc = [x for x in plan if x[0] not in ("z", "so")]
    mpos = {x: n for n, x in enumerate(misc)}
    mby = ["scalar" if x[0] in ("gk", "pT", "kdT", "o") or x == "gk" else "vector" for x in misc]

    ctx = ExitStack()
    with ctx:
        def sb(name, shape, dt=F32):
            return ctx.enter_context(nc.sbuf_tensor(name, shape, dt))

        def sem(name):
            return ctx.enter_context(nc.semaphore(name))

        bank = [ctx.enter_context(nc.psum_tensor(f"bank{i}", [P, 512], F32)) for i in range(8)]

        def view(tensor, at, *shape):
            n = int(np.prod(shape))
            v = tensor[:, at:at + n]
            if len(shape) == 1:
                return v
            names = "abcd"[:len(shape)]
            return v.rearrange("p (%s) -> p %s" % (" ".join(names), " ".join(names)),
                               **dict(zip(names[1:], shape[1:])))

        ring = sb("ring", [P, SLOTS * SLOT])
        hT = sb("hT", [P, KT * T])
        ident = sb("ident", [P, P])
        ones = sb("ones", [P, P])
        two_eyes = sb("two_eyes", [P, CAP])
        before = sb("before", [P, P])
        upto = sb("upto", [P, P])
        vecT = sb("vecT", [P, 40])
        biasT = sb("biasT", [P, 2 * KT * E])
        iota_c = sb("iota_c", [P, P])
        iota_e = sb("iota_e", [P, E])
        rank = sb("rank", [P, (NB + 1) * (E + 2)])
        wts = sb("wts", [P, (NB + 1) * (E + 2)])
        small = sb("small", [P, 128])
        ov_table = sb("ov_table", [P, 2 * MAX_OV + 1])
        ov_table_i = sb("ov_table_i", [P, 2 * MAX_OV + 1], I32)
        wrt = sb("wrt", [P, KT * E])
        brrow = sb("brrow", [P, E])
        pT = sb("pT", [P, PK * T])
        g2row = sb("g2row", [P, D])
        regA = sb("regA", [P, KT * T])
        regB = sb("regB", [P, (NB + 1) * D])
        regC = sb("regC", [P, (NB + 1) * D])
        regD = sb("regD", [P, KT * T])
        regE = sb("regE", [P, max(2 * D + H * T, (KT + 2) * T + MAX_OV * E)])
        w00 = sb("w00", [NS, MH])
        dw = sb("dw", [NS, MH * NS])
        rk = sb("rk", [P, NB + 1])

        hTv = view(hT, 0, KT, T)
        slot = [view(ring, s * SLOT, SLOT) for s in range(SLOTS)]
        by_k = [s.rearrange("p (k f) -> p k f", k=2) for s in slot]
        by_col = [s.rearrange("p (k f) -> p k f", k=KT) for s in slot]
        biasv = view(biasT, 0, 2, KT, E)
        rankv, wtsv = view(rank, 0, NB + 1, E + 2), view(wts, 0, NB + 1, E + 2)
        wrtv, pTv = view(wrt, 0, KT, E), view(pT, 0, PK, T)

        place = [FRONT_SLOTS * SLOT, (SLOTS - LATE_SLOTS) * SLOT]

        def front_buffer(*shape, late=False):
            at = place[late]
            place[late] += int(np.prod(shape))
            assert place[late] <= (SLOTS - LATE_SLOTS + late * LATE_SLOTS) * SLOT
            return view(ring, at, *shape)

        x_tok = front_buffer(NB + 1, D)
        S_ver = view(ring, FRONT_SLOTS * SLOT, NCH - 1, H * DV)
        S_last = front_buffer(H * DV)
        at_b = place[0]
        bT = front_buffer(H, T)
        att = view(ring, at_b, NB, H, P)
        e1 = front_buffer(H, T)
        qT = front_buffer(H, T)
        kT = front_buffer(H, T)
        at_junk = place[0]
        keT = front_buffer(H, T)
        kdT = front_buffer(H, T)
        v_tok = front_buffer(NB + 1, D)
        kd_tok = front_buffer(NB + 1, H * DK)
        kmask = front_buffer(2, H * DK)
        t = [front_buffer(T, late=True) for _ in range(5)]
        WT = front_buffer(MH, P, late=True)
        st = front_buffer(2, H * DV, late=True)
        attmask = front_buffer(P, late=True)
        scanmask = t[4]

        nT = view(regA, 0, KT, T)
        bias_rows = view(regB, 0, 2, D)
        o_tok, x2 = view(regB, 0, NB, D), view(regB, 0, NB + 1, D)
        xn, vn, hgT = view(regC, 0, NB + 1, D), view(regC, 0, NB + 1, D), view(regC, 0, KT, T)
        mixT = view(regD, 0, KT, T)
        wgk, wgk2, gkT = view(regD, 0, KT, RANK), view(regD, P, H * DK), view(regD, P + H * DK, T)
        vrows, wsp = view(regD, 1024, P), view(regD, 1024 + P, MH, P)
        p_tok = view(sb("p_tok", [P, (NB + 1) * DP]), 0, NB + 1, DP)
        vngrow, vnbrow, bspT = view(regE, 0, D), view(regE, D, D), view(regE, 2 * D, H, T)
        junk = view(ring, at_junk, D)

        EC = KT * CAP
        gs, us, sg = (view(regC, i * EC, KT, CAP) for i in range(3))
        xe = view(regC, 3 * EC, KT, P)
        Ssel, Swt = view(regC, 3 * EC + KT * P, NB + 1, P), view(regA, 0, NB + 1, P)
        y_rows, rows_sb = view(regD, 0, D), view(regD, D, D)
        pwT = view(regE, 0, KT, T)
        SWT = [view(regE, KT * T + i * T, T) for i in range(2)]
        cols = [0]

        def small_tile(n):
            cols[0] += n
            assert cols[0] <= 128
            return small[:, cols[0] - n:cols[0]]

        xss, xrs = small_tile(NB + 1), small_tile(NB + 1)
        decay, sdecay = small_tile(H * NCH).rearrange("p (h c) -> p h c", h=H), \
            sb("sdecay", [P, H * NS])[:].rearrange("p (h s) -> p h s", h=H)
        oss, ors = small_tile(NB * H), small_tile(NB * H)
        so_ss, so_rs = small_tile(1), small_tile(1)
        vstat, vmv, vrs = small_tile(12 * (NB + 1)), small_tile(2 * (NB + 1)), small_tile(NB + 1)
        hss, hrs = small_tile(2 * (NB + 1)), small_tile(NB + 1)
        yss = small_tile(NB + 1)
        GROUP = P // H
        o_s = view(regB, NB * D, DV)
        onehots, q_alone = view(regB, NB * D + DV, NS, NS), view(regB, NB * D + DV + NS * NS, H, NS, NS)

        rt = [KT * T]

        def route_tile(*shape):
            rt[0] += int(np.prod(shape))
            assert rt[0] <= (NB + 1) * D
            return view(regC, rt[0] - int(np.prod(shape)), *shape)

        lg = route_tile(NB + 1, E)
        m8, ew = route_tile(NB + 1, 8), route_tile(NB + 1, TOP_K)
        idx = route_tile(NB + 1, 8)
        idx_f = route_tile(NB + 1, TOP_K)
        esum = route_tile(NB + 1)
        negm = route_tile(NB + 1)
        hit = route_tile(NB + 1, TOP_K, E)
        selm = route_tile(NB + 1, E)
        cnt, nov, nov_end = sb("cnt", [P, E])[:], sb("nov", [P, E])[:], sb("nov_end", [P, E])[:]
        ovt = view(regE, (KT + 2) * T, MAX_OV, E)

        sqT, n3T, y3T = view(regC, 0, KT, T), view(regD, 0, KT, T), view(regA, 0, KT, T)
        gt = [view(regC, (KT + i) * T, T) for i in range(3)]
        rb = view(regE, KT * T, T)

        ld_x = [sem(f"ld_x{b}") for b in range(NB + 1)]
        ld_vec, ld_gk, ld_bias, ld_p = sem("ld_vec"), sem("ld_gk"), sem("ld_bias"), sem("ld_p")
        ld_wsp, ld_rows, ld_router = sem("ld_wsp"), sem("ld_rows"), sem("ld_router")
        slot_loaded = [sem(f"slot_loaded{s}") for s in range(SLOTS)]
        st_loaded = [sem(f"st_loaded{s}") for s in range(2)]
        st_stored = [sem(f"st_stored{s}") for s in range(2)]
        sp_stored, vn_stored, y_stored = sem("sp_stored"), sem("vn_stored"), sem("y_stored")
        ident_ready, consts_ready = sem("ident_ready"), sem("consts_ready")
        pool_step, dve_step, act_step = sem("pool_step"), sem("dve_step"), sem("act_step")
        z_done, misc_done, chunk_used = sem("z_done"), sem("misc_done"), sem("chunk_used")
        z_free = {"scalar": sem("z_free_scalar"), "vector": sem("z_free_vector")}
        misc_free = {"scalar": sem("misc_free_scalar"), "vector": sem("misc_free_vector")}
        x_squares, x_scale_sum, x_root = sem("x_squares"), sem("x_scale_sum"), sem("x_root")
        xn_ready = sem("xn_ready")
        abs_ready, la_ready, cum_ready, back_ready = (
            sem(n) for n in ("abs_ready", "la_ready", "cum_ready", "back_ready"))
        decays_ready, gla_in_ready = sem("decays_ready"), sem("gla_in_ready")
        att_ready, state_ready = sem("att_ready"), sem("state_ready")
        so_done, o_s_out = sem("so_done"), sem("o_s_out")
        o_squares, o_sum, o_root, o_ready = sem("o_squares"), sem("o_sum"), sem("o_root"), sem("o_ready")
        vn_var, vn_root, vn_scaled, vn_ready = sem("vn_var"), sem("vn_root"), sem("vn_scaled"), sem("vn_ready")
        dw_ready, bsp_ready = sem("dw_ready"), sem("bsp_ready")
        kmask_ready, st_ready = sem("kmask_ready"), sem("st_ready")
        b_done, a_done = sem("b_done"), sem("a_done")
        r_sig = sem("r_sig")
        h_ready, hg_ready = sem("h_ready"), sem("hg_ready")
        hrow_done, router_done = sem("hrow_done"), sem("router_done")
        h_squares, h_sum, h_root, hrs_ready = sem("h_squares"), sem("h_sum"), sem("h_root"), sem("hrs_ready")
        top_ready, top_exp, sel_ready, rank_done = sem("top_ready"), sem("top_exp"), sem("sel_ready"), sem("rank_done")
        zeros_ready, x2_ready, table_ready = sem("zeros_ready"), sem("x2_ready"), sem("table_ready")
        pw_done, pw_ready = sem("pw_done"), sem("pw_ready")
        ld_bdown, wT_done, wts_ready, x2_scaled = sem("ld_bdown"), sem("wT_done"), sem("wts_ready"), sem("x2_scaled")
        h2_ready, sq_ready, rms_done, rms_sum, rms_root = (
            sem(n) for n in ("h2_ready", "sq_ready", "rms_done", "rms_sum", "rms_root"))
        gate_done, gate_pre, gate_act, h3_ready = (
            sem(n) for n in ("gate_done", "gate_pre", "gate_act", "h3_ready"))
        ysq_ready, y_stat, y_sum, y_root, yrow_done = (
            sem(n) for n in ("ysq_ready", "y_stat", "y_sum", "y_root", "yrow_done"))
        yrow_ready = {"vector": sem("yrow_ready_vector"), "scalar": sem("yrow_ready_scalar")}
        h3_sum, y_scale = sem("h3_sum"), sem("y_scale")
        sq_added, ysq_added = sem("sq_added"), sem("ysq_added")
        ojunk, hjunk = [kT[:, h, 0:DV] for h in range(H)], [rows_sb[:, i * 512:(i + 1) * 512] for i in range(2)]
        tail_step = sem("tail_step")

        class Pass:
            def __init__(self, kind):
                self.selected = sem(f"{kind}_selected")
                self.gathered = sem(f"{kind}_gathered")
                self.xe_ready = sem(f"{kind}_xe_ready")
                self.rows_scalar = sem(f"{kind}_rows_scalar")
                self.rows_vector = sem(f"{kind}_rows_vector")
                self.turned = sem(f"{kind}_turned")
                self.g_ready = sem(f"{kind}_g_ready")
                self.sig_ready = sem(f"{kind}_sig_ready")
                self.mid_ready = sem(f"{kind}_mid_ready")
                self.handed_on = sem(f"{kind}_handed_on")
                self.y_ready = sem(f"{kind}_y_ready")
                self.scattered = sem(f"{kind}_scattered")
                self.added = sem(f"{kind}_added")
                self.vector_step = sem(f"{kind}_vector_step")

        main, extra = Pass("main"), Pass("extra")
        main.used, extra.used = chunk_used, sem("extra_used")
        extra_loaded = [sem(f"extra_loaded{s}") for s in range(PER_EXPERT)]

        def freed(by, free, n):
            return free[by[n]], by[:n + 1].count(by[n])

        def zcount(tile):
            return zpos[tile] + 1

        def mcount(x):
            return mpos[x] + 1

        def zbank(tile):
            return bank[zpos[tile] % ZBANKS]

        def mbank(x):
            return bank[MBANK + mpos[x] % MBANKS]

        FRONT_LOADS = [len(range(s, NFRONT + 1, FRONT_SLOTS)) for s in range(FRONT_SLOTS)] + [0] * (SLOTS - FRONT_SLOTS)

        def expert_loads(m):
            return 16 * (FRONT_LOADS[m % SLOTS] + m // SLOTS + 1)

        RANKS = (NB + 1) * E
        SELECTED = (2, 1)
        PW_EARLY = 3
        SCATTER = (4, 5, 6, 7, 2, 3, 6, 7)
        LAST = E * PER_EXPERT
        K3 = [(w_gate, "gate"), (w_up, "up"), (w_down, "down")]

        def chunk_source(e, c):
            w = K3[c // 4][0]
            return w[0, e, (c % 4) * 2 * P:(c % 4 + 1) * 2 * P, :].rearrange("(k p) f -> p k f", p=P)

        def chained(eng, s, base=0):
            n = [0]

            def link(ins):
                ins.then_inc(s, 1)
                n[0] += 1
                eng.wait_ge(s, base + n[0])
            link.count = n
            return link

        def load_vectors(eng, which):
            vectors = ((norm1_g[0], KT), (norm2_g[0], KT), (norm3_g[0], KT), (final_g, KT), (b_gk[0], H),
                       (gla_norm_g[0], DV // P))
            for i in which:
                x, n = vectors[i]
                r0 = sum(m for _, m in vectors[:i])
                eng.dma_start(vrows[r0:r0 + n, :], x.rearrange("(k p) -> k p", p=P)).then_inc(ld_vec, 16)

        block = ctx.enter_context(nc.Block())

        @block.sync
        def _(sp):
            for b, rows, t0 in BLOCKS:
                src = x_prompt[0, t0:t0 + rows, :] if b < NB else x_sample[:, 0, :]
                sp.dma_start(x_tok[0:rows, b, :], src).then_inc(ld_x[b], 16)
            sp.dma_start(wgk, w_in[0][:, CGK:CGK + RANK].rearrange("(k p) n -> p k n", p=P)).then_inc(ld_gk, 16)
            sp.dma_start(wgk2[0:RANK, :], w_gk2[0]).then_inc(ld_gk, 16)
            sp.wait_ge(pool_step, 1)
            load_vectors(sp, range(0, 3))
            sp.wait_ge(ld_vec, 16 * 6)
            sp.wait_ge(ld_gk, 32)
            def load(m):
                sp.dma_start(by_k[m % SLOTS], chunk_source(m // PER_EXPERT, m % PER_EXPERT))\
                    .then_inc(slot_loaded[m % SLOTS], 16)

            EARLY = zpos[("r", 0)] // 2 + FRONT_SLOTS
            for n in range(NFRONT):
                kind, f = ztiles[2 * n]
                if n >= FRONT_SLOTS:
                    sp.wait_ge(z_done, 2 * (n - FRONT_SLOTS + 1))
                w = w_o[0] if kind == "wo" else w_in[0]
                c0 = zcol[kind] + f * P
                sp.dma_start(by_col[n % FRONT_SLOTS], w[:, c0:c0 + 2 * P].rearrange("(k p) f -> p k f", p=P))\
                    .then_inc(slot_loaded[n % FRONT_SLOTS], 16)
                if n == EARLY:
                    sp.wait_ge(so_done, NS)
                    sp.wait_ge(sp_stored, 16)
                    sp.wait_ge(o_ready, 2)
                if EARLY <= n < EARLY + 4:
                    load(FRONT_SLOTS + 2 * (n - EARLY))
                    load(FRONT_SLOTS + 2 * (n - EARLY) + 1)

            sp.wait_ge(z_done, 2 * (NFRONT - FRONT_SLOTS + 1))
            sp.dma_start(by_k[NFRONT % FRONT_SLOTS], w_ple_proj[0].rearrange("(k p) f -> p k f", p=P))\
                .then_inc(slot_loaded[NFRONT % FRONT_SLOTS], 16)

            sp.wait_ge(a_done, KT)
            sp.wait_ge(st_stored[0], 16 * NS // 2)
            sp.wait_ge(st_stored[1], 16 * NS // 2)
            for m in range(SLOTS - LATE_SLOTS, SLOTS):
                load(m)
            for n in range(NFRONT - FRONT_SLOTS + 1, NFRONT):
                sp.wait_ge(z_done, 2 * (n + 1))
                load(n % FRONT_SLOTS)
            sp.wait_ge(pw_done, KT)
            load(NFRONT % FRONT_SLOTS)
            TURN = UNROLL * PER_EXPERT
            with sp.Fori(0, ROUNDS - 1) as i:
                for r in range(SLOTS, SLOTS + TURN):
                    sp.wait_ge(chunk_used, i * TURN + (r - SLOTS + 1))
                    sp.dma_start(by_k[r % SLOTS], chunk_source(i * UNROLL + r // PER_EXPERT, r % PER_EXPERT))\
                        .then_inc(slot_loaded[r % SLOTS], 16)
            for m in range(SLOTS + TURN * (ROUNDS - 1), LAST):
                sp.wait_ge(chunk_used, m - SLOTS + 1)
                load(m)

            sp.wait_ge(table_ready, 1)
            n_extra = sp.value_load(ov_table_i[0:1, 2 * MAX_OV:2 * MAX_OV + 1], min_val=0, max_val=MAX_OV)
            with sp.If(n_extra > 0):
                with sp.Fori(0, n_extra) as i:
                    e = sp.value_load(ov_table_i[0:1, bass.ds(i, 1)], min_val=0, max_val=E - 1)
                    for c in range(PER_EXPERT):
                        s = EXTRA_SLOT + c
                        sp.wait_ge(chunk_used, LAST - SLOTS + s + 1)
                        sp.wait_ge(extra.used, i * PER_EXPERT + (c + 1))
                        sp.dma_start(by_k[s], chunk_source(e, c)).then_inc(extra_loaded[c], 16)

            for m in range(LAST, LAST + KT // 2):
                sp.wait_ge(chunk_used, m - SLOTS + 1)
                sp.dma_start(by_col[m % SLOTS], w_ple_gate[0, :, (m - LAST) * 2 * P:(m - LAST + 1) * 2 * P]
                             .rearrange("(k p) f -> p k f", p=P)).then_inc(slot_loaded[m % SLOTS], 16)

            for b, rows, t0 in BLOCKS:
                sp.wait_ge(yrow_ready["vector"], b + 1)
                sp.wait_ge(yrow_ready["scalar"], b + 1)
                dst = y_prompt[0, t0:t0 + rows, :] if b < NB else y_sample[:, 0, :]
                sp.dma_start(dst, x2[0:rows, b, :]).then_inc(y_stored, 16)
            sp.wait_ge(y_stored, 16 * len(BLOCKS))

        @block.gpsimd
        def _(pool):
            link = chained(pool, pool_step)
            pool.memset(ident[:, :], 0.0)
            pool.memset(before[:, :], 1.0)
            pool.memset(upto[:, :], 1.0)
            pool.memset(ones[:, :], 1.0)
            pool.memset(scanmask, 1.0)
            link(pool.memset(vrows, 0.0))
            pool.affine_select(out=ident[:, :], in_=ident[:, :], compare_op=ALU.not_equal, fill=1.0, base=0,
                               pattern=[[-1, P]], channel_multiplier=1).then_inc(ident_ready, 1)
            pool.affine_select(out=before[:, :], in_=before[:, :], compare_op=ALU.is_gt, fill=0.0, base=0,
                               pattern=[[1, P]], channel_multiplier=-1)
            pool.affine_select(out=upto[:, :], in_=upto[:, :], compare_op=ALU.is_ge, fill=0.0, base=0,
                               pattern=[[1, P]], channel_multiplier=-1)
            pool.memset(scanmask[:, 0:L:GLA_CHUNK], 0.0)
            link(pool.memset(scanmask[:, L:T], 0.0))
            pool.tensor_tensor(two_eyes[:, :], ident[:, 0:CAP], ident[:, CAP:P], ALU.add)
            link(pool.tensor_copy(attmask, upto[:, :]))
            link(pool.memset(attmask[0:GLA_CHUNK, GLA_CHUNK:P], 0.0))
            pool.iota(iota_c[:, :], [[0, 2], [1, CAP]], base=0, channel_multiplier=0,
                      allow_small_or_imprecise_dtypes=True)
            link(pool.iota(iota_e[:, :], [[1, E]], base=0, channel_multiplier=0, allow_small_or_imprecise_dtypes=True))
            pool.memset(o_s, 0.0)
            pool.memset(rank[:, :], -1.0)
            pool.memset(wts[:, :], 0.0).then_inc(consts_ready, 1)
            pool.wait_ge(ld_rows, 16 * 3)
            link(pool.tensor_copy(bspT[:, :, P:2 * P], bspT[:, :, 0:P]))
            pool.tensor_copy(bspT[:, :, L:T], bspT[:, :, 0:1].to_broadcast([P, H, NS])).then_inc(bsp_ready, 1)
            for b in range(2):
                pool.dma_start(st[:, b, :].rearrange("p (h v) -> p h v", h=H),
                               state_gla[0, b].rearrange("h k v -> k h v")).then_inc(st_loaded[b], 16)
            for b in range(NB):
                pool.wait_ge(vn_scaled, b + 1)
                link(pool.tensor_tensor(vn[:, b, :], vn[:, b, :], vngrow, ALU.mult))
                pool.tensor_tensor(vn[:, b, :], vn[:, b, :], vnbrow, ALU.add).then_inc(vn_ready, 1)
            pool.wait_ge(vn_ready, NB + 1)
            pool.dma_start(mix_v_sample[0, :, 0, :], vn[0:NS, NB, :]).then_inc(vn_stored, 16)
            pool.wait_ge(state_ready, 2 * NCH)
            pool.dma_start(st_prompt[0, 0].rearrange("h k v -> k h v"),
                           S_last.rearrange("p (h v) -> p h v", h=H)).then_inc(sp_stored, 16)
            for b in range(NS):
                pool.wait_ge(st_ready, 2 * (b + 1))
                pool.dma_start(st_sample[0, b].rearrange("h k v -> k h v"),
                               st[:, b % 2, :].rearrange("p (h v) -> p h v", h=H)).then_inc(st_stored[b % 2], 16)
                if b + 2 < NS:
                    pool.wait_ge(st_stored[b % 2], 16 * (b // 2 + 1))
                    pool.wait_ge(so_done, b + 1)
                    pool.dma_start(st[:, b % 2, :].rearrange("p (h v) -> p h v", h=H),
                                   state_gla[0, b + 2].rearrange("h k v -> k h v")).then_inc(st_loaded[b % 2], 16)
            pool.wait_ge(misc_done, mcount(("oT", KT - 1)))
            pool.memset(x2[:, NB, :], 0.0)
            pool.wait_ge(b_done, KT)
            pool.memset(SWT[1], 0.0)
            pool.wait_ge(z_done, zcount(("wo", KT - 1)))
            pool.memset(y_rows, 0.0).then_inc(zeros_ready, 1)
            pool.wait_ge(zeros_ready, 1)
            pool.dma_start(y_rows[0:E, :], b_down[0]).then_inc(ld_bdown, 16)
            pool.wait_ge(ld_router, 48)
            for b in range(NB):
                pool.wait_ge(x2_scaled, b + 1)
                pool.tensor_tensor(x2[:, b, :], x2[:, b, :], g2row[:, :], ALU.mult).then_inc(x2_ready, 1)
            pool.wait_ge(vn_stored, 16)
            pool.wait_ge(sp_stored, 16)
            pool.wait_ge(st_stored[0], 16 * NS // 2)
            pool.wait_ge(st_stored[1], 16 * NS // 2)

        @block.tensor
        def _(pe):
            mm = nc.tensor.matmul
            turn = nc.tensor.transpose

            def z_tile(kind, f):
                n = zpos[(kind, f)]
                if n >= ZBANKS:
                    pe.wait_ge(*freed(zby, z_free, n - ZBANKS))
                chunk, half = n // 2, n % 2
                s = chunk % FRONT_SLOTS
                if half == 0:
                    pe.wait_ge(slot_loaded[s], 16 * (chunk // FRONT_SLOTS + 1))
                if (kind, f) == ("k", 0):
                    pe.wait_ge(misc_free["vector"], mby[:mcount(("nT", KT - 1))].count("vector"))
                rhs = mixT if kind == "wo" else nT
                for k in range(KT):
                    if (kind, f) == ("wo", 0):
                        pe.wait_ge(a_done, k + 1)
                    ins = mm(zbank((kind, f))[:, 0:T], by_col[s][:, k, half * P:(half + 1) * P], rhs[:, k, :],
                             start=(k == 0), stop=(k == KT - 1))
                ins.then_inc(z_done, 1)

            def misc_step(x):
                n = mpos[x]
                if n >= MBANKS:
                    pe.wait_ge(*freed(mby, misc_free, n - MBANKS))
                out = mbank(x)
                kind, *at = x if isinstance(x, tuple) else (x,)
                f = at[0] if at else None
                if kind == "vec":
                    pe.wait_ge(consts_ready, 1)
                    pe.wait_ge(ld_vec, 16 * 6)
                    ins = turn(out[:, 0:40], vrows[0:40, :], ident[0:40, 0:40])
                elif kind in ("nT", "xT"):
                    src = xn if kind == "nT" else x_tok
                    if f == 0 and kind == "nT":
                        pe.wait_ge(xn_ready, 1)
                    for b, rows, t0 in BLOCKS:
                        if f == 0 and kind == "xT":
                            pe.wait_ge(ident_ready, 1)
                            pe.wait_ge(ld_x[b], 16)
                        ins = turn(out[:, t0:t0 + rows], src[0:rows, b, f * P:(f + 1) * P], ident[0:rows, 0:rows])
                elif kind == "gk":
                    pe.wait_ge(ld_gk, 32)
                    pe.wait_ge(misc_free["vector"], mby[:mcount(("nT", KT - 1))].count("vector"))
                    for k in range(KT):
                        ins = mm(out[0:RANK, 0:T], wgk[:, k, :], nT[:, k, :], start=(k == 0), stop=(k == KT - 1))
                elif kind == "bias":
                    pe.wait_ge(ld_bias, 32)
                    for j in range(KT):
                        ins = turn(out[:, j * E:(j + 1) * E], bias_rows[0:E, f, j * P:(j + 1) * P], ident[0:E, 0:E])
                elif kind == "pT":
                    pe.wait_ge(ld_p, 48)
                    for b, rows, t0 in BLOCKS:
                        ins = turn(out[:, t0:t0 + rows], p_tok[0:rows, b, f * P:(f + 1) * P], ident[0:rows, 0:rows])
                elif kind == "wsp":
                    pe.wait_ge(ld_wsp, 32)
                    for h in range(MH):
                        ins = turn(out[:, h * P:(h + 1) * P], wsp[:, h, :], ident[:, :])
                elif kind == "la":
                    pe.wait_ge(*freed(mby, misc_free, mpos["gk"]))
                    ins = mm(out[:, 0:T], wgk2[0:RANK, f * P:(f + 1) * P], gkT[0:RANK, :], start=True, stop=True)
                elif kind in ("vT", "vgT"):
                    tile = ("v" if kind == "vT" else "vg", f)
                    pe.wait_ge(*freed(zby, z_free, zpos[tile]))
                    src = t[f % 2 + (2 if kind == "vgT" else 0)]
                    for b, rows, t0 in BLOCKS:
                        ins = turn(out[0:rows, b * P:(b + 1) * P], src[:, t0:t0 + rows], ident[:, :])
                elif kind == "kdT":
                    pe.wait_ge(gla_in_ready, 1)
                    b, rows, t0 = BLOCKS[f]
                    src = kdT if f < NB else kT
                    for h in range(H):
                        ins = turn(out[0:rows, h * DK:(h + 1) * DK], src[:, h, t0:t0 + rows], ident[:, :])
                elif kind == "att":
                    t0 = f * P
                    for h in range(H):
                        ins = mm(out[:, h * P:(h + 1) * P], keT[:, h, t0:t0 + P], qT[:, h, t0:t0 + P],
                                 start=True, stop=True)
                elif kind == "dS":
                    c, i = at
                    b, r0 = c * GLA_CHUNK // P, c * GLA_CHUNK % P
                    pe.wait_ge(*freed(mby, misc_free, mpos[("kdT", b)]))
                    pe.wait_ge(*freed(mby, misc_free, mpos[("vT", KT - 1)]))
                    for h in (2 * i, 2 * i + 1):
                        ins = mm(out[:, (h % 2) * DV:(h % 2 + 1) * DV],
                                 kd_tok[r0:r0 + GLA_CHUNK, b, h * DK:(h + 1) * DK],
                                 v_tok[r0:r0 + GLA_CHUNK, b, h * DV:(h + 1) * DV], start=True, stop=True)
                elif kind == "o":
                    b, i = at
                    pe.wait_ge(att_ready, b + 1)
                    pe.wait_ge(state_ready, 2 * min(2 * b + 1, NCH - 1))
                    for h in (2 * i, 2 * i + 1):
                        o0 = (h % 2) * DV
                        ins = mm(out[:, o0:o0 + DV], att[:, b, h, :], v_tok[:, b, h * DV:(h + 1) * DV],
                                 start=True, stop=False, skip_group_check=True)
                        for c in (2 * b, 2 * b + 1):
                            if c > 0:
                                r0, t0 = c * GLA_CHUNK % P, c * GLA_CHUNK
                                ins = mm(out[r0:r0 + GLA_CHUNK, o0:o0 + DV], qT[:, h, t0:t0 + GLA_CHUNK],
                                         S_ver[:, c - 1, h * DV:(h + 1) * DV], start=False, stop=True,
                                         skip_group_check=True)
                elif kind == "kv":
                    b, i = at
                    if i == 0:
                        pe.wait_ge(kmask_ready, b + 1)
                    for h in (2 * i, 2 * i + 1):
                        ins = mm(out[:, (h % 2) * DV:(h % 2 + 1) * DV], kmask[0:NS, b % 2, h * DK:(h + 1) * DK],
                                 v_tok[0:NS, NB, h * DV:(h + 1) * DV], start=True, stop=True)
                elif kind == "mix":
                    if f == 0:
                        pe.wait_ge(vn_ready, NB + 1)
                        pe.wait_ge(dw_ready, 1)
                    h = f * MH // KT
                    for b in range(NB):
                        mm(out[:, b * P:(b + 1) * P], vn[:, b, f * P:(f + 1) * P], WT[:, h, :], start=True, stop=True)
                    ins = mm(out[:, L:T], vn[0:NS, NB, f * P:(f + 1) * P], dw[:, h * NS:(h + 1) * NS],
                             start=True, stop=True)
                elif kind == "oT":
                    pe.wait_ge(o_ready, 2)
                    for b, rows, t0 in BLOCKS[:NB]:
                        turn(out[:, t0:t0 + rows], o_tok[0:rows, b, f * P:(f + 1) * P], ident[0:rows, 0:rows])
                    h, half = divmod(f, DV // P)
                    r = slice(GROUP * h, GROUP * h + NS)
                    ins = turn(out[:, L:T], o_s[r, half * P:(half + 1) * P], ident[r, r])
                ins.then_inc(misc_done, 1)

            def sample_o(b):
                pe.wait_ge(st_ready, 2 * (b + 1))
                for h in range(H):
                    ins = mm(bank[SO_BANK][GROUP * h:GROUP * h + NS, 0:DV], q_alone[:, h, b, :],
                             st[:, b % 2, h * DV:(h + 1) * DV], start=(b == 0), stop=(b == NS - 1),
                             skip_group_check=True)
                ins.then_inc(so_done, 1)

            for x in plan:
                if x[0] == "z":
                    z_tile(*x[1:])
                elif x[0] == "so":
                    sample_o(x[1])
                else:
                    misc_step(x)

            def pw_tile(f):
                if f == 1:
                    pe.wait_ge(x2_scaled, 1)
                if f > 1:
                    pe.wait_ge(pw_ready, f - 1)
                for k in range(PK):
                    ins = mm(bank[2 * (f % 2)][:, 0:T], by_k[s_pw][:, k, f * P:(f + 1) * P], pTv[:, k, :],
                             start=(k == 0), stop=(k == PK - 1))
                ins.then_inc(pw_done, 1)

            pe.wait_ge(h_ready, KT)
            for n in range(len(misc) - MBANKS, len(misc)):
                pe.wait_ge(*freed(mby, misc_free, n))
            for b, rows, t0 in BLOCKS:
                for i in range(2):
                    for j in range(HALF):
                        f = i * HALF + j
                        ins = turn(bank[2 + 2 * b + i][0:rows, j * P:(j + 1) * P], hTv[:, f, t0:t0 + rows], ident[:, :])
                    ins.then_inc(hrow_done, 1)
            pe.wait_ge(hg_ready, KT)
            pe.wait_ge(ld_router, 48)
            for b, rows, t0 in BLOCKS:
                for k in range(KT):
                    ins = mm(bank[1][0:rows, b * E:(b + 1) * E], hgT[:, k, t0:t0 + rows], wrtv[:, k, :],
                             start=(k == 0), stop=(k == KT - 1))
            ins.then_inc(router_done, 1)
            s_pw = NFRONT % FRONT_SLOTS
            pe.wait_ge(slot_loaded[s_pw], 16 * FRONT_LOADS[s_pw])
            for f in range(PW_EARLY):
                pw_tile(f)
            pe.wait_ge(sel_ready, 1)
            for b in range(NB + 1):
                for c in range(b + 1):
                    mm(bank[1][:, RANKS + b * E:RANKS + (b + 1) * E], (before if c == b else ones)[:, :], selm[:, c, :],
                       start=(c == 0), stop=(c == b))
            for c in range(NB + 1):
                ins = mm(bank[1][:, RANKS + (NB + 1) * E:RANKS + (NB + 2) * E], ones[:, :], selm[:, c, :],
                         start=(c == 0), stop=(c == NB))
            ins.then_inc(rank_done, 1)
            for f in range(PW_EARLY, KT):
                pw_tile(f)

            def weights_step(ps, banks, lhs, chunks):
                for s, loaded, value, k in chunks:
                    pe.wait_ge(loaded, value)
                    for n in range(2):
                        for i in range(2):
                            ins = mm(bank[banks[n]][i * CAP:(i + 1) * CAP, :], lhs[:, k + i, :],
                                     by_k[s][:, i, n * 512:(n + 1) * 512], start=(k == 0), stop=(k == KT - 2))
                    ins.then_inc(ps.used, 1)

            def turn_rows(ps, count, b):
                pe.wait_ge(ps.rows_scalar, count)
                pe.wait_ge(ps.rows_vector, count)
                for f in range(KT):
                    ins = mm(bank[b][:, f * CAP:(f + 1) * CAP], rows_sb[:, f * P:(f + 1) * P], two_eyes[:, :],
                             start=True, stop=True)
                ins.then_inc(ps.turned, 1)

            def gather(width):
                for f in range(KT):
                    for b in range(NB + 1):
                        mm(bank[6 + f // HALF][:, (f % HALF) * width:(f % HALF + 1) * width],
                           x2[:, b, f * P:(f + 1) * P], Ssel[:, b, 0:width], start=(b == 0), stop=(b == NB))

            def turn_selection(ps):
                for b, rows, t0 in BLOCKS:
                    ins = turn(bank[1][:, t0:t0 + rows], Swt[0:rows, b, :], ident[0:rows, 0:rows])
                ins.then_inc(ps.gathered, 1)

            def scatter(ps, n, parity, rows_copied=None, fs=range(KT)):
                if fs[0] == 0:
                    pe.wait_ge(ps.y_ready, n + 1)
                for f in fs:
                    if f == HALF and rows_copied is not None:
                        pe.wait_ge(ps.rows_scalar, rows_copied)
                        pe.wait_ge(ps.rows_vector, rows_copied)
                    if f >= 6:
                        pe.wait_ge(ps.added, n * KT + f - 3)
                    mm(bank[SCATTER[f]][:, 0:T], y_rows[:, f * P:(f + 1) * P], SWT[parity][:, :],
                       start=True, stop=True).then_inc(ps.scattered, 1)

            def expert_pass(ps, j, own, chunks, parity, gathers):
                pe.wait_ge(ps.xe_ready, j + 1)
                weights_step(ps, (0, 1), xe[:, :, own], chunks(0, 4))
                weights_step(ps, (2, 3), xe[:, :, own], chunks(4, 6))
                turn_rows(ps, 2 * j + 1, 6)
                weights_step(ps, (2, 3), xe[:, :, own], chunks(6, 8))
                pe.wait_ge(ps.g_ready, j + 1)
                scatter(ps, j, parity, 2 * j + 2, range(0, HALF))
                if gathers:
                    scatter(ps, j, parity, 2 * j + 2, range(HALF, KT))
                turn_rows(ps, 2 * j + 2, 0)
                if gathers:
                    pe.wait_ge(ps.selected, j + SELECTED[ps is extra])
                    pe.wait_ge(ps.added, j * KT + KT)
                    gather(gathers)
                else:
                    scatter(ps, j, parity, 2 * j + 2, range(HALF, KT))
                    pe.wait_ge(ps.selected, j + SELECTED[ps is extra])
                turn_selection(ps)
                pe.wait_ge(ps.mid_ready, j + 1)
                weights_step(ps, (4, 5), gs, chunks(8, 12))
                pe.wait_ge(ps.added, j * KT + KT)

            pe.wait_ge(pw_ready, KT)
            pe.wait_ge(zeros_ready, 1)
            pe.wait_ge(wts_ready, 1)
            for b, rows, t0 in BLOCKS:
                ins = turn(bank[0][0:E, t0:t0 + rows], wtsv[0:rows, b, 0:E], ident[0:rows, 0:rows])
            ins.then_inc(wT_done, 1)
            pe.sem_inc(extra.used, PER_EXPERT)
            pe.wait_ge(x2_ready, NB + 1)
            pe.wait_ge(main.selected, 1)
            gather(P)
            turn_selection(main)
            with pe.Fori(0, ROUNDS) as i:
                for u in range(UNROLL):
                    def main_chunks(c0, c1, u=u):
                        loads = 16 * UNROLL * PER_EXPERT // SLOTS
                        return [(r % SLOTS, slot_loaded[r % SLOTS], i * loads + expert_loads(r), 2 * (r % 4))
                                for r in range(u * PER_EXPERT + c0, u * PER_EXPERT + c1)]
                    expert_pass(main, i * UNROLL + u, slice(u % 2 * CAP, (u % 2 + 1) * CAP), main_chunks,
                                (u + 1) % 2, P if u % 2 else 0)
            pe.wait_ge(main.xe_ready, E + 1)

            pe.wait_ge(table_ready, 1)
            n_extra = pe.value_load(ov_table_i[0:1, 2 * MAX_OV:2 * MAX_OV + 1], min_val=0, max_val=MAX_OV)
            with pe.If(n_extra > 0):
                with pe.Fori(0, n_extra) as i:
                    def extra_chunks(c0, c1):
                        return [(EXTRA_SLOT + c, extra_loaded[c], i * 16 + 16, 2 * (c % 4)) for c in range(c0, c1)]
                    expert_pass(extra, i, slice(0, CAP), extra_chunks, 1, CAP)
            scatter(extra, n_extra, 1)

            for f in range(KT):
                s = (LAST + f // 2) % SLOTS
                if f % 2 == 0:
                    pe.wait_ge(slot_loaded[s], expert_loads(LAST + f // 2))
                if f >= 4:
                    pe.wait_ge(gate_pre, f - 3)
                for k in range(KT):
                    if f == 0:
                        pe.wait_ge(h2_ready, k + 1)
                    ins = mm(bank[f % 4][:, 0:T], by_col[s][:, k, (f % 2) * P:(f % 2 + 1) * P], n3T[:, k, :],
                             start=(k == 0), stop=(k == KT - 1))
                ins.then_inc(gate_done, 1)
                if f == 1:
                    pe.wait_ge(sq_added, 1)
                    mm(bank[4][:, 0:T], ones[:, :], sqT[:, 0, :], start=True, stop=True).then_inc(rms_done, 1)
            pe.wait_ge(ysq_added, KT - 1)
            for b, rows, t0 in BLOCKS:
                ins = mm(bank[5][0:rows, b:b + 1], sqT[:, 0, t0:t0 + rows], ones[:, 0:1], start=True, stop=True)
            ins.then_inc(y_stat, 1)
            pe.wait_ge(h3_ready, KT)
            for b, rows, t0 in BLOCKS:
                for i in range(2):
                    n = 2 * b + i
                    if n >= 4:
                        pe.wait_ge(yrow_ready["scalar" if i else "vector"], b - 1)
                    for j in range(HALF):
                        f = i * HALF + j
                        ins = turn(bank[n % 4][0:rows, j * P:(j + 1) * P], y3T[:, f, t0:t0 + rows], ident[:, :])
                    ins.then_inc(yrow_done, 1)

        @block.vector
        def _(dve):
            v = nc.vector
            link = chained(dve, dve_step)

            def vec(row, rows=P):
                return vecT[0:rows, row:row + 1]

            def empty(x):
                assert mby[mpos[x]] == "vector"
                return misc_free["vector"]

            for f in range(KT):
                dve.wait_ge(misc_done, mcount(("xT", f)))
                v.tensor_copy(hTv[:, f, :], mbank(("xT", f))[:, 0:T]).then_inc(empty(("xT", f)), 1)
            dve.wait_ge(misc_done, mcount("vec"))
            v.tensor_copy(vecT[:, 0:40], mbank("vec")[:, 0:40]).then_inc(empty("vec"), 1)
            dve.wait_ge(*freed(mby, misc_free, mpos["vec"]))
            dve.wait_ge(x_squares, NB + 1)
            for b, rows, _ in BLOCKS:
                ins = v.tensor_scalar(xrs[0:rows, b:b + 1], xss[0:rows, b:b + 1], 1.0 / D, EPS, ALU.mult, ALU.add)
            ins.then_inc(x_scale_sum, 1)
            dve.wait_ge(x_root, 1)
            for b, rows, _ in BLOCKS:
                ins = v.reciprocal(xrs[0:rows, b:b + 1], xrs[0:rows, b:b + 1])
            link(ins)
            for b, rows, _ in BLOCKS:
                ins = v.tensor_scalar(xn[0:rows, b, :], x_tok[0:rows, b, :], xrs[0:rows, b:b + 1], None, ALU.mult)
            ins.then_inc(xn_ready, 1)
            for f in range(KT):
                dve.wait_ge(misc_done, mcount(("nT", f)))
                v.tensor_scalar(nT[:, f, :], mbank(("nT", f))[:, 0:T], vec(f), None, ALU.mult)\
                    .then_inc(empty(("nT", f)), 1)
            for h in range(H):
                dve.wait_ge(misc_done, mcount(("la", h)))
                ins = v.tensor_scalar(keT[:, h, :], mbank(("la", h))[:, 0:T], vec(32 + h), None, ALU.add)
                ins.then_inc(empty(("la", h)), 1)
            dve.wait_ge(*freed(mby, misc_free, mpos[("la", H - 1)]))
            v.scalar_tensor_tensor(e1, keT, -1.0, keT, ALU.mult, ALU.max).then_inc(abs_ready, 1)
            dve.wait_ge(la_ready, 1)
            link(v.scalar_tensor_tensor(kdT, keT, 0.0, e1, ALU.min, ALU.subtract))
            for h in range(H):
                ins = v.tensor_tensor_scan(bT[:, h, :], scanmask, kdT[:, h, :], 0.0, ALU.mult, ALU.add)
            ins.then_inc(cum_ready, 1)
            dve.wait_ge(cum_ready, 1)
            for h in range(H):
                bh = bT[:, h, 0:L].rearrange("p (c s) -> p c s", c=NCH)
                ins = v.tensor_tensor(kdT[:, h, 0:L].rearrange("p (c s) -> p c s", c=NCH),
                                      bh[:, :, GLA_CHUNK - 1:GLA_CHUNK].to_broadcast([P, NCH, GLA_CHUNK]), bh,
                                      ALU.subtract)
            ins.then_inc(back_ready, 1)
            for i in range(2):
                dve.wait_ge(misc_done, mcount(("bias", i)))
                v.tensor_copy(biasT[:, i * KT * E:(i + 1) * KT * E], mbank(("bias", i))[:, 0:KT * E])\
                    .then_inc(empty(("bias", i)), 1)
            dve.wait_ge(misc_done, mcount("wsp"))
            v.tensor_tensor(WT, mbank("wsp")[:, 0:MH * P].rearrange("p (h t) -> p h t", h=MH),
                            upto[:, :].unsqueeze(1).to_broadcast([P, MH, P]), ALU.mult).then_inc(empty("wsp"), 1)
            for h in range(MH):
                ins = v.tensor_scalar(dw[:, h * NS:(h + 1) * NS], ident[0:NS, 0:NS], w00[:, h:h + 1], None, ALU.mult)
            ins.then_inc(dw_ready, 1)
            dve.wait_ge(decays_ready, 3)
            dve.wait_ge(*freed(zby, z_free, zpos[("q", H - 1)]))
            for h in range(H):
                v.tensor_copy(decay[:, h, :], e1[:, h, GLA_CHUNK - 1:L:GLA_CHUNK])
            v.tensor_copy(sdecay, e1[:, :, L:T])
            v.scalar_tensor_tensor(qT[:, :, 0:L], qT[:, :, 0:L], float(DK) ** -0.5, e1[:, :, 0:L], ALU.mult, ALU.mult)
            v.tensor_scalar(qT[:, :, L:T], qT[:, :, L:T], float(DK) ** -0.5, None, ALU.mult)
            v.tensor_tensor(onehots, iota_c[:, 0:NS].unsqueeze(2).to_broadcast([P, NS, NS]),
                            iota_c[:, 0:NS].unsqueeze(1).to_broadcast([P, NS, NS]), ALU.is_equal)
            v.tensor_tensor(keT[:, :, 0:L], keT[:, :, 0:L], kT[:, :, 0:L], ALU.mult)
            v.memset(att, 0.0)
            v.tensor_tensor(kdT[:, :, 0:L], kdT[:, :, 0:L], kT[:, :, 0:L], ALU.mult).then_inc(gla_in_ready, 1)
            dve.wait_ge(gla_in_ready, 1)
            for h in range(H):
                ins = v.tensor_tensor(q_alone[:, h, :, :], onehots,
                                      qT[:, h, L:T].unsqueeze(2).to_broadcast([P, NS, NS]), ALU.mult)
            link(ins)

            def rows_from(kind, f, out):
                x = (kind, f)
                dve.wait_ge(misc_done, mcount(x))
                v.tensor_copy(out[:, 0:NB, f * P:(f + 1) * P],
                              mbank(x)[:, 0:NB * P].rearrange("p (b f) -> p b f", b=NB))
                v.tensor_copy(out[0:NS, NB, f * P:(f + 1) * P], mbank(x)[0:NS, NB * P:(NB + 1) * P])\
                    .then_inc(empty(x), 1)

            def att_step(b):
                x = ("att", b)
                dve.wait_ge(misc_done, mcount(x))
                for h in range(H):
                    ins = v.copy_predicated(att[:, b, h, :], attmask.bitcast(I32), mbank(x)[:, h * P:(h + 1) * P])
                ins.then_inc(empty(x), 1)
                dve.wait_ge(*freed(mby, misc_free, mpos[x]))
                dve.sem_inc(att_ready, 1)

            def state_of(c):
                return S_ver[:, c, :] if c < NCH - 1 else S_last

            def state_step(c, i):
                x = ("dS", c, i)
                dve.wait_ge(misc_done, mcount(x))
                if c == 0:
                    ins = v.tensor_copy(state_of(0)[:, 2 * i * DV:(2 * i + 2) * DV], mbank(x)[:, :])
                else:
                    for h in (2 * i, 2 * i + 1):
                        hs = slice(h * DV, (h + 1) * DV)
                        ins = v.scalar_tensor_tensor(state_of(c)[:, hs], state_of(c - 1)[:, hs], decay[:, h, c:c + 1],
                                                     mbank(x)[:, (h % 2) * DV:(h % 2 + 1) * DV], ALU.mult, ALU.add)
                ins.then_inc(empty(x), 1)
                dve.wait_ge(*freed(mby, misc_free, mpos[x]))
                dve.sem_inc(state_ready, 1)

            def sample_state(b, i):
                x = ("kv", b, i)
                dve.wait_ge(misc_done, mcount(x))
                if i == 0:
                    dve.wait_ge(st_loaded[b % 2], 16 * (b // 2 + 1))
                for h in (2 * i, 2 * i + 1):
                    s = st[:, b % 2, h * DV:(h + 1) * DV]
                    ins = v.scalar_tensor_tensor(s, s, sdecay[:, h, b:b + 1],
                                                 mbank(x)[:, (h % 2) * DV:(h % 2 + 1) * DV], ALU.mult, ALU.add)
                ins.then_inc(empty(x), 1)
                dve.wait_ge(*freed(mby, misc_free, mpos[x]))
                dve.sem_inc(st_ready, 1)

            def o_norm():
                dve.wait_ge(o_squares, NB * H)
                v.tensor_scalar(ors, oss, 1.0 / DV, EPS, ALU.mult, ALU.add).then_inc(o_sum, 1)
                dve.wait_ge(o_root, 1)
                link(v.reciprocal(ors, ors))
                for b in range(NB):
                    for h in range(H):
                        hs = slice(h * DV, (h + 1) * DV)
                        ins = v.tensor_scalar(o_tok[:, b, hs], o_tok[:, b, hs], ors[:, b * H + h:b * H + h + 1], None,
                                              ALU.mult)
                ins.then_inc(o_ready, 1)

            def sample_o_norm():
                dve.wait_ge(o_squares, NB * H + 1)
                v.tensor_scalar(so_rs, so_ss, 1.0 / DV, EPS, ALU.mult, ALU.add).then_inc(o_sum, 1)
                dve.wait_ge(o_root, 2)
                link(v.reciprocal(so_rs, so_rs))
                v.tensor_scalar(o_s, o_s, so_rs, None, ALU.mult).then_inc(o_ready, 1)

            def v_stats(i):
                dve.wait_ge(*freed(mby, misc_free, mpos[("vgT", (i + 1) * HALF - 1)]))
                for b, rows, _ in BLOCKS:
                    ins = v.bn_stats(vstat[0:rows, 12 * b + 6 * i:12 * b + 6 * i + 6],
                                     vn[0:rows, b, i * 512:(i + 1) * 512])
                link(ins)

            def v_var():
                for b, rows, _ in BLOCKS:
                    ins = v.bn_aggr(vmv[0:rows, 2 * b:2 * b + 2], vstat[0:rows, 12 * b:12 * b + 12])
                link(ins)
                for b, rows, _ in BLOCKS:
                    ins = v.tensor_scalar(vrs[0:rows, b:b + 1], vmv[0:rows, 2 * b + 1:2 * b + 2], EPS, None, ALU.add)
                ins.then_inc(vn_var, 1)

            def v_scale():
                dve.wait_ge(vn_root, 1)
                for b, rows, _ in BLOCKS:
                    ins = v.reciprocal(vrs[0:rows, b:b + 1], vrs[0:rows, b:b + 1])
                link(ins)
                for b, rows, _ in BLOCKS:
                    v.tensor_scalar(vn[0:rows, b, :], vn[0:rows, b, :], vmv[0:rows, 2 * b:2 * b + 1],
                                    vrs[0:rows, b:b + 1], ALU.subtract, ALU.mult).then_inc(vn_scaled, 1)
                dve.wait_ge(ld_rows, 16 * 3)
                dve.wait_ge(vn_scaled, NB + 1)
                vs = vn[0:NS, NB, :]
                link(v.tensor_tensor(vs, vs, vngrow[0:NS, :], ALU.mult))
                v.tensor_tensor(vs, vs, vnbrow[0:NS, :], ALU.add).then_inc(vn_ready, 1)

            def b_step(f):
                x = ("mix", f)
                dve.wait_ge(misc_done, mcount(x))
                dve.wait_ge(*freed(zby, z_free, zpos[("gb", f)]))
                if f > 0:
                    dve.wait_ge(b_done, f)
                ins = v.tensor_tensor(t[4], mbank(x)[:, 0:T], bspT[:, f * MH // KT, :], ALU.add)
                ins.then_inc(empty(x), 1)
                dve.wait_ge(*freed(mby, misc_free, mpos[x]))
                link(v.tensor_tensor(t[4], t[4], t[f % 2], ALU.mult))
                v.tensor_tensor(mixT[:, f, :], t[4], t[2 + f % 2], ALU.mult).then_inc(b_done, 1)

            def r_step(f):
                dve.wait_ge(r_sig, f + 1)
                v.tensor_tensor(t[f % 2], t[f % 2], zbank(("r", f))[:, 0:T], ALU.mult).then_inc(z_free["vector"], 1)

            def a_step(f):
                x = ("oT", f)
                dve.wait_ge(*freed(zby, z_free, zpos[("ga", f)]))
                dve.wait_ge(*freed(zby, z_free, zpos[("r", f)]))
                link(v.tensor_tensor(t[2 + f % 2], t[f % 2], t[2 + f % 2], ALU.mult))
                if f == 0:
                    dve.wait_ge(b_done, KT)
                else:
                    dve.wait_ge(a_done, f)
                dve.wait_ge(misc_done, mcount(x))
                ins = v.scalar_tensor_tensor(t[4], mbank(x)[:, 0:T], vec(36 + f % 2), t[2 + f % 2], ALU.mult, ALU.mult)
                ins.then_inc(empty(x), 1)
                dve.wait_ge(*freed(mby, misc_free, mpos[x]))
                v.tensor_tensor(mixT[:, f, :], mixT[:, f, :], t[4], ALU.add).then_inc(a_done, 1)

            for x in plan:
                if x[0] not in ("z", "so") and mby[mpos[x]] == "vector":
                    kind, *at = x if isinstance(x, tuple) else (x,)
                    if kind == "vT":
                        rows_from("vT", at[0], v_tok)
                    elif kind == "vgT":
                        rows_from("vgT", at[0], vn)
                        if at[0] == HALF:
                            v_stats(0)
                        if at[0] == KT - 1:
                            v_stats(1)
                            v_var()
                    elif kind == "att":
                        att_step(*at)
                    elif kind == "dS":
                        state_step(*at)
                    elif kind == "kv":
                        sample_state(*at)
                        if at == [0, 1]:
                            v_scale()
                    elif kind == "mix":
                        if at[0] == 0:
                            dve.wait_ge(bsp_ready, 1)
                        b_step(*at)
                        if at[0] == 1:
                            o_norm()
                    elif kind == "oT":
                        if at[0] == 0:
                            sample_o_norm()
                        if at[0] % 2 == 0:
                            r_step(at[0])
                            r_step(at[0] + 1)
                        a_step(*at)

            dve.wait_ge(vn_stored, 16)
            for f in range(KT):
                dve.wait_ge(z_done, zcount(("wo", f)))
                if f == 0:
                    dve.wait_ge(*freed(mby, misc_free, mpos[("xT", KT - 1)]))
                v.tensor_tensor(hTv[:, f, :], hTv[:, f, :], zbank(("wo", f))[:, 0:T], ALU.add).then_inc(h_ready, 1)
                dve.wait_ge(h_ready, f + 1)
                v.tensor_scalar(hgT[:, f, :], hTv[:, f, :], vec(KT + f), None, ALU.mult).then_inc(hg_ready, 1)
                dve.sem_inc(z_free["vector"], 1)
            dve.wait_ge(h_squares, 2 * (NB + 1))
            for b, rows, _ in BLOCKS:
                ins = v.tensor_tensor(hrs[0:rows, b:b + 1], hss[0:rows, 2 * b:2 * b + 1],
                                      hss[0:rows, 2 * b + 1:2 * b + 2], ALU.add)
            link(ins)
            for b, rows, _ in BLOCKS:
                ins = v.tensor_scalar(hrs[0:rows, b:b + 1], hrs[0:rows, b:b + 1], 1.0 / D, EPS, ALU.mult, ALU.add)
            ins.then_inc(h_sum, 1)
            v.memset(selm, 0.0)
            dve.wait_ge(zeros_ready, 1)
            dve.wait_ge(h_root, 1)
            for b, rows, _ in BLOCKS:
                ins = v.reciprocal(hrs[0:rows, b:b + 1], hrs[0:rows, b:b + 1])
            ins.then_inc(hrs_ready, 1)
            dve.wait_ge(hrs_ready, 1)
            dve.wait_ge(router_done, 1)
            dve.wait_ge(ld_router, 48)
            for b, rows, _ in BLOCKS:
                ins = v.scalar_tensor_tensor(lg[0:rows, b, :], bank[1][0:rows, b * E:(b + 1) * E],
                                             hrs[0:rows, b:b + 1], brrow[0:rows, :], ALU.mult, ALU.add)
            link(ins)
            for b, rows, _ in BLOCKS:
                ins = v.max(m8[0:rows, b, :], lg[0:rows, b, :])
            link(ins)
            for b, rows, _ in BLOCKS:
                v.tensor_scalar(negm[0:rows, b:b + 1], m8[0:rows, b, 0:1], -1.0, None, ALU.mult).then_inc(top_ready, 1)
            for b, rows, _ in BLOCKS:
                ins = v.max_index(idx[0:rows, b, :].bitcast(U32), m8[0:rows, b, :], lg[0:rows, b, :])
            link(ins)
            for b, rows, _ in BLOCKS:
                ins = v.tensor_copy(idx_f[0:rows, b, :], idx[0:rows, b, 0:TOP_K].bitcast(U32))
            link(ins)
            for b, rows, _ in BLOCKS:
                r = slice(0, rows)
                ins = v.tensor_tensor(hit[r, b], iota_e[r, :].unsqueeze(1).to_broadcast([rows, TOP_K, E]),
                                      idx_f[r, b, :].unsqueeze(2).to_broadcast([rows, TOP_K, E]), ALU.is_equal)
            link(ins)
            for b, rows, _ in BLOCKS:
                r = slice(0, rows)
                ins = v.tensor_reduce(selm[r, b, :], hit[r, b].rearrange("p k e -> p e k"), AX.X, ALU.add)
            ins.then_inc(sel_ready, 1)
            dve.wait_ge(top_exp, NB + 1)
            for b, rows, _ in BLOCKS:
                ins = v.reciprocal(esum[0:rows, b:b + 1], esum[0:rows, b:b + 1])
            link(ins)
            for b, rows, _ in BLOCKS:
                ins = v.tensor_scalar(ew[0:rows, b, :], ew[0:rows, b, :], esum[0:rows, b:b + 1], None, ALU.mult)
            link(ins)
            for b, rows, _ in BLOCKS:
                r = slice(0, rows)
                ins = v.tensor_tensor(hit[r, b], hit[r, b], ew[r, b, :].unsqueeze(2).to_broadcast([rows, TOP_K, E]),
                                      ALU.mult)
            link(ins)
            for b, rows, _ in BLOCKS:
                r = slice(0, rows)
                ins = v.tensor_reduce(wtsv[r, b, 0:E], hit[r, b].rearrange("p k e -> p e k"), AX.X, ALU.add)
            ins.then_inc(wts_ready, 1)
            for c in (slice(0, 512), slice(512, 1024)):
                ins = v.scalar_tensor_tensor(x2[0:NS, NB, c], bank[2 + 2 * NB + c.start // 512][0:NS, :],
                                             hrs[0:NS, NB:NB + 1], g2row[0:NS, c], ALU.mult, ALU.mult)
            ins.then_inc(x2_ready, 1)
            dve.wait_ge(rank_done, 1)
            v.tensor_copy(cnt, bank[1][:, RANKS + (NB + 1) * E:RANKS + (NB + 2) * E])
            placed = rankv[:, :, 0:E]
            ranks_before = bank[1][:, RANKS:RANKS + (NB + 1) * E].rearrange("p (b e) -> p b e", b=NB + 1)
            link(v.scalar_tensor_tensor(placed, ranks_before, 1.0, selm, ALU.add, ALU.mult))
            link(v.tensor_scalar(placed, placed, -1.0, None, ALU.add))

            def select_pair(e):
                for i in range(2):
                    for b in range(NB + 1):
                        v.tensor_scalar(Ssel[:, b, i * CAP:(i + 1) * CAP], iota_c[:, 0:CAP],
                                        rankv[:, b, bass.ds(e + i, 1)], None, ALU.is_equal)

            def select(ps, col, w_col, offset=None, columns=None):
                if offset is None:
                    at_rank = lambda b: rankv[:, b, col]
                else:
                    vlink(v.tensor_scalar(rk[:, :], rankv[:, :, col].rearrange("p b e -> p (b e)"), offset, None,
                                          ALU.subtract))
                    at_rank = lambda b: rk[:, b:b + 1]
                if columns is not None:
                    for b in range(NB + 1):
                        v.tensor_scalar(Ssel[:, b, columns], iota_c[:, 0:CAP], at_rank(b), None, ALU.is_equal)
                for b in range(NB + 1):
                    ins = v.tensor_scalar(Swt[:, b, :], iota_c[:, :], at_rank(b), wtsv[:, b, w_col],
                                          ALU.is_equal, ALU.mult)
                ins.then_inc(ps.selected, 1)

            def through(ps, item, chunks):
                return item * PER_EXPERT + (chunks + (PER_EXPERT if ps is extra else 0))

            def rows_out(ps, item, chunks, b):
                dve.wait_ge(ps.used, through(ps, item, chunks))
                v.tensor_copy(rows_sb[:, 512:1024], bank[b][:, :]).then_inc(ps.rows_vector, 1)

            def biased(out, b, m, col):
                v_in = bank[b][:, 0:EC].rearrange("p (f c) -> p f c", f=KT)
                return v.tensor_tensor(out, v_in, biasv[:, m, :, col].to_broadcast([P, KT, CAP]), ALU.add)

            def gate_step(ps, item, col):
                rows_out(ps, item, 4, 1)
                dve.wait_ge(ps.turned, 2 * item + 1)
                vlink(biased(gs, 6, 0, col))
                v.tensor_scalar(gs, gs, LIMIT, None, ALU.min).then_inc(ps.g_ready, 1)

            def silu_step(ps, item):
                dve.wait_ge(ps.sig_ready, item + 1)
                vlink(v.tensor_tensor(sg, gs, sg, ALU.mult))

            def up_step(ps, item, col):
                dve.wait_ge(ps.turned, 2 * item + 2)
                vlink(biased(us, 0, 1, col))
                vlink(v.tensor_scalar(us, us, LIMIT, -LIMIT, ALU.min, ALU.max))
                v.scalar_tensor_tensor(gs, us, 1.0, sg, ALU.add, ALU.mult).then_inc(ps.mid_ready, 1)

            def add_y(ps, n, fs=range(KT)):
                for f in fs:
                    dve.wait_ge(ps.scattered, n * KT + f + 1)
                    v.tensor_tensor(hTv[:, f, :], hTv[:, f, :], bank[SCATTER[f]][:, 0:T], ALU.add)\
                        .then_inc(ps.added, 1)

            STEPS = 4
            vlink = chained(dve, main.vector_step)
            select_pair(0)
            select(main, bass.ds(0, 1), bass.ds(0, 1))
            link(v.tensor_scalar(nov, cnt, float(CAP), None, ALU.is_gt))
            for n in range(2, LEVELS + 1):
                link(v.scalar_tensor_tensor(nov, cnt, float(n * CAP), nov, ALU.is_gt, ALU.add))
            link(v.tensor_tensor_scan(nov_end, ones[:, 0:E], nov, 0.0, ALU.mult, ALU.add))
            ends = nov_end.unsqueeze(1).to_broadcast([P, MAX_OV, E])
            link(v.tensor_tensor(ovt, ends, iota_c[:, 0:MAX_OV].unsqueeze(2).to_broadcast([P, MAX_OV, E]), ALU.is_le))
            link(v.tensor_reduce(ov_table[:, 0:MAX_OV], ovt, AX.X, ALU.add))
            link(v.tensor_tensor(ovt, ovt, nov.unsqueeze(1).to_broadcast([P, MAX_OV, E]), ALU.mult))
            link(v.tensor_reduce(ov_table[:, MAX_OV:2 * MAX_OV], ovt, AX.X, ALU.add))
            link(v.scalar_tensor_tensor(ov_table[:, MAX_OV:2 * MAX_OV], iota_c[:, 0:MAX_OV], 1.0,
                                        ov_table[:, MAX_OV:2 * MAX_OV], ALU.add, ALU.subtract))
            link(v.tensor_scalar(ov_table[:, MAX_OV:2 * MAX_OV], ov_table[:, MAX_OV:2 * MAX_OV], float(CAP), None,
                                 ALU.mult))
            link(v.tensor_copy(ov_table[:, 2 * MAX_OV:2 * MAX_OV + 1], nov_end[:, E - 1:E]))
            v.tensor_copy(ov_table_i[:, :], ov_table[:, :]).then_inc(table_ready, 1)
            dve.wait_ge(table_ready, 1)
            e = dve.value_load(ov_table_i[0:1, 0:1], min_val=0, max_val=E)
            v.tensor_scalar(rankv[:, :, E], rankv[:, :, bass.ds(e, 1)].rearrange("p b e -> p (b e)"),
                            ov_table[:, MAX_OV:MAX_OV + 1], None, ALU.subtract)
            link(v.tensor_copy(wtsv[:, :, E], wtsv[:, :, bass.ds(e, 1)].rearrange("p b e -> p (b e)")))

            with dve.Fori(0, ROUNDS) as i:
                for u in range(UNROLL):
                    j = i * UNROLL + u
                    vlink = chained(dve, main.vector_step, base=j * STEPS)
                    gate_step(main, j, bass.ds(j, 1))
                    if u % 2 == 1:
                        select_pair(j + 1)
                    select(main, bass.ds(j + 1, 1), bass.ds(j + 1, 1))
                    silu_step(main, j)
                    rows_out(main, j, 8, 3)
                    if u % 2 == 0:
                        add_y(main, j, range(HALF))
                        up_step(main, j, bass.ds(j, 1))
                        add_y(main, j, range(HALF, KT))
                    else:
                        add_y(main, j)
                        up_step(main, j, bass.ds(j, 1))
                    assert vlink.count[0] == STEPS

            n_extra = dve.value_load(ov_table_i[0:1, 2 * MAX_OV:2 * MAX_OV + 1], min_val=0, max_val=MAX_OV)
            with dve.If(n_extra > 0):
                with dve.Fori(0, n_extra) as i:
                    e = dve.value_load(ov_table_i[0:1, bass.ds(i, 1)], min_val=0, max_val=E - 1)
                    after = dve.value_load(ov_table_i[0:1, bass.ds(i + 1, 1)], min_val=0, max_val=E)
                    vlink = chained(dve, extra.vector_step, base=i * (STEPS + 1))
                    gate_step(extra, i, bass.ds(e, 1))
                    select(extra, bass.ds(after, 1), bass.ds(after, 1), ov_table[:, bass.ds(i + (MAX_OV + 1), 1)],
                           slice(0, CAP))
                    silu_step(extra, i)
                    rows_out(extra, i, 8, 3)
                    add_y(extra, i)
                    up_step(extra, i, bass.ds(e, 1))
                    assert vlink.count[0] == STEPS + 1
            add_y(extra, n_extra)
            dve.wait_ge(extra.added, n_extra * KT + KT)

            link = chained(dve, tail_step)
            for f in range(KT):
                v.tensor_scalar(n3T[:, f, :], hTv[:, f, :], vec(2 * KT + f), None, ALU.mult).then_inc(h2_ready, 1)
            dve.wait_ge(sq_ready, KT)
            n = KT // 2
            while n > 1:
                link(v.tensor_tensor(sqT[:, 0:n, :], sqT[:, 0:n, :], sqT[:, n:2 * n, :], ALU.add))
                n //= 2
            v.tensor_tensor(sqT[:, 0, :], sqT[:, 0, :], sqT[:, 1, :], ALU.add).then_inc(sq_added, 1)
            dve.wait_ge(rms_done, 1)
            v.tensor_scalar(rb, bank[4][:, 0:T], 1.0 / D, EPS, ALU.mult, ALU.add).then_inc(rms_sum, 1)
            dve.wait_ge(rms_root, 1)
            link(v.reciprocal(rb, rb))

            def third(f):
                g = gt[f % 3]
                dve.wait_ge(gate_act, f + 1)
                dve.wait_ge(pw_ready, KT)
                link(v.tensor_tensor(g, g, pwT[:, f, :], ALU.mult))
                v.tensor_tensor(hTv[:, f, :], hTv[:, f, :], g, ALU.add).then_inc(h3_sum, 1)
                dve.wait_ge(h3_sum, f + 1)
                v.tensor_scalar(y3T[:, f, :], hTv[:, f, :], vec(3 * KT + f), None, ALU.mult).then_inc(h3_ready, 1)

            def add_squares(f):
                dve.wait_ge(ysq_ready, f + 1)
                if f > 1:
                    dve.wait_ge(ysq_added, f - 1)
                v.tensor_tensor(sqT[:, 0, :], sqT[:, 0, :], sqT[:, f, :], ALU.add).then_inc(ysq_added, 1)

            for f in range(KT):
                dve.wait_ge(gate_done, f + 1)
                v.tensor_tensor(gt[f % 3], bank[f % 4][:, 0:T], rb, ALU.mult).then_inc(gate_pre, 1)
                if f > 0:
                    third(f - 1)
                if f > 1:
                    add_squares(f - 1)
            third(KT - 1)
            add_squares(KT - 1)
            dve.wait_ge(y_stat, 1)
            for b, rows, _ in BLOCKS:
                ins = v.tensor_scalar(yss[0:rows, b:b + 1], bank[5][0:rows, b:b + 1], 1.0 / D, EPS, ALU.mult, ALU.add)
            ins.then_inc(y_sum, 1)
            dve.wait_ge(y_root, 1)
            for b, rows, _ in BLOCKS:
                ins = v.reciprocal(yss[0:rows, b:b + 1], yss[0:rows, b:b + 1])
            ins.then_inc(y_scale, 1)
            dve.wait_ge(y_scale, 1)
            for b, rows, _ in BLOCKS:
                dve.wait_ge(yrow_done, 2 * b + 1)
                v.tensor_scalar(x2[0:rows, b, 0:512], bank[2 * b % 4][0:rows, :], yss[0:rows, b:b + 1], None, ALU.mult)\
                    .then_inc(yrow_ready["vector"], 1)

        @block.scalar
        def _(act):
            a = nc.scalar.activation
            link = chained(act, act_step)

            act.wait_ge(pool_step, 1)
            load_vectors(act, range(3, 6))
            for b, rows, _ in BLOCKS:
                act.wait_ge(ld_x[b], 16)
                if b > 0:
                    act.wait_ge(x_squares, b)
                a(junk[0:rows, :], x_tok[0:rows, b, :], ACT.Square, accum_out=xss[0:rows, b:b + 1])\
                    .then_inc(x_squares, 1)
            act.wait_ge(x_scale_sum, 1)
            for b, rows, _ in BLOCKS:
                ins = a(xrs[0:rows, b:b + 1], xrs[0:rows, b:b + 1], ACT.Sqrt)
            ins.then_inc(x_root, 1)
            act.dma_start(w00[:, :], w_sp[0, :, 0, 0].unsqueeze(0).to_broadcast([NS, MH]),
                          allow_slow_non_contiguous=True).then_inc(ld_wsp, 16)
            act.dma_start(wsp, w_sp[0].rearrange("h t s -> t h s")).then_inc(ld_wsp, 16)
            for b, rows, t0 in BLOCKS:
                src = p_prompt[0, 0, t0:t0 + rows, :] if b < NB else p_sample[0, :, 0, :]
                act.dma_start(p_tok[0:rows, b, :], src).then_inc(ld_p, 16)
            for m, x in enumerate((b_gate, b_up)):
                act.dma_start(bias_rows[0:E, m, :], x[0]).then_inc(ld_bias, 16)
            act.dma_start(vngrow, v_norm_g.to_broadcast([P, D])).then_inc(ld_rows, 16)
            act.dma_start(vnbrow, v_norm_b.to_broadcast([P, D])).then_inc(ld_rows, 16)
            act.dma_start(bspT[:, :, 0:P], b_sp.to_broadcast([P, MH, P])).then_inc(ld_rows, 16)
            act.dma_start(g2row[:, :], norm2_g.to_broadcast([P, D])).then_inc(ld_router, 16)
            act.dma_start(brrow[:, :], b_router.to_broadcast([P, E])).then_inc(ld_router, 16)
            act.dma_start(wrtv, w_router[0].rearrange("(k p) n -> p k n", p=P)).then_inc(ld_router, 16)

            def z_out(kind, f):
                tile = (kind, f)
                p, free = zbank(tile)[:, 0:T], z_free["scalar"]
                act.wait_ge(z_done, zcount(tile))
                if kind in ("k", "q"):
                    a((kT if kind == "k" else qT)[:, f, :], p, ACT.Copy).then_inc(free, 1)
                elif kind == "v":
                    if f >= 2:
                        act.wait_ge(misc_done, mcount(("vT", f - 2)))
                    a(t[f % 2], p, ACT.Copy).then_inc(free, 1)
                elif kind == "vg":
                    if f >= 2:
                        act.wait_ge(misc_done, mcount(("vgT", f - 2)))
                    a(t[2 + f % 2], p, ACT.Gelu).then_inc(free, 1)
                elif kind in ("u", "gb"):
                    if f >= 2:
                        act.wait_ge(b_done, f - 1)
                    else:
                        act.wait_ge(misc_done, mcount(("vT" if kind == "u" else "vgT", KT - 1)))
                    if kind == "u":
                        a(t[f % 2], p, ACT.Gelu).then_inc(free, 1)
                    else:
                        a(t[2 + f % 2], p, ACT.Sigmoid).then_inc(free, 1)
                elif kind in ("r", "ga"):
                    if f >= 2:
                        act.wait_ge(a_done, f - 1)
                    else:
                        act.wait_ge(b_done, KT - 1 + f)
                    if kind == "r":
                        a(t[f % 2], p, ACT.Sigmoid).then_inc(r_sig, 1)
                    else:
                        a(t[2 + f % 2], p, ACT.Sigmoid).then_inc(free, 1)

            def mask_keys(b):
                a(kmask[0:NS, b % 2, :], kd_tok[0:NS, NB, :], ACT.Copy, scale=ident[0:NS, b:b + 1])\
                    .then_inc(kmask_ready, 1)

            def misc_out(x):
                kind, *at = x if isinstance(x, tuple) else (x,)
                p, free = mbank(x), misc_free["scalar"]
                act.wait_ge(misc_done, mcount(x))
                f = at[0] if at else None
                if kind == "gk":
                    a(gkT[0:RANK, :], p[0:RANK, 0:T], ACT.Copy).then_inc(free, 1)
                elif kind == "pT":
                    a(pTv[:, f, :], p[:, 0:T], ACT.Copy).then_inc(free, 1)
                elif kind == "kdT":
                    rows = BLOCKS[f][1]
                    a(kd_tok[0:rows, f, :], p[0:rows, :], ACT.Copy).then_inc(free, 1)
                    if f == NB:
                        act.wait_ge(*freed(mby, misc_free, mpos[x]))
                        mask_keys(0)
                        mask_keys(1)
                elif kind == "o":
                    b, i = at
                    a(o_tok[:, b, i * 512:(i + 1) * 512], p[:, :], ACT.Copy).then_inc(free, 1)
                    act.wait_ge(*freed(mby, misc_free, mpos[x]))
                    for h in (2 * i, 2 * i + 1):
                        a(ojunk[h % 2], o_tok[:, b, h * DV:(h + 1) * DV], ACT.Square,
                          accum_out=oss[:, b * H + h:b * H + h + 1]).then_inc(o_squares, 1)
                    act.wait_ge(o_squares, 2 * (2 * b + i + 1))

            def sample_o_out():
                for h in range(H):
                    r = slice(GROUP * h, GROUP * h + NS)
                    ins = a(o_s[r, :], bank[SO_BANK][r, 0:DV], ACT.Copy)
                ins.then_inc(o_s_out, 1)
                act.wait_ge(o_s_out, 1)
                a(ojunk[0], o_s, ACT.Square, accum_out=so_ss).then_inc(o_squares, 1)
                act.wait_ge(o_sum, 2)
                a(so_rs, so_rs, ACT.Sqrt).then_inc(o_root, 1)

            for x in plan:
                if x[0] == "z":
                    if zby[zpos[x[1:]]] == "scalar" or x[1] == "r":
                        z_out(*x[1:])
                elif x[0] == "so":
                    act.wait_ge(so_done, x[1] + 1)
                    if x[1] + 2 < NS:
                        mask_keys(x[1] + 2)
                elif mby[mpos[x]] == "scalar":
                    misc_out(x)
                if x == ("mix", KT - 1):
                    sample_o_out()
                if x == ("z", "q", 0):
                    act.wait_ge(abs_ready, 1)
                    link(a(e1, e1, ACT.Exp, scale=-1.0))
                    a(e1, e1, ACT.Ln, bias=1.0).then_inc(la_ready, 1)
                if x == ("z", "v", 0):
                    act.wait_ge(cum_ready, 1)
                    a(e1, bT, ACT.Exp, scale=1.0 / GATE_NORMALIZER).then_inc(decays_ready, 1)
                    a(keT[:, :, 0:L], bT[:, :, 0:L], ACT.Exp, scale=-1.0 / GATE_NORMALIZER).then_inc(decays_ready, 1)
                    act.wait_ge(back_ready, 1)
                    a(kdT[:, :, 0:L], kdT[:, :, 0:L], ACT.Exp, scale=1.0 / GATE_NORMALIZER).then_inc(decays_ready, 1)
                if x == ("z", "u", 0):
                    act.wait_ge(vn_var, 1)
                    for b, rows, _ in BLOCKS:
                        ins = a(vrs[0:rows, b:b + 1], vrs[0:rows, b:b + 1], ACT.Sqrt)
                    ins.then_inc(vn_root, 1)
                if x == ("z", "gb", 1):
                    act.wait_ge(o_sum, 1)
                    a(ors[:, 0:NB * H], ors[:, 0:NB * H], ACT.Sqrt).then_inc(o_root, 1)

            def pw_out(f):
                act.wait_ge(pw_done, f + 1)
                a(pwT[:, f, :], bank[2 * (f % 2)][:, 0:T], ACT.Copy).then_inc(pw_ready, 1)

            for b, rows, _ in BLOCKS:
                for i in range(2):
                    act.wait_ge(hrow_done, 2 * b + i + 1)
                    if b > 0:
                        act.wait_ge(h_squares, 2 * b + i - 1)
                    a(hjunk[(2 * b + i) % 2][0:rows, :], bank[2 + 2 * b + i][0:rows, :], ACT.Square,
                      accum_out=hss[0:rows, 2 * b + i:2 * b + i + 1]).then_inc(h_squares, 1)
            act.wait_ge(h_sum, 1)
            for b, rows, _ in BLOCKS:
                ins = a(hrs[0:rows, b:b + 1], hrs[0:rows, b:b + 1], ACT.Sqrt)
            ins.then_inc(h_root, 1)
            act.wait_ge(hrs_ready, 1)
            for b in range(NB):
                for i in range(2):
                    ins = a(x2[:, b, i * 512:(i + 1) * 512], bank[2 + 2 * b + i][:, :], ACT.Copy, scale=hrs[:, b:b + 1])
                ins.then_inc(x2_scaled, 1)
            pw_out(0)
            for b, rows, _ in BLOCKS:
                act.wait_ge(top_ready, b + 1)
                a(ew[0:rows, b, :], m8[0:rows, b, 0:TOP_K], ACT.Exp, bias=negm[0:rows, b:b + 1],
                  accum_out=esum[0:rows, b:b + 1]).then_inc(top_exp, 1)
            for f in range(1, KT):
                pw_out(f)

            def gathered_out(ps, item, parity, width=0):
                act.wait_ge(ps.gathered, item + 1)
                if width:
                    for i in range(2):
                        a(xe[:, i * HALF:(i + 1) * HALF, 0:width],
                          bank[6 + i][:, 0:HALF * width].rearrange("p (f c) -> p f c", f=HALF), ACT.Copy)
                a(SWT[parity], bank[1][:, 0:T], ACT.Copy).then_inc(ps.xe_ready, 1)

            def rows_out(ps, item, chunks, b):
                base = PER_EXPERT if ps is extra else 0
                act.wait_ge(ps.used, item * PER_EXPERT + (chunks + base))
                a(rows_sb[:, 0:512], bank[b][:, :], ACT.Copy).then_inc(ps.rows_scalar, 1)

            def sigmoid(ps, item):
                act.wait_ge(ps.g_ready, item + 1)
                a(sg, gs, ACT.Sigmoid, scale=ALPHA).then_inc(ps.sig_ready, 1)

            def y_out(ps, item):
                base = PER_EXPERT if ps is extra else 0
                act.wait_ge(ps.used, item * PER_EXPERT + (PER_EXPERT + base))
                for i in range(2):
                    ins = a(y_rows[:, i * 512:(i + 1) * 512], bank[4 + i][:, :], ACT.Copy)
                ins.then_inc(ps.y_ready, 1)

            act.wait_ge(wT_done, 1)
            link(a(SWT[1][0:E, :], bank[0][0:E, 0:T], ACT.Copy))
            act.wait_ge(ld_bdown, 16)
            act.sem_inc(main.y_ready, 1)
            gathered_out(main, 0, 0, P)
            with act.Fori(0, ROUNDS) as i:
                for u in range(UNROLL):
                    j = i * UNROLL + u
                    rows_out(main, j, 4, 0)
                    sigmoid(main, j)
                    rows_out(main, j, 8, 2)
                    gathered_out(main, j + 1, (u + 1) % 2, P if u % 2 else 0)
                    y_out(main, j)

            act.wait_ge(main.y_ready, E + 1)
            act.sem_inc(extra.y_ready, 1)
            act.sem_inc(extra.xe_ready, 1)
            act.wait_ge(table_ready, 1)
            n_extra = act.value_load(ov_table_i[0:1, 2 * MAX_OV:2 * MAX_OV + 1], min_val=0, max_val=MAX_OV)
            with act.If(n_extra > 0):
                with act.Fori(0, n_extra) as i:
                    rows_out(extra, i, 4, 0)
                    sigmoid(extra, i)
                    rows_out(extra, i, 8, 2)
                    act.wait_ge(extra.scattered, i * KT + KT)
                    a(SWT[1], SWT[0], ACT.Copy).then_inc(extra.handed_on, 1)
                    act.wait_ge(extra.handed_on, i + 1)
                    gathered_out(extra, i, 0, CAP)
                    y_out(extra, i)

            for f in range(KT):
                act.wait_ge(h2_ready, f + 1)
                a(sqT[:, f, :], hTv[:, f, :], ACT.Square).then_inc(sq_ready, 1)
            act.wait_ge(rms_sum, 1)
            a(rb, rb, ACT.Sqrt).then_inc(rms_root, 1)

            def gate_sigmoid(f):
                act.wait_ge(gate_pre, f + 1)
                a(gt[f % 3], gt[f % 3], ACT.Sigmoid).then_inc(gate_act, 1)

            for f in range(KT):
                gate_sigmoid(f)
                if f > 0:
                    act.wait_ge(h3_sum, f)
                    a(sqT[:, f - 1, :], hTv[:, f - 1, :], ACT.Square).then_inc(ysq_ready, 1)
            act.wait_ge(h3_sum, KT)
            a(sqT[:, KT - 1, :], hTv[:, KT - 1, :], ACT.Square).then_inc(ysq_ready, 1)
            act.wait_ge(y_sum, 1)
            for b, rows, _ in BLOCKS:
                ins = a(yss[0:rows, b:b + 1], yss[0:rows, b:b + 1], ACT.Sqrt)
            ins.then_inc(y_root, 1)
            act.wait_ge(y_scale, 1)
            for b, rows, _ in BLOCKS:
                act.wait_ge(yrow_done, 2 * b + 2)
                a(x2[0:rows, b, 512:1024], bank[(2 * b + 1) % 4][0:rows, :], ACT.Copy, scale=yss[0:rows, b:b + 1])\
                    .then_inc(yrow_ready["scalar"], 1)


_INS = ["x_prompt", "x_sample", "state_gla", "p_prompt", "p_sample", "norm1_g", "w_in", "w_gk2", "b_gk", "gla_norm_g",
        "v_norm_g", "v_norm_b", "w_sp", "b_sp", "w_o", "norm2_g", "w_router", "b_router", "w_gate", "b_gate", "w_up",
        "b_up", "w_down", "b_down", "norm3_g", "w_ple_gate", "w_ple_proj", "final_g"]
_OUTS = [(1, 256, 1024), (8, 1, 1024), (1, 1, 4, 128, 256), (1, 8, 4, 128, 256), (1, 8, 1, 1024)]


def kernel(**inputs):
    import numpy as _np
    import concourse.bacc as _bacc
    from concourse import mybir as _mybir
    from concourse.bass_utils import run_bass_kernel_spmd as _run

    nc = _bacc.Bacc("TRN2", target_bir_lowering=False, num_devices=1)
    arrays, args = {}, []
    for name in _INS:
        a = _np.ascontiguousarray(inputs[name])
        arrays[f"in_{name}_dram"] = a
        args.append(nc.dram_tensor(f"in_{name}_dram", a.shape, _mybir.dt.from_np(a.dtype), kind="ExternalInput").ap())
    for i, shape in enumerate(_OUTS):
        args.append(nc.dram_tensor(f"out_{i}_dram", shape, _mybir.dt.float32, kind="ExternalOutput").ap())
    hybrid_step(nc, *args)
    r = _run(nc, [arrays], core_ids=[0])
    return tuple(r.results[0][f"out_{i}_dram"] for i in range(len(_OUTS)))
```
